# Optimizing a Trainium2 kernel written in Bass

```python
import math
import jax, jax.numpy as jnp
from jax import lax
import numpy as np

D_MODEL = 1024
BATCH = 1
SEQ = 512
DEPTH = 1

MIX_WIDTH = D_MODEL
SSM_WIDTH = MIX_WIDTH // 2
SSM_GROUP = 16
SSM_GROUPS = SSM_WIDTH // SSM_GROUP
SSM_STATE = 64
ATTN_WIDTH = MIX_WIDTH - SSM_WIDTH
HEAD_DIM = 64
N_Q_HEADS = ATTN_WIDTH // HEAD_DIM
N_KV_HEADS = 2
Q_PER_KV = N_Q_HEADS // N_KV_HEADS
KV_WIDTH = N_KV_HEADS * HEAD_DIM
IN_WIDTH = SSM_WIDTH + ATTN_WIDTH + 2 * KV_WIDTH
WINDOW = 128
BLOCK = 128
ROPE_DIM = HEAD_DIM // 4
ROPE_THETA = 500000.0
D_FF = -(-8 * D_MODEL // (3 * 256)) * 256
NORM_EPS = 1e-6
DT_MIN = 1e-3
DT_MAX = 1e-1
MASK_VALUE = -1e30


def rms_norm(x, g):
    xf = x.astype(jnp.float32)
    y = xf * lax.rsqrt(jnp.mean(xf * xf, axis=-1, keepdims=True) + NORM_EPS)
    return (y * g.astype(jnp.float32)).astype(x.dtype)

def _s5_combine(e1, e2):
    a1r, a1i, b1r, b1i = e1
    a2r, a2i, b2r, b2i = e2
    ar = a2r * a1r - a2i * a1i
    ai = a2r * a1i + a2i * a1r
    br = a2r * b1r - a2i * b1i + b2r
    bi = a2r * b1i + a2i * b1r + b2i
    return (ar, ai, br, bi)

def s5_mixer(u, lam_re, lam_im, log_dt, b_re, b_im, c_re, c_im, d, w_glu, b_glu):
    bsz, L, _ = u.shape
    uf = u.astype(jnp.float32).reshape(bsz, L, SSM_GROUPS, SSM_GROUP)
    lr = jnp.minimum(lam_re.astype(jnp.float32), -1e-4)
    li = lam_im.astype(jnp.float32)
    dt = jnp.exp(log_dt.astype(jnp.float32))[:, None]
    mag = jnp.exp(lr * dt)
    ar = mag * jnp.cos(li * dt)
    ai = mag * jnp.sin(li * dt)
    den = lr * lr + li * li
    fr = ((ar - 1.0) * lr + ai * li) / den
    fi = (ai * lr - (ar - 1.0) * li) / den
    br = b_re.astype(jnp.float32)
    bi = b_im.astype(jnp.float32)
    bbar_re = fr[..., None] * br - fi[..., None] * bi
    bbar_im = fr[..., None] * bi + fi[..., None] * br
    bu_re = jnp.einsum('blgh,gph->blgp', uf, bbar_re)
    bu_im = jnp.einsum('blgh,gph->blgp', uf, bbar_im)
    a_re = jnp.broadcast_to(ar, (1, L, SSM_GROUPS, SSM_STATE))
    a_im = jnp.broadcast_to(ai, (1, L, SSM_GROUPS, SSM_STATE))
    _, _, xr, xi = lax.associative_scan(_s5_combine, (a_re, a_im, bu_re, bu_im), axis=1)
    y = (jnp.einsum('blgp,ghp->blgh', xr, c_re.astype(jnp.float32))
         - jnp.einsum('blgp,ghp->blgh', xi, c_im.astype(jnp.float32))
         + d.astype(jnp.float32) * uf)
    y = jax.nn.gelu(y.reshape(bsz, L, SSM_WIDTH))
    z = y @ w_glu.astype(jnp.float32) + b_glu.astype(jnp.float32)
    out = z[..., :SSM_WIDTH] * jax.nn.sigmoid(z[..., SSM_WIDTH:])
    return out.astype(u.dtype)

def partial_rotary(t, positions):
    half = ROPE_DIM // 2
    inv_freq = ROPE_THETA ** (-jnp.arange(half, dtype=jnp.float32) * 2.0 / ROPE_DIM)
    ang = positions.astype(jnp.float32)[..., None] * inv_freq
    cos = jnp.cos(ang)[:, :, None, :]
    sin = jnp.sin(ang)[:, :, None, :]
    tf = t.astype(jnp.float32)
    t1 = tf[..., :half]
    t2 = tf[..., half:ROPE_DIM]
    rot = jnp.concatenate([t1 * cos - t2 * sin, t2 * cos + t1 * sin, tf[..., ROPE_DIM:]], axis=-1)
    return rot.astype(t.dtype)

def sliding_window_sink_attention(q, k, v, sinks):
    bsz, L = q.shape[0], q.shape[1]
    nb = L // BLOCK
    qb = q.reshape(bsz, nb, BLOCK, N_KV_HEADS, Q_PER_KV, HEAD_DIM).transpose(1, 0, 2, 3, 4, 5)

    def windows(t):
        tb = t.reshape(bsz, nb, BLOCK, N_KV_HEADS, HEAD_DIM)
        prev = jnp.pad(tb, ((0, 0), (1, 0), (0, 0), (0, 0), (0, 0)))[:, :-1]
        return jnp.concatenate([prev, tb], axis=2).transpose(1, 0, 2, 3, 4)

    kw = windows(k)
    vw = windows(v)
    qi = jnp.arange(BLOCK)[:, None]
    kj = jnp.arange(2 * BLOCK)[None, :]
    rel = qi + BLOCK - kj
    band = (rel >= 0) & (rel < WINDOW)
    sink = sinks.astype(jnp.float32).reshape(N_KV_HEADS, Q_PER_KV)[None, :, :, None, None]
    scale = HEAD_DIM ** -0.5

    def one_block(args):
        q_blk, k_blk, v_blk, blk = args
        valid = band & (blk * BLOCK - BLOCK + kj >= 0)
        s = jnp.einsum('bqhgd,bkhd->bhgqk', q_blk, k_blk).astype(jnp.float32) * scale
        s = jnp.where(valid, s, MASK_VALUE)
        m = jnp.maximum(jnp.max(s, axis=-1, keepdims=True), sink)
        p = jnp.exp(s - m)
        p = p / (jnp.sum(p, axis=-1, keepdims=True) + jnp.exp(sink - m))
        return jnp.einsum('bhgqk,bkhd->bqhgd', p.astype(v_blk.dtype), v_blk)

    o = lax.map(one_block, (qb, kw, vw, jnp.arange(nb)))
    return o.transpose(1, 0, 2, 3, 4, 5).reshape(bsz, L, ATTN_WIDTH)

def first_inputs(seed: int = 0) -> dict:
    key = jax.random.key(seed)
    ks = jax.random.split(key, 24)
    f32 = jnp.float32

    def nrm(k, shape, std):
        return jax.random.normal(k, shape, f32) * std

    def gain(k, n):
        return 1.0 + 0.05 * jax.random.normal(k, (DEPTH, n), f32)

    n_idx = jnp.arange(SSM_STATE, dtype=f32)
    lam_re = -0.5 + 0.01 * jax.random.normal(ks[3], (DEPTH, SSM_GROUPS, SSM_STATE), f32)
    lam_im = math.pi * n_idx + 0.01 * jax.random.normal(ks[4], (DEPTH, SSM_GROUPS, SSM_STATE), f32)
    log_dt = jax.random.uniform(ks[5], (DEPTH, SSM_GROUPS), f32, math.log(DT_MIN), math.log(DT_MAX))
    return {
        "x": jax.random.normal(ks[0], (BATCH, SEQ, D_MODEL), f32),
        "positions": jnp.broadcast_to(jnp.arange(SEQ, dtype=jnp.int32), (BATCH, SEQ)),
        "g_pre_mix": gain(ks[1], D_MODEL),
        "w_in": nrm(ks[2], (DEPTH, D_MODEL, IN_WIDTH), D_MODEL ** -0.5),
        "ssm_lambda_re": lam_re,
        "ssm_lambda_im": lam_im,
        "ssm_log_dt": log_dt,
        "ssm_b_re": nrm(ks[6], (DEPTH, SSM_GROUPS, SSM_STATE, SSM_GROUP), (2 * SSM_GROUP) ** -0.5),
        "ssm_b_im": nrm(ks[7], (DEPTH, SSM_GROUPS, SSM_STATE, SSM_GROUP), (2 * SSM_GROUP) ** -0.5),
        "ssm_c_re": nrm(ks[8], (DEPTH, SSM_GROUPS, SSM_GROUP, SSM_STATE), (2 * SSM_STATE) ** -0.5),
        "ssm_c_im": nrm(ks[9], (DEPTH, SSM_GROUPS, SSM_GROUP, SSM_STATE), (2 * SSM_STATE) ** -0.5),
        "ssm_d": nrm(ks[10], (DEPTH, SSM_GROUPS, SSM_GROUP), 1.0),
        "w_glu": nrm(ks[11], (DEPTH, SSM_WIDTH, 2 * SSM_WIDTH), SSM_WIDTH ** -0.5),
        "b_glu": nrm(ks[12], (DEPTH, 2 * SSM_WIDTH), 0.01),
        "attn_sinks": nrm(ks[13], (DEPTH, N_Q_HEADS), 0.5),
        "g_ssm_out": gain(ks[14], SSM_WIDTH),
        "g_attn_out": gain(ks[15], ATTN_WIDTH),
        "w_out": nrm(ks[16], (DEPTH, MIX_WIDTH, D_MODEL), MIX_WIDTH ** -0.5),
        "g_post_mix": gain(ks[17], D_MODEL),
        "g_pre_ffn": gain(ks[18], D_MODEL),
        "w_gate_up": nrm(ks[19], (DEPTH, D_MODEL, 2 * D_FF), D_MODEL ** -0.5),
        "w_down": nrm(ks[20], (DEPTH, D_FF, D_MODEL), D_FF ** -0.5),
        "g_post_ffn": gain(ks[21], D_MODEL),
    }

def first_block(x, positions, g_pre_mix, w_in, ssm_lambda_re, ssm_lambda_im, ssm_log_dt,
              ssm_b_re, ssm_b_im, ssm_c_re, ssm_c_im, ssm_d, w_glu, b_glu, attn_sinks,
              g_ssm_out, g_attn_out, w_out, g_post_mix, g_pre_ffn, w_gate_up, w_down, g_post_ffn):
    bsz, L, _ = x.shape
    h = x
    for l in range(DEPTH):
        hn = rms_norm(h, g_pre_mix[l])
        proj = hn @ w_in[l]
        u = proj[..., :SSM_WIDTH]
        q = proj[..., SSM_WIDTH:SSM_WIDTH + ATTN_WIDTH]
        k = proj[..., SSM_WIDTH + ATTN_WIDTH:SSM_WIDTH + ATTN_WIDTH + KV_WIDTH]
        v = proj[..., SSM_WIDTH + ATTN_WIDTH + KV_WIDTH:]

        y_ssm = s5_mixer(u, ssm_lambda_re[l], ssm_lambda_im[l], ssm_log_dt[l],
                         ssm_b_re[l], ssm_b_im[l], ssm_c_re[l], ssm_c_im[l], ssm_d[l],
                         w_glu[l], b_glu[l])

        q = partial_rotary(q.reshape(bsz, L, N_Q_HEADS, HEAD_DIM), positions)
        k = partial_rotary(k.reshape(bsz, L, N_KV_HEADS, HEAD_DIM), positions)
        v = v.reshape(bsz, L, N_KV_HEADS, HEAD_DIM)
        y_attn = sliding_window_sink_attention(q, k, v, attn_sinks[l])

        merged = jnp.concatenate([rms_norm(y_ssm, g_ssm_out[l]), rms_norm(y_attn, g_attn_out[l])], axis=-1)
        h = h + rms_norm(merged @ w_out[l], g_post_mix[l])

        hn = rms_norm(h, g_pre_ffn[l])
        gu = hn @ w_gate_up[l]
        ff = (jax.nn.silu(gu[..., :D_FF]) * gu[..., D_FF:]) @ w_down[l]
        h = h + rms_norm(ff, g_post_ffn[l])
    return h


DEPTH_2 = 2

N_MIXERS = 2
N_ATTN_LAYERS = (DEPTH_2 + 1) // 2
N_HGRN_LAYERS = DEPTH_2 // 2
ATTN_HEAD_DIM = 64
ATTN_HEADS = D_MODEL // ATTN_HEAD_DIM
DILATED_PATTERNS = ((128, 1), (512, 4), (2048, 16))
N_GROUPS = len(DILATED_PATTERNS)
ROPE_THETA_2 = 10000.0
HGRN_EXPAND = 128
HGRN_HEADS = D_MODEL // HGRN_EXPAND
HGRN_DK = HGRN_EXPAND
HGRN_DV = D_MODEL // HGRN_HEADS
HGRN_CHUNK = 64
D_FF_2 = 4 * D_MODEL
LN_EPS = 1e-5
RMS_EPS = 1e-6
DEEPNORM_ALPHA = (2 * DEPTH_2) ** 0.25
DEEPNORM_BETA = (8 * DEPTH_2) ** -0.25


F32 = jnp.float32

def layer_norm(x, g, b):
    xf = x.astype(F32)
    mu = jnp.mean(xf, axis=-1, keepdims=True)
    var = jnp.mean(jnp.square(xf - mu), axis=-1, keepdims=True)
    return ((xf - mu) * lax.rsqrt(var + LN_EPS) * g.astype(F32) + b.astype(F32)).astype(x.dtype)

def rotary(x, pos):
    e = x.shape[-1]
    half = e // 2
    inv = ROPE_THETA_2 ** (-jnp.arange(half, dtype=F32) * (2.0 / e))
    ang = pos.astype(F32)[:, None] * inv[None, :]
    cos = jnp.cos(ang)[None, :, None, :]
    sin = jnp.sin(ang)[None, :, None, :]
    xf = x.astype(F32)
    x1, x2 = xf[..., :half], xf[..., half:]
    return jnp.concatenate([x1 * cos - x2 * sin, x2 * cos + x1 * sin], axis=-1).astype(x.dtype)

def dilated_window_attention(q, k, v, window, dilation):
    B, S, H, E = q.shape
    blk = window // dilation
    span = dilation * blk
    s_pad = -(-S // span) * span
    n = s_pad // dilation
    nb = n // blk
    pad = ((0, 0), (0, s_pad - S), (0, 0), (0, 0))

    def to_blocks(t):
        t = jnp.pad(t, pad).reshape(B, n, dilation, H, E).transpose(0, 2, 1, 3, 4)
        return t.reshape(B * dilation, nb, blk, H, E)

    def with_prev(t):
        prev = jnp.pad(t, ((0, 0), (1, 0), (0, 0), (0, 0), (0, 0)))[:, :-1]
        return jnp.concatenate([prev, t], axis=2)

    qb, kb, vb = to_blocks(q), to_blocks(k), to_blocks(v)
    kk, vv = with_prev(kb), with_prev(vb)
    s = jnp.einsum('znqhe,znkhe->znhqk', qb, kk).astype(F32) * (E ** -0.5)
    qi = jnp.arange(blk)[:, None]
    kj = jnp.arange(2 * blk)[None, :]
    dist = qi + blk - kj
    in_band = (dist >= 0) & (dist <= blk)
    kabs = jnp.arange(nb)[:, None, None] * blk + kj[None] - blk
    valid = in_band[None] & (kabs >= 0)
    s = jnp.where(valid[None, :, None], s, -jnp.inf)
    m = jnp.max(s, axis=-1, keepdims=True)
    p = jnp.exp(s - m)
    l = jnp.sum(p, axis=-1, keepdims=True)
    o = jnp.einsum('znhqk,znkhe->znqhe', (p / l).astype(v.dtype), vv)
    lse = (m + jnp.log(l))[..., 0].transpose(0, 1, 3, 2)

    def from_blocks(t):
        t = t.reshape(B, dilation, n, *t.shape[3:]).swapaxes(1, 2)
        return t.reshape(B, s_pad, *t.shape[3:])[:, :S]

    return from_blocks(o), from_blocks(lse)

def dilated_attention_mixer(x, w_in, w_out):
    B, S, _ = x.shape
    proj = (x @ w_in).reshape(B, S, N_GROUPS, 3, ATTN_HEADS, ATTN_HEAD_DIM)
    pos = jnp.arange(S)
    outs, lses = [], []
    for g, (window, dilation) in enumerate(DILATED_PATTERNS):
        q = rotary(proj[:, :, g, 0], pos)
        k = rotary(proj[:, :, g, 1], pos)
        o, lse = dilated_window_attention(q, k, proj[:, :, g, 2], window, dilation)
        outs.append(o)
        lses.append(lse)
    wts = jax.nn.softmax(jnp.stack(lses, axis=0), axis=0)
    o = jnp.einsum('gbsh,gbshe->bshe', wts, jnp.stack(outs, axis=0).astype(F32))
    return o.reshape(B, S, ATTN_HEADS * ATTN_HEAD_DIM).astype(x.dtype) @ w_out

def forget_lower_bounds(lb_logits):
    c = jnp.cumsum(jax.nn.softmax(lb_logits.astype(F32), axis=0), axis=0)
    return c - c[0]

def hgrn2_mixer(x, w_in, w_out, norm_g, lb):
    B, S, _ = x.shape
    H, K, V, C = HGRN_HEADS, HGRN_DK, HGRN_DV, HGRN_CHUNK
    nc = S // C
    q_raw, f_raw, i_raw = jnp.split(x @ w_in, [H * K, 2 * H * K], axis=-1)
    z = f_raw.astype(F32)
    log_f = jnp.logaddexp(jnp.log(lb), jnp.log1p(-lb) + jax.nn.log_sigmoid(z))
    key = (1.0 - lb) * jax.nn.sigmoid(-z)
    q = jax.nn.silu(q_raw.astype(F32))
    v = i_raw.astype(F32)

    def chunks(t, d):
        return t.reshape(B, nc, C, H, d).transpose(0, 3, 1, 2, 4)

    q, key, log_f, v = chunks(q, K), chunks(key, K), chunks(log_f, K), chunks(v, V)
    b = jnp.cumsum(log_f, axis=3)
    q_dec = q * jnp.exp(b)
    k_dec = key * jnp.exp(-b)
    causal = jnp.tril(jnp.ones((C, C), dtype=bool))
    a = jnp.where(causal, jnp.einsum('bhcid,bhcjd->bhcij', q_dec, k_dec), 0.0)
    o_intra = jnp.einsum('bhcij,bhcje->bhcie', a, v)
    b_last = b[:, :, :, -1:, :]
    kv = jnp.einsum('bhcjd,bhcje->bhcde', key * jnp.exp(b_last - b), v)
    chunk_decay = jnp.exp(b_last[:, :, :, 0, :])

    def step(state, inp):
        dec, kv_c = inp
        return dec[..., None] * state + kv_c, state

    s0 = jnp.zeros((B, H, K, V), F32)
    _, states = lax.scan(step, s0, (jnp.moveaxis(chunk_decay, 2, 0), jnp.moveaxis(kv, 2, 0)))
    o_inter = jnp.einsum('bhcid,cbhde->bhcie', q_dec, states)
    o = (o_intra + o_inter).transpose(0, 2, 3, 1, 4).reshape(B, S, H, V)
    o = o * lax.rsqrt(jnp.mean(o * o, axis=-1, keepdims=True) + RMS_EPS) * norm_g.astype(F32).reshape(H, V)
    return o.reshape(B, S, H * V).astype(x.dtype) @ w_out

def squared_relu_mlp(x, w_up, w_down):
    return jnp.square(jax.nn.relu(x @ w_up)) @ w_down

def second_inputs(seed: int = 0) -> dict:
    key = jax.random.key(seed)
    ks = jax.random.split(key, 13)
    d_attn_in = N_GROUPS * 3 * ATTN_HEADS * ATTN_HEAD_DIM
    d_attn_out = ATTN_HEADS * ATTN_HEAD_DIM
    d_hgrn_in = 2 * HGRN_HEADS * HGRN_DK + HGRN_HEADS * HGRN_DV
    d_hgrn_out = HGRN_HEADS * HGRN_DV
    nrm = lambda k, shape, scale: jax.random.normal(k, shape, F32) * scale
    return {
        'x': nrm(ks[0], (BATCH, SEQ, D_MODEL), 1.0),
        'attn_w_in': nrm(ks[1], (N_ATTN_LAYERS, D_MODEL, d_attn_in), D_MODEL ** -0.5),
        'attn_w_out': nrm(ks[2], (N_ATTN_LAYERS, d_attn_out, D_MODEL), d_attn_out ** -0.5 * DEEPNORM_BETA),
        'hgrn_w_in': nrm(ks[3], (N_HGRN_LAYERS, D_MODEL, d_hgrn_in), D_MODEL ** -0.5),
        'hgrn_w_out': nrm(ks[4], (N_HGRN_LAYERS, d_hgrn_out, D_MODEL), d_hgrn_out ** -0.5 * DEEPNORM_BETA),
        'hgrn_norm_g': 1.0 + nrm(ks[5], (N_HGRN_LAYERS, d_hgrn_out), 0.02),
        'lb_logits': nrm(ks[6], (DEPTH_2, HGRN_HEADS * HGRN_DK), 0.1),
        'ln_mix_g': 1.0 + nrm(ks[7], (DEPTH_2, D_MODEL), 0.02),
        'ln_mix_b': nrm(ks[8], (DEPTH_2, D_MODEL), 0.02),
        'ln_ffn_g': 1.0 + nrm(ks[9], (DEPTH_2, D_MODEL), 0.02),
        'ln_ffn_b': nrm(ks[10], (DEPTH_2, D_MODEL), 0.02),
        'ffn_w_up': nrm(ks[11], (DEPTH_2, D_MODEL, D_FF_2), D_MODEL ** -0.5),
        'ffn_w_down': nrm(ks[12], (DEPTH_2, D_FF_2, D_MODEL), D_FF_2 ** -0.5 * DEEPNORM_BETA),
    }

def second_block(x, attn_w_in, attn_w_out, hgrn_w_in, hgrn_w_out, hgrn_norm_g, lb_logits,
              ln_mix_g, ln_mix_b, ln_ffn_g, ln_ffn_b, ffn_w_up, ffn_w_down):
    lbs = forget_lower_bounds(lb_logits)
    for i in range(DEPTH_2):
        j = i // N_MIXERS
        if i % N_MIXERS == 0:
            y = dilated_attention_mixer(x, attn_w_in[j], attn_w_out[j])
        else:
            y = hgrn2_mixer(x, hgrn_w_in[j], hgrn_w_out[j], hgrn_norm_g[j], lbs[i])
        x = layer_norm(DEEPNORM_ALPHA * x + y, ln_mix_g[i], ln_mix_b[i])
        y = squared_relu_mlp(x, ffn_w_up[i], ffn_w_down[i])
        x = layer_norm(DEEPNORM_ALPHA * x + y, ln_ffn_g[i], ln_ffn_b[i])
    return x


def setup_inputs(seed=0):
    out = dict(first_inputs(seed))
    for name, value in second_inputs(seed + 1).items():
        if name != "x":
            out[name + "_2"] = value
    return out


def reference(
    x, positions, g_pre_mix, w_in, ssm_lambda_re, ssm_lambda_im, ssm_log_dt, ssm_b_re, ssm_b_im,
    ssm_c_re, ssm_c_im, ssm_d, w_glu, b_glu, attn_sinks, g_ssm_out, g_attn_out, w_out,
    g_post_mix, g_pre_ffn, w_gate_up, w_down, g_post_ffn, attn_w_in_2, attn_w_out_2,
    hgrn_w_in_2, hgrn_w_out_2, hgrn_norm_g_2, lb_logits_2, ln_mix_g_2, ln_mix_b_2, ln_ffn_g_2,
    ln_ffn_b_2, ffn_w_up_2, ffn_w_down_2,
):
    x = first_block(
        x, positions, g_pre_mix, w_in, ssm_lambda_re, ssm_lambda_im, ssm_log_dt, ssm_b_re,
        ssm_b_im, ssm_c_re, ssm_c_im, ssm_d, w_glu, b_glu, attn_sinks, g_ssm_out, g_attn_out,
        w_out, g_post_mix, g_pre_ffn, w_gate_up, w_down, g_post_ffn,
    )
    return second_block(
        x, attn_w_in_2, attn_w_out_2, hgrn_w_in_2, hgrn_w_out_2, hgrn_norm_g_2, lb_logits_2,
        ln_mix_g_2, ln_mix_b_2, ln_ffn_g_2, ln_ffn_b_2, ffn_w_up_2, ffn_w_down_2,
    )


_drawn_inputs = setup_inputs


def setup_inputs(seed=0):
    import zlib

    import numpy as np

    out = dict(_drawn_inputs(seed))
    spreads = {}
    factors = {'ssm_lambda_re': 200.0,
     'b_glu': 5.164,
     'attn_sinks': 7.005,
     'hgrn_norm_g_2': 67.866,
     'lb_logits_2': 8.0,
     'ssm_lambda_im': 35.104,
     'ssm_log_dt': 40.856,
     'ssm_b_re': 48.376,
     'ssm_b_im': 48.768,
     'ssm_c_re': 48.768,
     'ssm_c_im': 48.928}
    for name, (base, spread) in spreads.items():
        noise = np.random.default_rng([zlib.crc32(name.encode()), seed]).standard_normal(out[name].shape)
        drawn = base * np.exp(spread * noise) if base else spread * noise
        out[name] = __import__('jax').numpy.asarray(drawn.astype(out[name].dtype))
    for name, factor in factors.items():
        out[name] = (out[name] * factor).astype(out[name].dtype)
    return out
```

```python
from contextlib import ExitStack

import numpy as np

import concourse.bass as bass
from concourse import mybir

P = 128
T = 512
D = 1024
DC = D // P
TB = T // P
HALF = 512
N_PAIR = 16
GW = 32
DFF = 2816
FFN1_PARTS = (12, 10)
FFN2_PART = 16
HEAD_PAIRS = 8
GROUPS = 3
PAIR_TILES = 3 * GROUPS
CHUNK = 64
HG_HEADS = 8
SLAB = 2048
ALPHA = 4.0 ** 0.25
RMS_EPS = 1e-6
LN_EPS = 1e-5
NEG = -1e30
TWO_PI = 2.0 * np.pi
PI_HI = 6.28125
PI_LO = TWO_PI - PI_HI
PI_IN = 3.1415925
ROUND = 1.5 * 2.0 ** 23
LN2_HI = 0.693359375
LN2_LO = float(np.log(2.0) - 0.693359375)


class Stage:

    def __init__(self, name, slab0, tile0, slabs, kc, body, before, free0):
        self.name, self.slab0, self.tile0, self.slabs = name, slab0, tile0, slabs
        self.kc, self.body = kc, body
        self.reader = "act" if name.startswith(("attn_in", "up_", "hgrn_in")) else "dve"
        self.free0 = free0[self.reader]
        self.before = before
        self.cum = [0]
        for n in body:
            self.cum.append(self.cum[-1] + n)
        self.trips = slabs // len(body)
        self.tiles = self.cum[-1] * self.trips


def plan():
    rows = [("w_in", 5, 8, [2] * 5), ("w_glu", 2, 4, [4, 4]), ("w_out", 4, 8, [2, 2])]
    for n, c in enumerate(FFN1_PARTS):
        rows += [(f"gate_up{n}", c, 8, [2, 2]), (f"down{n}", 8, c, [1, 1])]
    rows += [("attn_in", 5 * HEAD_PAIRS, 8, [2, 2, 2, 2, 1] * 2), ("attn_out", 4, 8, [2, 2])]
    for n in range(2):
        rows += [(f"up_a{n}", 8, 8, [2, 2]), (f"down_a{n}", 8, 16, [1, 1])]
    rows += [("hgrn_in", 12, 8, [2] * 6), ("hgrn_out", 4, 8, [2, 2])]
    for n in range(2):
        rows += [(f"up_h{n}", 8, 8, [2, 2]), (f"down_h{n}", 8, 16, [1, 1])]
    stages, slab, tile, s, free = {}, 0, 0, None, {"act": 0, "dve": 0}
    for name, slabs, kc, body in rows:
        s = Stage(name, slab, tile, slabs, kc, body, s, free)
        stages[name] = s
        slab, tile = slab + s.slabs, tile + s.tiles
        free[s.reader] += s.tiles
    return stages


STAGES = plan()
GAINS = ["g_pre_mix", "g_ssm", "g_attn", "g_post_mix", "g_pre_ffn", "g_post_ffn", "d", "b_glu", "g_hgrn", "lb0", "lb1",
         "ln_mix_g0", "ln_mix_b0", "ln_ffn_g0", "ln_ffn_b0", "ln_mix_g1", "ln_mix_b1", "ln_ffn_g1", "ln_ffn_b1"]
GAIN_COLS = [8, 4, 4, 8, 8, 8, 4, 8, 8, 8, 8] + [8] * 8
GAIN_AT = dict(zip(GAINS, np.cumsum([0] + GAIN_COLS[:-1]).tolist()))
N_GAIN = sum(GAIN_COLS)


def build(nc, w, x_in, gains_in, lam_in, sink_in, b_in, c_in, pos_in, iota_in, const_in, freq_in, mask_in, rope2_in,
          hmask_in, out):
    f32, f32r, bf16, i32 = mybir.dt.float32, mybir.dt.float32r, mybir.dt.bfloat16, mybir.dt.int32
    ALU, ACT, AX = mybir.AluOpType, mybir.ActivationFunctionType, mybir.AxisListType
    ds = bass.ds

    base = (nc.sbuf_base + 63) // 64 * 64
    KB = 1024
    RAW_AT = base
    WH_AT = RAW_AT + 16 * KB
    WL_AT = WH_AT + 16 * KB
    XH_AT = WL_AT + 16 * KB
    XL_AT = XH_AT + 16 * KB
    H_AT = XL_AT + 16 * KB
    Y_AT = H_AT + 16 * KB
    BIG_AT = Y_AT + 16 * KB
    EX_AT = BIG_AT + 64 * KB
    used = [EX_AT]

    def at(name, offset, shape, dt=f32):
        return nc.alloc_sbuf_tensor_at(name, [P] + list(shape), dt, offset=offset)

    where = {}

    def extra(name, shape, dt=f32):
        size = int(np.prod(shape)) * (2 if dt == bf16 else 4)
        where[name] = used[0]
        used[0] += (size + 31) // 32 * 32
        return at(name, where[name], shape, dt)

    raw = at("raw", RAW_AT, [2, SLAB])
    w_hi = at("w_hi", WH_AT, [2, SLAB], f32r)
    w_lo = at("w_lo", WL_AT, [2, SLAB], f32r)
    x_hi = at("x_hi", XH_AT, [DC, T], f32r)
    x_lo = at("x_lo", XL_AT, [DC, T], f32r)
    h = at("h", H_AT, [DC, T])
    y = at("y", Y_AT, [DC, T])
    hid_hi = at("hid_hi", BIG_AT, [16, T], f32r)
    hid_lo = at("hid_lo", BIG_AT + 32 * KB, [16, T], f32r)

    x_raw = at("x_raw", Y_AT, [DC, T])
    u = at("u", Y_AT, [4, T])
    q1 = at("q1", Y_AT + 8 * KB, [4, T])
    o1_tok = at("o1_tok", Y_AT, [TB, HALF])
    mask_raw = at("mask_raw", H_AT, [1536])
    b_re = at("b_re", BIG_AT + 56 * KB, [N_PAIR, GW])
    b_im = at("b_im", BIG_AT + 58 * KB, [N_PAIR, GW])
    bb_re = at("bb_re", BIG_AT + 60 * KB, [N_PAIR, GW])
    bb_im = at("bb_im", BIG_AT + 62 * KB, [N_PAIR, GW])
    cos_t = at("cos_t", BIG_AT, [N_PAIR, T])
    sin_t = at("sin_t", BIG_AT + 32 * KB, [N_PAIR, T])
    prod = at("prod", H_AT, [4, T])
    k1 = at("k1", H_AT + 8 * KB, [T])
    v1 = at("v1", H_AT + 10 * KB, [T])
    v1_tok = at("v1_tok", H_AT + 12 * KB, [TB, P])
    qr1 = at("qr1", H_AT + 14 * KB, [T])
    mod = at("mod", XH_AT + 8 * KB, [4, T])
    scan = at("scan", XL_AT + 8 * KB, [2, T])
    p1 = at("p1", XL_AT + 12 * KB, [2, 2 * P])
    p1_t = at("p1_t", XL_AT + 14 * KB, [2, 2 * P])

    qkv = at("qkv", BIG_AT, [2, PAIR_TILES, T])
    v_tok = at("v_tok", BIG_AT + 36 * KB, [2, GROUPS, TB, P])
    p2 = at("p2", BIG_AT + 48 * KB, [2, 10 * P])
    p2_t = at("p2_t", BIG_AT + 58 * KB, [10 * P])
    o2_tok = at("o2_tok", Y_AT, [TB, D])

    hg_q = at("hg_q", BIG_AT, [HG_HEADS, T])
    hg_s = at("hg_s", BIG_AT + 16 * KB, [HG_HEADS, T])
    hg_k = at("hg_k", BIG_AT + 32 * KB, [HG_HEADS, T])
    hg_v = at("hg_v", BIG_AT + 48 * KB, [HG_HEADS, T])
    f_run = at("f_run", Y_AT, [T])
    f_start = at("f_start", Y_AT + 2 * KB, [T])
    f_cum = at("f_cum", Y_AT + 4 * KB, [T])
    q_dec = at("q_dec", Y_AT + 6 * KB, [T])
    k_dec = at("k_dec", Y_AT + 8 * KB, [T])
    v_head = at("v_head", Y_AT + 10 * KB, [T])
    k_tok = at("k_tok", Y_AT + 12 * KB, [TB, P])
    v_htok = at("v_htok", Y_AT + 14 * KB, [TB, P])

    consts = extra("consts", [4, P])
    ident, swap1, swap2, ones = (consts[:, n, :] for n in range(4))
    ident_b = extra("ident_b", [P], bf16)
    masks = extra("masks", [1536], bf16)
    rope_c = extra("rope_c", [T])
    rope_s = extra("rope_s", [T])
    gains = extra("gains", [N_GAIN])
    lam = extra("lam", [3, N_PAIR])
    par = extra("par", [26, N_PAIR])
    sink = extra("sink", [8])
    eps = extra("eps", [3])
    freq = extra("freq", [1])
    sq = extra("sq", [2, T])
    root = extra("root", [T])
    rstd = extra("rstd", [T])
    tmp = extra("tmp", [4, T])
    c_re = extra("c_re", [N_PAIR, GW])
    c_im = extra("c_im", [N_PAIR, GW])
    assert used[0] <= nc.sbuf_usable_end, used[0] - nc.sbuf_usable_end
    b_lhs = at("b_lhs", where["sq"], [2, 4, P])
    c_neg = at("c_neg", where["root"], [N_PAIR, GW])
    iota = at("iota", where["tmp"] + 6 * KB, [T])
    pos = at("pos", where["tmp"], [T], i32)
    a_mask = at("a_mask", where["c_re"], [T])
    run_mask = at("run_mask", where["rope_c"], [T])
    stat = at("stat", where["c_im"], [2, 8])
    lbp = at("lbp", where["c_im"] + 256, [6, HG_HEADS])
    start_mask = at("start_mask", where["rope_s"], [T])
    state = at("state", where["tmp"] + 2 * KB, [8, P])
    m1, m2, mp2, mp3 = masks[:, 0:256], masks[:, 256:512], masks[:, 512:1024], masks[:, 1024:1536]

    def gain(name, c):
        return gains[:, GAIN_AT[name] + c:GAIN_AT[name] + c + 1]

    def chunk(buf, c):
        if isinstance(c, int):
            return buf[:, c, :]
        return buf[:, ds(c, 1), :].rearrange("p a t -> p (a t)")

    ps = nc.alloc_psum_tensor("ps", [P, 8, T], f32)
    SUM = 7

    def counts(rows):
        at_, n = {}, 0
        for name, c in rows:
            at_[name] = n
            n += c
        return at_

    XB = counts([("w_in", 8), ("w_glu", 4), ("w_out", 8), ("gate_up", 8), ("attn_in", 8), ("attn_out", 8),
                 ("up_a", 8), ("hgrn_in", 8), ("hgrn_out", 8), ("up_h", 8)])
    LN = [(f"{kind}_{part}_{layer}", 8) for layer in "ah" for part in ("mix", "ffn") for kind in ("out", "mid", "res")]
    YB = counts([("attn1", 4), ("glu", 4), ("w_out", 8), ("res_mix", 8), ("ffn", 8), ("res_ffn", 8)] + LN)
    HB = counts([("0", FFN1_PARTS[0]), ("1", FFN1_PARTS[1])] +
                [(f"{layer}{n}", FFN2_PART) for layer in "ah" for n in range(2)])
    SUMS = [("pre_mix", 8), ("ssm", 4), ("attn", 4), ("post_mix", 8), ("pre_ffn", 8), ("post_ffn", 8)]
    for part in ("mix_a", "ffn_a"):
        SUMS += [("mean_" + part, 0), ("var_" + part, 8)]
    SUMS += [(f"head{n}", 1) for n in range(HG_HEADS)]
    for part in ("mix_h", "ffn_h"):
        SUMS += [("mean_" + part, 0), ("var_" + part, 8)]
    SB = counts(SUMS)
    SK = {name: k for k, (name, _) in enumerate(SUMS)}
    MEANS = {"amix": 0, "affn": 1, "hmix": 2, "hffn": 3}
    SK_ROOT = counts([(name, 1 if n else 0) for name, n in SUMS])
    PR = {name: k for k, name in enumerate(
        ["lr", "dt", "z", "k", "f", "e", "two_k", "em1", "mag", "th", "r", "r_turn", "r_hi", "r_lo", "sin", "sin_half",
         "c1", "am1", "ai", "den", "nr", "ni", "fr", "fi", "t0", "t1"])}

    def sem(name):
        return nc.alloc_semaphore(name)

    raw_ready = [sem("raw_ready0"), sem("raw_ready1")]
    whi_ready = sem("whi_ready")
    wlo_ready = sem("wlo_ready")
    tile_done = sem("tile_done")
    tile_free = {e: sem("tile_free_" + e) for e in ("dve", "act")}
    xhi_ready = sem("xhi_ready")
    xlo_ready = sem("xlo_ready")
    y_ready = sem("y_ready")
    merge_ready = sem("merge_ready")
    gate_scaled = sem("gate_scaled")
    silu_ready = sem("silu_ready")
    hid_pre = sem("hid_pre")
    hid_half = sem("hid_half")
    hid_ready = sem("hid_ready")
    sq_ready = sem("sq_ready")
    sq_used = sem("sq_used")
    mean_ready = sem("mean_ready")
    root_ready = sem("root_ready")
    rstd_ready = sem("rstd_ready")
    x_ready = [sem("x_ready0"), sem("x_ready1")]
    small_ready = sem("small_ready")
    eps_ready = sem("eps_ready")
    mask_ready = sem("mask_ready")
    dt_ready = sem("dt_ready")
    turn_ready = sem("turn_ready")
    sines_ready = sem("sines_ready")
    rope_ang = sem("rope_ang")
    rope_ready = sem("rope_ready")
    bb_ready = sem("bb_ready")
    bt_done = sem("bt_done")
    blhs_ready = sem("blhs_ready")
    ang_ready = sem("ang_ready")
    ang_used = sem("ang_used")
    bu_done = sem("bu_done")
    bu_free = sem("bu_free")
    scan_ready = sem("scan_ready")
    prod_ready = sem("prod_ready")
    yssm_done = sem("yssm_done")
    pre_gelu = sem("pre_gelu")
    gelu_ready = sem("gelu_ready")
    gate_ready = sem("gate_ready")
    vt1_done, vt1_ready = sem("vt1_done"), sem("vt1_ready")
    kr1_swap, kr1_ready = sem("kr1_swap"), sem("kr1_ready")
    qr1_swap, qr1_ready = sem("qr1_swap"), sem("qr1_ready")
    s1_done = sem("s1_done")
    max1_ready = sem("max1_ready")
    p1_ready = sem("p1_ready")
    p1t_done, p1t_ready = sem("p1t_done"), sem("p1t_ready")
    o1_done, o1_ready = sem("o1_done"), sem("o1_ready")
    o1t_done = sem("o1t_done")
    h_back = sem("h_back")
    swap_done = sem("swap_done")
    rot_ready = sem("rot_ready")
    vtok_ready = sem("vtok_ready")
    s2_done, max2_ready, p2_ready = sem("s2_done"), sem("max2_ready"), sem("p2_ready")
    p2t_done = sem("p2t_done")
    p2t_dve, p2t_act = sem("p2t_dve"), sem("p2t_act")
    o2_done, o2_ready = sem("o2_done"), sem("o2_ready")
    o2t_done = sem("o2t_done")
    rope2_ready = sem("rope2_ready")
    hm_ready = sem("hm_ready")
    lb_half, lb_exp = sem("lb_half"), sem("lb_exp")
    dec_ready, vh_ready = sem("dec_ready"), sem("vh_ready")
    a_done, a_ready = sem("a_done"), sem("a_ready")
    ht_done, ht_ready = sem("ht_done"), sem("ht_ready")
    kv_done, st_ready = sem("kv_done"), sem("st_ready")
    oh_done, oh_ready = sem("oh_done"), sem("oh_ready")
    out_done = sem("out_done")

    LAST = STAGES["down_h1"]
    SMALL = 12
    BLOCKS1 = [(b, min(b, 1) + 1) for b in range(TB)]
    BLOCKS2 = [(b, min(b, 1) + 1, b + 1) for b in range(TB)]
    STEPS2 = [(hh, *blk) for hh in range(2) for blk in BLOCKS2]
    ROUNDS = [-(-(n1 + 2 * n2) // 4) for _, _, n1, n2 in STEPS2]
    TURNS = np.cumsum([0] + ROUNDS).tolist()
    DVE_TURNS = np.cumsum([0] + [(r + 1) // 2 for r in ROUNDS]).tolist()
    ACT_TURNS = np.cumsum([0] + [r // 2 for r in ROUNDS]).tolist()

    def run(eng, st, body):
        if st.trips == 1:
            body(0, False)
        elif st is LAST:
            with eng.Fori(0, st.trips - 1) as i:
                body(i, False)
            body(st.trips - 1, True)
        else:
            with eng.Fori(0, st.trips) as i:
                body(i, False)

    with nc.Block() as block:

        @block.sync
        def _(sp):
            for half in range(2):
                sp.dma_start(x_raw[:, 4 * half:4 * half + 4, :], x_in[:, 4 * half:4 * half + 4, :]) \
                  .then_inc(x_ready[half], 16)
            for name, st in STAGES.items():

                def load(i, last, st=st, src=w[name]):
                    for c, tiles in enumerate(st.body):
                        n = st.slab0 + c + len(st.body) * i
                        slot, width = (st.slab0 + c) % 2, tiles * st.kc * P
                        if st.slab0 + c >= 2:
                            sp.wait_ge(wlo_ready, n - 1)
                        row = c + len(st.body) * i
                        part = src[row, :, 0:width] if isinstance(row, int) else \
                            src[ds(row, 1), :, 0:width].rearrange("a p n -> p (a n)")
                        sp.dma_start(raw[:, slot, 0:width], part).then_inc(raw_ready[slot], 16)

                with_loop = st.trips > 1
                if with_loop:
                    with sp.Fori(0, st.trips) as i:
                        load(i, False)
                else:
                    load(0, False)
            for c in range(DC):
                sp.wait_ge(y_ready, YB["res_ffn_h"] + c + 1)
                sp.dma_start(out[:, c, :], h[:, c, :]).then_inc(out_done, 16)
            sp.wait_ge(out_done, 16 * DC)

        @block.gpsimd
        def _(pool):
            for pr in range(N_PAIR):
                pool.wait_ge(scan_ready, pr + 1)
                if pr:
                    pool.wait_ge(yssm_done, pr)
                co, si = cos_t[:, pr, :], sin_t[:, pr, :]
                pool.tensor_tensor(prod[:, 0, :], scan[:, 0, :], co, ALU.mult)
                pool.tensor_tensor(prod[:, 1, :], scan[:, 1, :], si, ALU.mult)
                pool.tensor_tensor(prod[:, 2, :], scan[:, 0, :], si, ALU.mult)
                pool.tensor_tensor(prod[:, 3, :], scan[:, 1, :], co, ALU.mult).then_inc(prod_ready, 1)

        @block.tensor
        def _(pe):
            def slab(st, c, i, xs=None):
                slot, per = (st.slab0 + c) % 2, st.cum[-1]
                pe.wait_ge(wlo_ready, st.slab0 + c + 1 + len(st.body) * i)
                hi, lo = xs or (x_hi, x_lo)
                for m in range(st.body[c]):
                    t0 = st.tile0 + st.cum[c] + m
                    if st.free0 + st.cum[c] + m >= 2:
                        pe.wait_ge(tile_free[st.reader], st.free0 + st.cum[c] + m - 1 + per * i)
                    o = ps[:, t0 % 2, :]
                    for k in range(st.kc):
                        a = (m * st.kc + k) * P
                        pe.matmul(o, w_lo[:, slot, a:a + P], hi[:, k, :], start=k == 0, stop=False)
                        pe.matmul(o, w_hi[:, slot, a:a + P], lo[:, k, :], start=False, stop=False)
                        last = pe.matmul(o, w_hi[:, slot, a:a + P], hi[:, k, :], start=False, stop=k == st.kc - 1)
                    last.then_inc(tile_done, 1)

            def read_out(before, st):
                if before.reader != st.reader:
                    pe.wait_ge(tile_free[before.reader], before.free0 + before.tiles)

            def dense(name, operand=None, xs=None):
                st = STAGES[name]
                if operand:
                    pe.wait_ge(xlo_ready, XB[operand] + st.kc)
                read_out(st.before, st)
                run(pe, st, lambda i, last: [slab(st, c, i, xs) for c in range(len(st.body))])

            def feature_sum(name, n):
                if SK[name]:
                    pe.wait_ge(root_ready, SK[name])
                for c in range(n):
                    j = SB[name] + c
                    pe.wait_ge(sq_ready, j + 1)
                    pe.matmul(ps[:, SUM, :], ones, sq[:, j % 2, :], start=c == 0, stop=c == n - 1) \
                      .then_inc(sq_used, 1)

            def mean_sum(name, event):
                pe.wait_ge(root_ready, SK[name])
                for c in range(DC):
                    pe.wait_ge(y_ready, YB[event] + c + 1)
                    last = pe.matmul(ps[:, SUM, :], ones, y[:, c, :], start=c == 0, stop=c == DC - 1)
                last.then_inc(mean_ready, 1)

            pe.wait_ge(small_ready, 16 * SMALL)
            pe.wait_ge(xlo_ready, XB["w_in"] + DC)
            st = STAGES["w_in"]
            slab(st, 0, 0)
            feature_sum("pre_mix", DC)
            pe.wait_ge(bb_ready, 1)
            for n, bb in enumerate((bb_re, bb_im)):
                for i in range(4):
                    last = pe.transpose(ps[:, 2 + n, i * P:(i + 1) * P],
                                        bb[:, 4 * i:4 * i + 4, :].rearrange("p a c -> p (a c)"), ident)
            last.then_inc(bt_done, 1)
            for c in range(1, 5):
                slab(st, c, 0)

            def ssm_in(pr):
                i, q = divmod(pr, 4)
                if pr >= 2:
                    pe.wait_ge(bu_free, pr - 1)
                for n in range(2):
                    last = pe.matmul(ps[:, 2 + 2 * (pr % 2) + n, :], b_lhs[GW * q:GW * q + GW, n, i, :],
                                     u[GW * q:GW * q + GW, i, :], start=True, stop=True)
                last.then_inc(bu_done, 1)

            def ssm_out(pr):
                i, q = divmod(pr, 4)
                pe.wait_ge(prod_ready, pr + 1)
                if q == 0 and i:
                    pe.wait_ge(pre_gelu, i)
                for n, cc in enumerate((c_re, c_neg, c_im, c_im)):
                    last = pe.matmul(ps[GW * q:GW * q + GW, 6, :], cc[:, pr, :], prod[:, n, :],
                                     start=n == 0, stop=n == 3)
                last.then_inc(yssm_done, 1)

            pe.wait_ge(blhs_ready, 1)
            pe.wait_ge(tile_free["dve"], STAGES["w_in"].tiles)
            ssm_in(0)
            for pr in range(N_PAIR):
                if pr + 1 < N_PAIR:
                    ssm_in(pr + 1)
                ssm_out(pr)

            pe.wait_ge(mask_ready, 1)
            pe.wait_ge(pre_gelu, 4)
            for b in range(TB):
                last = pe.transpose(ps[:, 2, b * P:(b + 1) * P], v1[:, b * P:(b + 1) * P], ident)
            last.then_inc(vt1_done, 1)
            pe.matmul(ps[:, 3, :], swap1, k1[:, :], start=True, stop=True).then_inc(kr1_swap, 1)
            pe.wait_ge(vt1_ready, 1)
            pe.wait_ge(kr1_ready, 1)
            steps = [(hh, b, n) for hh in range(2) for b, n in BLOCKS1]
            with pe.Fori(0, 4) as i:
                pe.matmul(ps[:, 2, :], swap1, chunk(q1, i), start=True, stop=True).then_inc(qr1_swap, 1)
                pe.wait_ge(qr1_ready, i + 1)

                def scores1(s):
                    hh, b, n = steps[s]
                    if s >= 2:
                        pe.wait_ge(p1_ready, 8 * i + s - 1)
                    o = ps[:, 3 + s % 2, 0:n * P]
                    pe.matmul(o, qr1[64 * hh:64 * hh + 64, b * P:(b + 1) * P],
                              k1[64 * hh:64 * hh + 64, (b + 1 - n) * P:(b + 1) * P], start=True, stop=False)
                    pe.matmul(o, ident_b[:, :], m1[:, 2 * P - n * P:2 * P], start=False, stop=True).then_inc(s1_done, 1)

                def values1(s):
                    hh, b, n = steps[s]
                    pe.wait_ge(p1_ready, 8 * i + s + 1)
                    for j in range(n):
                        last = pe.transpose(ps[:, 5, j * P:(j + 1) * P], p1[:, s % 2, j * P:(j + 1) * P], ident)
                    last.then_inc(p1t_done, 1)
                    pe.wait_ge(p1t_ready, 8 * i + s + 1)
                    if s:
                        pe.wait_ge(o1_ready, 8 * i + s)
                    for j in range(n):
                        last = pe.matmul(ps[:, 6, 0:64], p1_t[:, s % 2, j * P:(j + 1) * P],
                                         v1_tok[:, b + 1 - n + j, 64 * hh:64 * hh + 64], start=j == 0, stop=j == n - 1)
                    last.then_inc(o1_done, 1)

                scores1(0)
                for s in range(8):
                    if s < 7:
                        scores1(s + 1)
                    values1(s)
            pe.wait_ge(o1_ready, 32)
            for c in range(4):
                if c >= 2:
                    pe.wait_ge(y_ready, YB["attn1"] + c - 1)
                for b in range(TB):
                    last = pe.transpose(ps[:, 4 + c % 2, b * P:(b + 1) * P], o1_tok[:, b, c * P:(c + 1) * P], ident)
                last.then_inc(o1t_done, 1)

            dense("w_glu", "w_glu")
            feature_sum("ssm", 4)
            feature_sum("attn", 4)
            dense("w_out", "w_out")
            feature_sum("post_mix", DC)
            feature_sum("pre_ffn", DC)
            for n in range(2):
                dense(f"gate_up{n}", "gate_up" if n == 0 else None)
                pe.wait_ge(hid_ready, HB[str(n)] + FFN1_PARTS[n])
                dense(f"down{n}", None, (hid_hi, hid_lo))
            feature_sum("post_ffn", DC)

            st = STAGES["attn_in"]

            def attention(p, sub, i, project, attend):
                old, pa = 1 - sub, p - 1
                tile = st.free0 + PAIR_TILES * p
                for j in range(10):
                    s = j - 1
                    if attend and 1 <= j <= 8:
                        hh, b, n1, n2 = STEPS2[s]
                        nb = n1 + 2 * n2
                        pe.wait_ge(p2_ready, 8 * pa + s + 1)
                        for r in range(ROUNDS[s]):
                            if r == 2:
                                pe.wait_ge(p2t_dve, DVE_TURNS[-1] * pa + DVE_TURNS[s] + 1)
                            for a in range(4 * r, min(4 * r + 4, nb)):
                                last = pe.transpose(ps[:, 5 + r % 2, (a - 4 * r) * P:(a - 4 * r + 1) * P],
                                                    p2[:, s % 2, a * P:(a + 1) * P], ident)
                            last.then_inc(p2t_done, 1)
                    if attend and j <= 7:
                        hh, b, n1, n2 = STEPS2[j]
                        if j == 0:
                            pe.wait_ge(rot_ready, 6 * pa + 6)
                            pe.wait_ge(vtok_ready, 3 * pa + 3)
                        lo_, hi_ = 64 * hh, 64 * hh + 64
                        for g, (n, mask) in enumerate(((n1, m2), (n2, mp2), (n2, mp3))):
                            o = ps[:, 2 + g, 0:n * P]
                            k0 = b + 1 - n
                            pe.matmul(o, qkv[lo_:hi_, old, 3 * g, b * P:(b + 1) * P],
                                      qkv[lo_:hi_, old, 3 * g + 1, k0 * P:(b + 1) * P], start=True, stop=False)
                            full = 2 * P if g == 0 else 4 * P
                            last = pe.matmul(o, ident_b[:, :], mask[:, full - n * P:full], start=False, stop=True)
                        last.then_inc(s2_done, 1)
                    if attend and 1 <= j <= 8:
                        hh, b, n1, n2 = STEPS2[s]
                        pe.wait_ge(p2t_dve, DVE_TURNS[-1] * pa + DVE_TURNS[s + 1])
                        if ACT_TURNS[s + 1] > ACT_TURNS[s]:
                            pe.wait_ge(p2t_act, ACT_TURNS[-1] * pa + ACT_TURNS[s + 1])
                        if j >= 2 and project:
                            if (j - 2) % 3 == 2:
                                pe.wait_ge(vtok_ready, 3 * p + (j - 2) // 3 + 1)
                            else:
                                pe.wait_ge(rot_ready, 6 * p + 2 * ((j - 2) // 3) + (j - 2) % 3 + 1)
                        elif j >= 2:
                            pe.wait_ge(o2_ready, 8 * pa + s)
                        a = 0
                        nb = n1 + 2 * n2
                        for g, n in enumerate((n1, n2, n2)):
                            for kb in range(b + 1 - n, b + 1):
                                last = pe.matmul(ps[:, 7, 0:64], p2_t[:, a * P:(a + 1) * P],
                                                 v_tok[:, old, g, kb, 64 * hh:64 * hh + 64],
                                                 start=a == 0, stop=a == nb - 1)
                                a += 1
                        last.then_inc(o2_done, 1)
                    if project and j <= 8:
                        project_tile(p, sub, i, j)
                    if project and j >= 1:
                        t = j - 1
                        pe.wait_ge(tile_free["act"], tile + t + 1)
                        if attend and j <= 8:
                            pe.wait_ge(o2_ready, 8 * pa + s + 1)
                        elif t >= 1:
                            if (t - 1) % 3 == 2:
                                pe.wait_ge(vtok_ready, 3 * p + (t - 1) // 3 + 1)
                            else:
                                pe.wait_ge(rot_ready, 6 * p + 2 * ((t - 1) // 3) + (t - 1) % 3 + 1)
                        if t % 3 == 2:
                            for b in range(TB):
                                last = pe.transpose(ps[:, 7, b * P:(b + 1) * P], qkv[:, sub, t, b * P:(b + 1) * P], ident)
                        else:
                            last = pe.matmul(ps[:, 7, :], swap2, qkv[:, sub, t, :], start=True, stop=True)
                        last.then_inc(swap_done, 1)

            def project_tile(p, sub, i, j):
                c = 5 * sub + j // 2
                slot, m = (st.slab0 + c) % 2, j % 2
                if m == 0:
                    pe.wait_ge(wlo_ready, st.slab0 + 5 * p + j // 2 + 1)
                t0 = st.tile0 + 9 * sub + j
                if not (isinstance(p, int) and p == 0 and j < 2):
                    pe.wait_ge(tile_free["act"], st.free0 + 9 * p + j - 1)
                o = ps[:, t0 % 2, :]
                for k in range(DC):
                    a = (m * DC + k) * P
                    pe.matmul(o, w_lo[:, slot, a:a + P], x_hi[:, k, :], start=k == 0, stop=False)
                    pe.matmul(o, w_hi[:, slot, a:a + P], x_lo[:, k, :], start=False, stop=False)
                    last = pe.matmul(o, w_hi[:, slot, a:a + P], x_hi[:, k, :], start=False, stop=k == DC - 1)
                last.then_inc(tile_done, 1)

            pe.wait_ge(xlo_ready, XB["attn_in"] + DC)
            read_out(st.before, st)
            attention(0, 0, 0, True, False)
            with pe.Fori(0, HEAD_PAIRS // 2 - 1) as i:
                attention(2 * i + 1, 1, i, True, True)
                attention(2 * i + 2, 0, i, True, True)
            attention(HEAD_PAIRS - 1, 1, 0, True, True)
            attention(HEAD_PAIRS, 0, 0, False, True)
            pe.wait_ge(o2_ready, 8 * HEAD_PAIRS)
            for c in range(DC):
                if c >= 2:
                    pe.wait_ge(xlo_ready, XB["attn_out"] + c - 1)
                for b in range(TB):
                    last = pe.transpose(ps[:, 5 + c % 2, b * P:(b + 1) * P], o2_tok[:, b, c * P:(c + 1) * P], ident)
                last.then_inc(o2t_done, 1)

            def norm_and_ffn(layer, proj, up, down, part):
                dense(proj, proj)
                mean_sum(f"mean_mix_{layer}", f"out_mix_{layer}")
                feature_sum(f"var_mix_{layer}", DC)
                for n in range(2):
                    dense(f"{up}{n}", up if n == 0 else None)
                    pe.wait_ge(hid_ready, HB[f"{layer}{n}"] + part)
                    dense(f"{down}{n}", None, (hid_hi, hid_lo))
                mean_sum(f"mean_ffn_{layer}", f"out_ffn_{layer}")
                feature_sum(f"var_ffn_{layer}", DC)

            norm_and_ffn("a", "attn_out", "up_a", "down_a", FFN2_PART)

            dense("hgrn_in", "hgrn_in")
            pe.wait_ge(hm_ready, 48)

            def head(hd, first):
                pe.wait_ge(dec_ready, hd + 1)
                for b in range(TB):
                    sl = slice(b * P, (b + 1) * P)
                    last = pe.matmul(ps[:, 2, sl], k_dec[:, sl], q_dec[:, sl], start=True, stop=True)
                last.then_inc(a_done, 1)
                pe.wait_ge(vh_ready, hd + 1)
                for n, src in enumerate((k_dec, v_head)):
                    for b in range(TB):
                        sl = slice(b * P, (b + 1) * P)
                        last = pe.transpose(ps[:, 3 + n, sl], src[:, sl], ident)
                last.then_inc(ht_done, 1)
                pe.wait_ge(ht_ready, hd + 1)
                for c in range(7):
                    half = slice(CHUNK * (c % 2), CHUNK * (c % 2) + CHUNK)
                    last = pe.matmul(ps[:, 5 + c % 2, (c // 2) * P:(c // 2 + 1) * P], k_tok[half, c // 2, :],
                                     v_htok[half, c // 2, :], start=True, stop=True)
                last.then_inc(kv_done, 1)
                pe.wait_ge(a_ready, hd + 1)
                if not first:
                    pe.wait_ge(oh_ready, hd)
                for b in range(TB):
                    sl = slice(b * P, (b + 1) * P)
                    pe.matmul(ps[:, 0, sl], v_htok[:, b, :], tmp[:, 3, sl], start=b == 0, stop=False,
                              skip_group_check=True)
                pe.wait_ge(st_ready, hd + 1)
                for c in range(1, 8):
                    sl = slice(c * CHUNK, (c + 1) * CHUNK)
                    last = pe.matmul(ps[:, 0, sl], state[:, c, :], q_dec[:, sl], start=False, stop=c == 7,
                                     skip_group_check=True)
                last.then_inc(oh_done, 1)
                pe.wait_ge(sq_ready, SB["head0"] + hd + 1)
                pe.wait_ge(root_ready, SK["head0"] + hd)
                pe.matmul(ps[:, SUM, :], ones, sq[:, 0, :], start=True, stop=True).then_inc(sq_used, 1)

            pe.wait_ge(tile_free["act"], STAGES["hgrn_in"].free0 + STAGES["hgrn_in"].tiles)
            head(0, True)
            with pe.Fori(1, HG_HEADS) as hd:
                head(hd, False)
            norm_and_ffn("h", "hgrn_out", "up_h", "down_h", FFN2_PART)

        @block.scalar
        def _(act):
            small = [(gains, gains_in), (consts, const_in), (lam, lam_in), (sink, sink_in), (freq, freq_in),
                     (pos, pos_in), (iota, iota_in), (b_re, b_in[:, 0]), (b_im, b_in[:, 1]),
                     (c_re, c_in[:, 0]), (c_im, c_in[:, 1]), (mask_raw, mask_in)]
            assert len(small) == SMALL
            for dst, src in small:
                dst = dst[:, :, :] if len(dst.shape) == 3 else dst[:, :]
                act.dma_start(dst, src).then_inc(small_ready, 16)

            def split_hi(st, c, i, unready=False):
                n0 = st.slab0 + c + 1
                slot, trip = n0 % 2, len(st.body)
                act.wait_ge(raw_ready[slot], 16 * (n0 // 2 + 1 + (trip // 2) * i))
                if n0 >= 2:
                    act.wait_ge(tile_done, st.tile0 + st.cum[c] + st.cum[-1] * i)
                act.activation(w_hi[:, slot, :], raw[:, slot, :], ACT.Copy).then_inc(whi_ready, 1)

            def part_hi(event, c, src, scale=1.0):
                act.activation(chunk(x_hi, c), src, ACT.Copy, scale=scale).then_inc(xhi_ready, 1)

            def square(name, c, src):
                j = SB[name] + c
                if j >= 2:
                    act.wait_ge(sq_used, j - 1)
                act.activation(sq[:, j % 2, :], src, ACT.Square).then_inc(sq_ready, 1)

            def take_root(name, n, width, e=0):
                act.wait_ge(sq_used, SB[name] + n)
                act.wait_ge(eps_ready, 1)
                if SK[name]:
                    act.wait_ge(rstd_ready, SK_ROOT[name])
                act.activation(root[:, :], ps[:, SUM, :], ACT.Sqrt, bias=eps[:, e:e + 1], scale=1.0 / width) \
                   .then_inc(root_ready, 1)

            act.wait_ge(small_ready, 16 * SMALL)
            for c in range(DC):
                if c % 4 == 0:
                    act.wait_ge(x_ready[c // 4], 16)
                part_hi("w_in", c, x_raw[:, c, :], gain("g_pre_mix", c))
            act.wait_ge(raw_ready[0], 16)
            act.activation(w_hi[:, 0, :], raw[:, 0, :], ACT.Copy).then_inc(whi_ready, 1)
            w_in = STAGES["w_in"]
            split_hi(w_in, 0, 0)
            for c in range(DC):
                square("pre_mix", c, x_raw[:, c, :])
            take_root("pre_mix", DC, D)
            act.activation(masks[:, :], mask_raw[:, :], ACT.Copy)
            act.activation(ident_b[:, :], ident, ACT.Copy).then_inc(mask_ready, 1)

            act.wait_ge(turn_ready, 1)
            act.activation(par[:, PR["sin"], :], par[:, PR["r"], :], ACT.Sin)
            act.activation(par[:, PR["sin_half"], :], par[:, PR["r"], :], ACT.Sin, scale=0.5).then_inc(sines_ready, 1)

            def sin_cos(co, si, angle):
                act.activation(co, angle, ACT.Abs)
                act.activation(si, angle, ACT.Sin)
                act.drain()
                return act.activation(co, co, ACT.Sin, scale=-1.0, bias=eps[:, 2:3])

            act.wait_ge(rope_ang, 1)
            sin_cos(rope_c[:, :], rope_s[:, :], tmp[:, 1, :]).then_inc(rope_ready, 1)
            act.wait_ge(bt_done, 1)
            act.activation(b_lhs[:, 0, :, :].rearrange("p a c -> p (a c)"), ps[:, 2, :], ACT.Copy)
            act.activation(b_lhs[:, 1, :, :].rearrange("p a c -> p (a c)"), ps[:, 3, :], ACT.Copy).then_inc(blhs_ready, 1)

            for c in range(1, 5):
                split_hi(w_in, c, 0)
                for pr in range(max(0, 4 * c - 4), 4 * c):
                    act.wait_ge(ang_ready, pr + 1)
                    sin_cos(cos_t[:, pr, :], sin_t[:, pr, :], tmp[:, 1 + pr % 2, :]).then_inc(ang_used, 1)

            for i in range(4):
                act.wait_ge(pre_gelu, i + 1)
                if i >= 2:
                    act.wait_ge(xlo_ready, XB["w_glu"] + i - 1)
                act.activation(tmp[:, 2 + i % 2, :], tmp[:, i % 2, :], ACT.Gelu_apprx_tanh)
                act.drain()
                part_hi("w_glu", i, tmp[:, 2 + i % 2, :])

            act.wait_ge(vt1_done, 1)
            act.activation(v1_tok[:, :, :].rearrange("p a c -> p (a c)"), ps[:, 2, :], ACT.Copy).then_inc(vt1_ready, 1)
            with act.Fori(0, 4) as i:
                for s in range(8):
                    hh, (b, n) = s // 4, BLOCKS1[s % 4]
                    act.wait_ge(max1_ready, 8 * i + s + 1)
                    if s >= 2:
                        act.wait_ge(p1t_ready, 8 * i + s - 1)
                    st_ = stat[:, s % 2, :]
                    head = 2 * i + hh
                    act.activation(p1[:, s % 2, 0:n * P], ps[:, 3 + s % 2, 0:n * P], ACT.Exp, bias=st_[:, 2:3],
                                   scale=0.125, accum_out=st_[:, 4:5])
                    act.activation(st_[:, 3:4], sink[:, ds(head, 1)], ACT.Exp, bias=st_[:, 2:3]).then_inc(p1_ready, 1)

            st = STAGES["w_glu"]
            for c in range(2):
                split_hi(st, c, 0)
                for m in range(2):
                    j = 2 * c + m
                    act.wait_ge(tile_done, st.tile0 + 2 * j + 2)
                    if j >= 2:
                        act.wait_ge(y_ready, YB["glu"] + j - 1)
                    act.activation(tmp[:, j % 2, :], ps[:, (st.tile0 + 2 * j + 1) % 2, :], ACT.Sigmoid,
                                   bias=gain("b_glu", 4 + j)).then_inc(gate_ready, 1)

            act.wait_ge(y_ready, YB["glu"] + 4)
            act.dma_start(h[:, :, :], x_in).then_inc(h_back, 16)

            for c in range(4):
                square("ssm", c, y[:, c, :])
            take_root("ssm", 4, HALF)
            for c in range(4):
                square("attn", c, y[:, 4 + c, :])
            take_root("attn", 4, HALF)
            for c in range(DC):
                act.wait_ge(merge_ready, c + 1)
                part_hi("w_out", c, y[:, c, :])

            def rest(name, body=None):
                st = STAGES[name]

                def trip(i, last):
                    for c in range(len(st.body)):
                        if not (last and c == len(st.body) - 1):
                            split_hi(st, c, i)
                        if body:
                            body(st, c, i)

                run(act, st, trip)

            rest("w_out")
            for c in range(DC):
                if c == 0:
                    act.wait_ge(y_ready, YB["w_out"] + DC)
                square("post_mix", c, y[:, c, :])
            take_root("post_mix", DC, D)
            for c in range(DC):
                act.wait_ge(y_ready, YB["res_mix"] + c + 1)
                part_hi("gate_up", c, h[:, c, :], gain("g_pre_ffn", c))
                square("pre_ffn", c, h[:, c, :])
            take_root("pre_ffn", DC, D)

            for n in range(2):

                def gated(st, c, i, n=n):
                    k = c + 2 * i
                    act.wait_ge(gate_scaled, HB[str(n)] + k + 1)
                    act.activation(tmp[:, 2, :], tmp[:, 0, :], ACT.Silu).then_inc(silu_ready, 1)
                    act.wait_ge(hid_pre, HB[str(n)] + k + 1)
                    if n == 0:
                        act.wait_ge(prod_ready, N_PAIR)
                    else:
                        act.wait_ge(tile_done, st.tile0)
                    act.activation(chunk(hid_hi, k), tmp[:, 3, :], ACT.Copy).then_inc(hid_half, 1)

                rest(f"gate_up{n}", gated)
                rest(f"down{n}")
            for c in range(DC):
                if c == 0:
                    act.wait_ge(y_ready, YB["ffn"] + DC)
                square("post_ffn", c, y[:, c, :])
            take_root("post_ffn", DC, D)
            for c in range(DC):
                act.wait_ge(y_ready, YB["res_ffn"] + c + 1)
                part_hi("attn_in", c, h[:, c, :])

            act.dma_start(rope_c[:, :], rope2_in[:, 0]).then_inc(rope2_ready, 16)
            act.dma_start(rope_s[:, :], rope2_in[:, 1]).then_inc(rope2_ready, 16)
            st = STAGES["attn_in"]

            def attention(p, sub, i, project, attend):
                pa = p - 1
                for j in range(10):
                    if attend and 1 <= j <= 8:
                        s = j - 1
                        for r in range(1, ROUNDS[s], 2):
                            act.wait_ge(p2t_done, TURNS[-1] * pa + TURNS[s] + r + 1)
                            nb = STEPS2[s][2] + 2 * STEPS2[s][3]
                            cols = (min(4 * r + 4, nb) - 4 * r) * P
                            act.activation(p2_t[:, 4 * r * P:4 * r * P + cols], ps[:, 5 + r % 2, 0:cols], ACT.Copy) \
                               .then_inc(p2t_act, 1)
                    if attend and j <= 7:
                        hh, b, n1, n2 = STEPS2[j]
                        act.wait_ge(max2_ready, 8 * pa + j + 1)
                        st_ = stat[:, j % 2, :]
                        act.activation(p2[:, j % 2, 0:n1 * P], ps[:, 2, 0:n1 * P], ACT.Exp, bias=st_[:, 2:3],
                                       scale=0.125, accum_out=st_[:, 4:5])
                        act.activation(p2[:, j % 2, n1 * P:(n1 + 2 * n2) * P].rearrange("p (a c) -> p a c", a=2),
                                       ps[:, 3:5, 0:n2 * P], ACT.Exp, bias=st_[:, 2:3],
                                       scale=0.125, accum_out=st_[:, 5:6]).then_inc(p2_ready, 1)
                    if project and j <= 8:
                        if j % 2 == 0:
                            c = 5 * sub + j // 2
                            n0 = st.slab0 + c + 1
                            act.wait_ge(raw_ready[n0 % 2], 16 * (n0 // 2 + 1 + 5 * i))
                            act.wait_ge(tile_done, st.tile0 + 9 * p + j)
                            act.activation(w_hi[:, n0 % 2, :], raw[:, n0 % 2, :], ACT.Copy).then_inc(whi_ready, 1)
                        act.wait_ge(tile_done, st.tile0 + 9 * p + j + 1)
                        act.activation(qkv[:, sub, j, :], ps[:, (st.tile0 + 9 * sub + j) % 2, :], ACT.Copy) \
                           .then_inc(tile_free["act"], 1)
                    if project and j >= 1 and (j - 1) % 3 == 2:
                        act.wait_ge(swap_done, 9 * p + j)
                        act.activation(v_tok[:, sub, (j - 1) // 3, :, :].rearrange("p a c -> p (a c)"), ps[:, 7, :],
                                       ACT.Copy).then_inc(vtok_ready, 1)

            attention(0, 0, 0, True, False)
            with act.Fori(0, HEAD_PAIRS // 2 - 1) as i:
                attention(2 * i + 1, 1, i, True, True)
                attention(2 * i + 2, 0, i + 1, True, True)
            attention(HEAD_PAIRS - 1, 1, HEAD_PAIRS // 2 - 1, True, True)
            attention(HEAD_PAIRS, 0, 0, False, True)
            for c in range(DC):
                act.wait_ge(o2t_done, c + 1)
                part_hi("attn_out", c, ps[:, 5 + c % 2, :])

            def hidden(key):

                def body(st, c, i):
                    for m in range(2):
                        t = 2 * c + m
                        k = t + 4 * i
                        act.wait_ge(tile_done, st.tile0 + t + 4 * i + 1)
                        act.wait_ge(hid_ready, HB[key] + k - 1)
                        act.activation(tmp[:, t % 2, :], ps[:, (st.tile0 + t) % 2, :], ACT.Relu).then_inc(tile_free["act"], 1)
                        act.drain()
                        act.activation(chunk(hid_hi, k), tmp[:, t % 2, :], ACT.Square).then_inc(hid_half, 1)

                return body

            def layer_norm(layer, part):
                act.wait_ge(mean_ready, MEANS[layer + part] + 1)
                act.activation(root[:, :], ps[:, SUM, :], ACT.Copy, scale=1.0 / D).then_inc(root_ready, 1)
                for c in range(DC):
                    act.wait_ge(y_ready, YB[f"mid_{part}_{layer}"] + c + 1)
                    square(f"var_{part}_{layer}", c, y[:, c, :])
                take_root(f"var_{part}_{layer}", DC, D, 1)

            def norm_and_ffn(layer, proj, up, down, after):
                rest(proj)
                layer_norm(layer, "mix")
                for c in range(DC):
                    act.wait_ge(y_ready, YB[f"res_mix_{layer}"] + c + 1)
                    part_hi(up, c, h[:, c, :])
                for n in range(2):
                    rest(f"{up}{n}", hidden(f"{layer}{n}"))
                    rest(f"{down}{n}")
                layer_norm(layer, "ffn")
                if after:
                    for c in range(DC):
                        act.wait_ge(y_ready, YB[f"res_ffn_{layer}"] + c + 1)
                        part_hi(after, c, h[:, c, :])

            norm_and_ffn("a", "attn_out", "up_a", "down_a", "hgrn_in")

            for n, dst in enumerate((a_mask, run_mask, start_mask)):
                act.dma_start(dst[:, :], hmask_in[:, n]).then_inc(hm_ready, 16)
            act.wait_ge(lb_half, 1)
            act.activation(lbp[:, 2:4, :].rearrange("p a c -> p (a c)"), lbp[:, 2:4, :].rearrange("p a c -> p (a c)"),
                           ACT.Exp).then_inc(lb_exp, 1)

            def gates(st, c, i):
                for m in range(2):
                    t = 2 * c + m
                    hd = t // 3 + 4 * i
                    act.wait_ge(tile_done, st.tile0 + t + 12 * i + 1)
                    act.wait_ge(tile_done, st.tile0)
                    src = ps[:, (st.tile0 + t) % 2, :]
                    if t % 3 == 0:
                        last = act.activation(chunk(hg_q, hd), src, ACT.Silu)
                    elif t % 3 == 1:
                        act.activation(chunk(hg_s, hd), src, ACT.Sigmoid)
                        last = act.activation(chunk(hg_k, hd), src, ACT.Sigmoid, scale=-1.0)
                    else:
                        last = act.activation(chunk(hg_v, hd), src, ACT.Copy)
                    last.then_inc(tile_free["act"], 1)

            rest("hgrn_in", gates)

            def head(hd, first):
                if not first:
                    act.wait_ge(kv_done, hd)
                    act.wait_ge(tile_done, STAGES["hgrn_out"].tile0)
                act.activation(v_head[:, :], chunk(hg_v, hd), ACT.Copy).then_inc(vh_ready, 1)
                act.wait_ge(ht_done, hd + 1)
                if not first:
                    act.wait_ge(oh_done, hd)
                act.activation(k_tok[:, :, :].rearrange("p a c -> p (a c)"), ps[:, 3, :], ACT.Copy)
                act.activation(v_htok[:, :, :].rearrange("p a c -> p (a c)"), ps[:, 4, :], ACT.Copy).then_inc(ht_ready, 1)
                act.wait_ge(oh_done, hd + 1)
                act.wait_ge(sq_used, SB["head0"] + hd)
                act.activation(sq[:, 0, :], ps[:, 0, :], ACT.Square).then_inc(sq_ready, 1)
                act.wait_ge(sq_used, SB["head0"] + hd + 1)
                act.wait_ge(rstd_ready, SK_ROOT["head0"] + hd)
                act.activation(root[:, :], ps[:, SUM, :], ACT.Sqrt, bias=eps[:, 0:1], scale=1.0 / P).then_inc(root_ready, 1)
                act.wait_ge(oh_ready, hd + 1)
                act.wait_ge(tile_done, STAGES["hgrn_out"].tile0)
                part_hi("hgrn_out", hd, tmp[:, 0, :])

            act.wait_ge(tile_done, STAGES["hgrn_out"].tile0)
            head(0, True)
            with act.Fori(1, HG_HEADS) as hd:
                head(hd, False)
            norm_and_ffn("h", "hgrn_out", "up_h", "down_h", None)

        @block.vector
        def _(dve):
            tt, ts, stt, settle = dve.tensor_tensor, dve.tensor_scalar, dve.scalar_tensor_tensor, dve.drain

            def split_lo(st, c, i):
                n0 = st.slab0 + c + 1
                slot = n0 % 2
                dve.wait_ge(whi_ready, n0 + 1 + len(st.body) * i)
                tt(w_lo[:, slot, :], raw[:, slot, :], w_hi[:, slot, :].bitcast(f32), ALU.subtract).then_inc(wlo_ready, 1)

            def part_lo(event, c, src):
                dve.wait_ge(xhi_ready, XB[event] + c + 1)
                tt(chunk(x_lo, c), src, chunk(x_hi, c).bitcast(f32), ALU.subtract).then_inc(xlo_ready, 1)

            def part_lo_gain(event, c, src, scale):
                dve.wait_ge(xhi_ready, XB[event] + c + 1)
                stt(x_lo[:, c, :], src, scale, x_hi[:, c, :].bitcast(f32), ALU.mult, ALU.subtract).then_inc(xlo_ready, 1)

            def invert(name):
                dve.wait_ge(root_ready, SK[name] + 1)
                dve.reciprocal(rstd[:, :], root[:, :]).then_inc(rstd_ready, 1)
                settle()

            for n, value in enumerate((RMS_EPS, LN_EPS, np.pi / 2)):
                last = dve.memset(eps[:, n:n + 1], float(value))
            last.then_inc(eps_ready, 1)
            dve.wait_ge(small_ready, 16 * SMALL)
            for c in range(DC):
                part_lo_gain("w_in", c, x_raw[:, c, :], gain("g_pre_mix", c))
            dve.wait_ge(whi_ready, 1)
            tt(w_lo[:, 0, :], raw[:, 0, :], w_hi[:, 0, :].bitcast(f32), ALU.subtract).then_inc(wlo_ready, 1)
            split_lo(STAGES["w_in"], 0, 0)

            def col(name):
                return par[:, PR[name], :]

            def exp_parts(z):
                ts(col("z"), z, -87.0, 88.0, ALU.max, ALU.min)
                settle()
                ts(col("k"), col("z"), float(1 / np.log(2.0)), ROUND, ALU.mult, ALU.add)
                settle()
                ts(col("k"), col("k"), ROUND, None, ALU.subtract)
                settle()
                stt(col("f"), col("k"), -LN2_HI, col("z"), ALU.mult, ALU.add)
                settle()
                stt(col("f"), col("k"), -LN2_LO, col("f"), ALU.mult, ALU.add)
                ts(col("two_k").bitcast(i32), col("k"), 127.0, 2.0 ** 23, ALU.add, ALU.mult)
                settle()
                ts(col("e"), col("f"), 1 / 5040.0, None, ALU.mult)
                for factor in (720.0, 120.0, 24.0, 6.0, 2.0, 1.0):
                    settle()
                    stt(col("e"), col("e"), 1 / factor, col("f"), ALU.add, ALU.mult)
                settle()

            def reduce_turns(angle, k, by):
                stt(angle, k, -PI_HI, angle, ALU.mult, ALU.add)
                settle()
                stt(angle, k, -PI_LO, angle, ALU.mult, ALU.add)
                settle()

            li = lam[:, 1, :]
            ts(col("lr"), lam[:, 0, :], -1e-4, None, ALU.min)
            exp_parts(lam[:, 2, :])
            stt(col("dt"), col("e"), 1.0, col("two_k"), ALU.add, ALU.mult)
            settle()
            tt(col("t0"), col("lr"), col("dt"), ALU.mult)
            tt(col("th"), li, col("dt"), ALU.mult)
            settle()
            exp_parts(col("t0"))
            tt(col("t0"), col("two_k"), col("e"), ALU.mult)
            settle()
            stt(col("em1"), col("two_k"), -1.0, col("t0"), ALU.add, ALU.add)
            ts(col("k"), col("th"), float(1 / TWO_PI), ROUND, ALU.mult, ALU.add)
            settle()
            ts(col("mag"), col("em1"), 1.0, None, ALU.add)
            ts(col("k"), col("k"), ROUND, None, ALU.subtract)
            dve.tensor_copy(col("r"), col("th"))
            settle()
            reduce_turns(col("r"), col("k"), 0)
            ts(col("r"), col("r"), PI_IN, -PI_IN, ALU.min, ALU.max)
            settle()
            ts(col("r_turn"), col("r"), float(1 / TWO_PI), None, ALU.mult).then_inc(turn_ready, 1)
            ts(col("t1"), col("r"), 2048.0, ROUND, ALU.mult, ALU.add)
            settle()
            ts(col("r_hi"), col("t1"), ROUND, 1 / 2048.0, ALU.subtract, ALU.mult)
            settle()
            tt(col("r_lo"), col("r"), col("r_hi"), ALU.subtract)
            dve.wait_ge(sines_ready, 1)
            tt(col("c1"), col("sin_half"), col("sin_half"), ALU.mult)
            tt(col("ai"), col("mag"), col("sin"), ALU.mult)
            settle()
            stt(col("c1"), col("c1"), -2.0, col("mag"), ALU.mult, ALU.mult)
            settle()
            tt(col("am1"), col("c1"), col("em1"), ALU.add)
            tt(col("den"), col("lr"), col("lr"), ALU.mult)
            tt(col("t0"), li, li, ALU.mult)
            settle()
            tt(col("den"), col("den"), col("t0"), ALU.add)
            tt(col("nr"), col("am1"), col("lr"), ALU.mult)
            tt(col("t1"), col("ai"), li, ALU.mult)
            settle()
            dve.reciprocal(col("den"), col("den"))
            tt(col("nr"), col("nr"), col("t1"), ALU.add)
            tt(col("ni"), col("ai"), col("lr"), ALU.mult)
            tt(col("t0"), col("am1"), li, ALU.mult)
            settle()
            tt(col("ni"), col("ni"), col("t0"), ALU.subtract)
            settle()
            tt(col("fr"), col("nr"), col("den"), ALU.mult)
            tt(col("fi"), col("ni"), col("den"), ALU.mult)
            settle()
            fr = col("fr").unsqueeze(2).to_broadcast([P, N_PAIR, GW])
            fi = col("fi").unsqueeze(2).to_broadcast([P, N_PAIR, GW])
            scratch = tmp[:, 0, :].rearrange("p (a c) -> p a c", a=N_PAIR)
            for dst, first, second, op in ((bb_re, b_re, b_im, ALU.subtract), (bb_im, b_im, b_re, ALU.add)):
                tt(dst[:, :, :], fr, first[:, :, :], ALU.mult)
                tt(tmp[:, 2, :].rearrange("p (a c) -> p a c", a=N_PAIR), fi, second[:, :, :], ALU.mult)
                settle()
                last = tt(dst[:, :, :], dst[:, :, :], tmp[:, 2, :].rearrange("p (a c) -> p a c", a=N_PAIR), op)
                settle()
            last.then_inc(bb_ready, 1)

            dve.tensor_copy(tmp[:, 1, :], pos[:, :])
            settle()
            ts(tmp[:, 1, :], tmp[:, 1, :], freq[:, 0:1], None, ALU.mult)
            settle()
            ts(tmp[:, 0, :], tmp[:, 1, :], float(1 / TWO_PI), ROUND, ALU.mult, ALU.add)
            settle()
            ts(tmp[:, 0, :], tmp[:, 0, :], ROUND, None, ALU.subtract)
            settle()
            reduce_turns(tmp[:, 1, :], tmp[:, 0, :], 0)
            ts(tmp[:, 1, :], tmp[:, 1, :], PI_IN, -PI_IN, ALU.min, ALU.max).then_inc(rope_ang, 1)

            invert("pre_mix")
            st = STAGES["w_in"]
            places = [u[:, c, :] for c in range(4)] + [q1[:, c, :] for c in range(4)] + [k1[:, :], v1[:, :]]
            dve.wait_ge(mask_ready, 1)
            dve.wait_ge(sq_used, DC)
            for c in range(5):
                if c:
                    split_lo(st, c, 0)
                for m in range(2):
                    t = 2 * c + m
                    dve.wait_ge(tile_done, t + 1)
                    tt(places[t], ps[:, t % 2, :], rstd[:, :], ALU.mult).then_inc(tile_free["dve"], 1)
                for pr in range(max(0, 4 * c - 4), 4 * c):
                    ang, k = tmp[:, 1 + pr % 2, :], tmp[:, 0, :]
                    if pr == 0:
                        dve.wait_ge(rope_ready, 1)
                    if pr >= 2:
                        dve.wait_ge(ang_used, pr - 1)
                    ts(ang, iota[:, :], par[:, PR["r_hi"], pr:pr + 1], None, ALU.mult)
                    ts(k, iota[:, :], par[:, PR["r_turn"], pr:pr + 1], ROUND, ALU.mult, ALU.add)
                    settle()
                    ts(k, k, ROUND, None, ALU.subtract)
                    settle()
                    reduce_turns(ang, k, 0)
                    stt(ang, iota[:, :], par[:, PR["r_lo"], pr:pr + 1], ang, ALU.mult, ALU.add)
                    settle()
                    ts(ang, ang, PI_IN, -PI_IN, ALU.min, ALU.max).then_inc(ang_ready, 1)
            ts(c_neg[:, :, :], c_re[:, :, :], -1.0, None, ALU.mult)
            ts(c_im[:, :, :], c_im[:, :, :], -1.0, None, ALU.mult)
            settle()

            for pr in range(N_PAIR):
                i, q = divmod(pr, 4)
                if pr == 0:
                    dve.wait_ge(ang_used, N_PAIR)
                dve.wait_ge(bu_done, pr + 1)
                re, im = ps[:, 2 + 2 * (pr % 2), :], ps[:, 3 + 2 * (pr % 2), :]
                settle()
                tt(mod[:, 0, :], re, cos_t[:, pr, :], ALU.mult)
                tt(mod[:, 1, :], im, sin_t[:, pr, :], ALU.mult)
                tt(mod[:, 2, :], im, cos_t[:, pr, :], ALU.mult)
                tt(mod[:, 3, :], re, sin_t[:, pr, :], ALU.mult).then_inc(bu_free, 1)
                settle()
                tt(mod[:, 0, :], mod[:, 0, :], mod[:, 1, :], ALU.add)
                tt(mod[:, 2, :], mod[:, 2, :], mod[:, 3, :], ALU.subtract)
                settle()
                if pr:
                    dve.wait_ge(prod_ready, pr)
                mag = par[:, PR["mag"], pr:pr + 1].to_broadcast([P, T])
                dve.tensor_tensor_scan(scan[:, 0, :], mag, mod[:, 0, :], 0.0, ALU.mult, ALU.add)
                dve.tensor_tensor_scan(scan[:, 1, :], mag, mod[:, 2, :], 0.0, ALU.mult, ALU.add).then_inc(scan_ready, 1)
                if (q == 0 and i) or pr == N_PAIR - 1:
                    done = [i - 1] if q == 0 else [i]
                    for c in done:
                        dve.wait_ge(yssm_done, 4 * c + 4)
                        if c >= 2:
                            dve.wait_ge(xlo_ready, XB["w_glu"] + c - 1)
                        stt(tmp[:, c % 2, :], u[:, c, :], gain("d", c), ps[:, 6, :], ALU.mult, ALU.add).then_inc(pre_gelu, 1)
                        part_lo("w_glu", c, tmp[:, 2 + c % 2, :])

            dve.wait_ge(kr1_swap, 1)
            tt(tmp[:, 0, :], ps[:, 3, :], rope_s[:, :], ALU.mult)
            tt(k1[:, :], k1[:, :], rope_c[:, :], ALU.mult)
            settle()
            tt(k1[:, :], k1[:, :], tmp[:, 0, :], ALU.add).then_inc(kr1_ready, 1)
            with dve.Fori(0, 4) as i:
                dve.wait_ge(qr1_swap, i + 1)
                tt(tmp[:, 0, :], ps[:, 2, :], rope_s[:, :], ALU.mult)
                tt(qr1[:, :], chunk(q1, i), rope_c[:, :], ALU.mult)
                settle()
                tt(qr1[:, :], qr1[:, :], tmp[:, 0, :], ALU.add).then_inc(qr1_ready, 1)

                def maximum1(s):
                    hh, (b, n) = s // 4, BLOCKS1[s % 4]
                    st_ = stat[:, s % 2, :]
                    dve.wait_ge(s1_done, 8 * i + s + 1)
                    dve.tensor_reduce(st_[:, 0:1], ps[:, 3 + s % 2, 0:n * P], AX.X, ALU.max)
                    settle()
                    ts(st_[:, 1:2], st_[:, 0:1], 0.125, sink[:, ds(2 * i + hh, 1)], ALU.mult, ALU.max)
                    settle()
                    ts(st_[:, 2:3], st_[:, 1:2], -1.0, None, ALU.mult).then_inc(max1_ready, 1)

                maximum1(0)
                for s in range(8):
                    hh, (b, n) = s // 4, BLOCKS1[s % 4]
                    st_ = stat[:, s % 2, :]
                    if s < 7:
                        maximum1(s + 1)
                    dve.wait_ge(p1t_done, 8 * i + s + 1)
                    dve.tensor_copy(p1_t[:, s % 2, 0:n * P], ps[:, 5, 0:n * P]).then_inc(p1t_ready, 1)
                    tt(st_[:, 5:6], st_[:, 3:4], st_[:, 4:5], ALU.add)
                    settle()
                    dve.reciprocal(st_[:, 6:7], st_[:, 5:6])
                    settle()
                    dve.wait_ge(o1_done, 8 * i + s + 1)
                    ts(o1_tok[:, b, ds(2 * i * 64 + 64 * hh, 64)], ps[:, 6, 0:64], st_[:, 6:7], None, ALU.mult) \
                        .then_inc(o1_ready, 1)
            for c in range(4):
                dve.wait_ge(o1t_done, c + 1)
                dve.tensor_copy(y[:, 4 + c, :], ps[:, 4 + c % 2, :]).then_inc(y_ready, 1)

            st = STAGES["w_glu"]
            for c in range(2):
                split_lo(st, c, 0)
                for m in range(2):
                    j = 2 * c + m
                    dve.wait_ge(gate_ready, j + 1)
                    stt(y[:, j, :], ps[:, (st.tile0 + 2 * j) % 2, :], gain("b_glu", j), tmp[:, j % 2, :],
                        ALU.add, ALU.mult).then_inc(tile_free["dve"], 2)
                    settle()
                    dve.sem_inc(y_ready, 1)

            invert("ssm")
            for c in range(DC):
                if c == 4:
                    invert("attn")
                stt(y[:, c, :], y[:, c, :], gain("g_ssm", c) if c < 4 else gain("g_attn", c - 4), rstd[:, :],
                    ALU.mult, ALU.mult).then_inc(merge_ready, 1)
                settle()
                part_lo("w_out", c, y[:, c, :])

            def rest(name, body):
                st = STAGES[name]

                def trip(i, last):
                    for c in range(len(st.body)):
                        if not (last and c == len(st.body) - 1):
                            split_lo(st, c, i)
                        body(st, c, i)

                run(dve, st, trip)

            def tiles(put):

                def body(st, c, i):
                    for m in range(st.body[c]):
                        t = st.cum[c] + m
                        dve.wait_ge(tile_done, st.tile0 + t + st.cum[-1] * i + 1)
                        put(t + st.cum[-1] * i, ps[:, (st.tile0 + t) % 2, :])

                return body

            def keep(t, bank):
                ts(chunk(y, t), bank, 1.0, None, ALU.mult).then_inc(tile_free["dve"], 1)

            def keep_and_tell(t, bank):
                ts(chunk(y, t), bank, 1.0, None, ALU.mult).then_inc(tile_free["dve"], 1)
                settle()
                dve.sem_inc(y_ready, 1)

            def add_and_tell(t, bank):
                tt(chunk(y, t), bank, chunk(y, t), ALU.add).then_inc(tile_free["dve"], 1)
                settle()
                dve.sem_inc(y_ready, 1)

            def residual(t, bank):
                stt(chunk(y, t), chunk(h, t), ALPHA, bank, ALU.mult, ALU.add).then_inc(tile_free["dve"], 1)

            def residual_and_tell(t, bank):
                residual(t, bank)
                settle()
                dve.sem_inc(y_ready, 1)

            def post_norm(name, g, after, event):
                invert(name)
                for c in range(DC):
                    stt(y[:, c, :], y[:, c, :], gain(g, c), rstd[:, :], ALU.mult, ALU.mult)
                    settle()
                    tt(h[:, c, :], h[:, c, :], y[:, c, :], ALU.add).then_inc(y_ready, 1)
                    settle()
                    after(c)

            rest("w_out", tiles(keep_and_tell))
            dve.wait_ge(h_back, 16)
            post_norm("post_mix", "g_post_mix",
                      lambda c: part_lo_gain("gate_up", c, h[:, c, :], gain("g_pre_ffn", c)), "res_mix")

            invert("pre_ffn")
            for n in range(2):

                def gated(st, c, i, n=n):
                    k = c + 2 * i
                    for m in range(2):
                        t = 2 * c + m
                        dve.wait_ge(tile_done, st.tile0 + t + 4 * i + 1)
                        scaled = tt(tmp[:, m, :], ps[:, (st.tile0 + t) % 2, :], rstd[:, :], ALU.mult)
                        scaled.then_inc(tile_free["dve"], 1)
                        settle()
                        if m == 0:
                            dve.sem_inc(gate_scaled, 1)
                    dve.wait_ge(silu_ready, HB[str(n)] + k + 1)
                    tt(tmp[:, 3, :], tmp[:, 2, :], tmp[:, 1, :], ALU.mult).then_inc(hid_pre, 1)
                    settle()
                    dve.wait_ge(hid_half, HB[str(n)] + k + 1)
                    tt(chunk(hid_lo, k), tmp[:, 3, :], chunk(hid_hi, k).bitcast(f32), ALU.subtract).then_inc(hid_ready, 1)

                rest(f"gate_up{n}", gated)
                rest(f"down{n}", tiles(keep if n == 0 else add_and_tell))
            post_norm("post_ffn", "g_post_ffn", lambda c: part_lo("attn_in", c, h[:, c, :]), "res_ffn")

            dve.wait_ge(rope2_ready, 32)
            st = STAGES["attn_in"]

            def attention(p, sub, i, project, attend):
                pa = p - 1
                for j in range(10):
                    s = j - 1
                    if attend and 1 <= j <= 8:
                        hh, b, n1, n2 = STEPS2[s]
                        nb = n1 + 2 * n2
                        for r in range(0, ROUNDS[s], 2):
                            dve.wait_ge(p2t_done, TURNS[-1] * pa + TURNS[s] + r + 1)
                            cols = (min(4 * r + 4, nb) - 4 * r) * P
                            dve.tensor_copy(p2_t[:, 4 * r * P:4 * r * P + cols], ps[:, 5 + r % 2, 0:cols]) \
                               .then_inc(p2t_dve, 1)
                    if attend and j <= 7:
                        hh, b, n1, n2 = STEPS2[j]
                        st_ = stat[:, j % 2, :]
                        dve.wait_ge(s2_done, 8 * pa + j + 1)
                        dve.tensor_reduce(st_[:, 0:1], ps[:, 2, 0:n1 * P], AX.X, ALU.max)
                        dve.tensor_reduce(st_[:, 1:2], ps[:, 3:5, 0:n2 * P], AX.XY, ALU.max)
                        settle()
                        ts(st_[:, 2:3], st_[:, 0:1], st_[:, 1:2], -0.125, ALU.max, ALU.mult).then_inc(max2_ready, 1)
                    if attend and 1 <= j <= 8:
                        st_ = stat[:, s % 2, :]
                        dve.wait_ge(p2_ready, 8 * pa + s + 1)
                        tt(st_[:, 6:7], st_[:, 4:5], st_[:, 5:6], ALU.add)
                        settle()
                        dve.reciprocal(st_[:, 7:8], st_[:, 6:7])
                        settle()
                        dve.wait_ge(o2_done, 8 * pa + s + 1)
                        first = 128 * pa + 64 * hh if False else 128 * pa + 64 * STEPS2[s][0]
                        place = o2_tok[:, STEPS2[s][1], ds(first, 64)]
                        ts(place, ps[:, 7, 0:64], st_[:, 7:8], None, ALU.mult).then_inc(o2_ready, 1)
                    if project and j <= 8 and j % 2 == 0:
                        c = 5 * sub + j // 2
                        n0 = st.slab0 + c + 1
                        dve.wait_ge(whi_ready, st.slab0 + 5 * p + j // 2 + 2)
                        tt(w_lo[:, n0 % 2, :], raw[:, n0 % 2, :], w_hi[:, n0 % 2, :].bitcast(f32), ALU.subtract) \
                            .then_inc(wlo_ready, 1)
                    if project and j >= 1 and (j - 1) % 3 != 2:
                        dve.wait_ge(swap_done, 9 * p + j)
                        tile = qkv[:, sub, j - 1, :]
                        tt(tmp[:, 0, :], ps[:, 7, :], rope_s[:, :], ALU.mult)
                        tt(tile, tile, rope_c[:, :], ALU.mult)
                        settle()
                        tt(tile, tile, tmp[:, 0, :], ALU.add).then_inc(rot_ready, 1)
                        settle()

            attention(0, 0, 0, True, False)
            with dve.Fori(0, HEAD_PAIRS // 2 - 1) as i:
                attention(2 * i + 1, 1, i, True, True)
                attention(2 * i + 2, 0, i + 1, True, True)
            attention(HEAD_PAIRS - 1, 1, 0, True, True)
            attention(HEAD_PAIRS, 0, 0, False, True)
            for c in range(DC):
                part_lo("attn_out", c, ps[:, 5 + c % 2, :])

            def hidden(key):
                def body(st, c, i):
                    for m in range(2):
                        t = 2 * c + m
                        k = t + 4 * i
                        dve.wait_ge(hid_half, HB[key] + k + 1)
                        tt(tmp[:, 2 + t % 2, :], tmp[:, t % 2, :], tmp[:, t % 2, :], ALU.mult)
                        settle()
                        tt(chunk(hid_lo, k), tmp[:, 2 + t % 2, :], chunk(hid_hi, k).bitcast(f32), ALU.subtract) \
                            .then_inc(hid_ready, 1)

                return body

            def layer_norm(layer, part, n, after):
                dve.wait_ge(root_ready, SK[f"mean_{part}_{layer}"] + 1)
                for c in range(DC):
                    tt(y[:, c, :], y[:, c, :], root[:, :], ALU.subtract).then_inc(y_ready, 1)
                settle()
                invert(f"var_{part}_{layer}")
                for c in range(DC):
                    tt(y[:, c, :], y[:, c, :], rstd[:, :], ALU.mult)
                    settle()
                    ts(h[:, c, :], y[:, c, :], gain(f"ln_{part}_g{n}", c), gain(f"ln_{part}_b{n}", c), ALU.mult, ALU.add) \
                        .then_inc(y_ready, 1)
                    settle()
                    if after:
                        part_lo(after, c, h[:, c, :])

            def norm_and_ffn(layer, proj, up, down, n, after):
                rest(proj, tiles(residual_and_tell))
                layer_norm(layer, "mix", n, up)
                rest(f"{up}0", hidden(f"{layer}0"))
                rest(f"{down}0", tiles(residual))
                rest(f"{up}1", hidden(f"{layer}1"))
                rest(f"{down}1", tiles(add_and_tell))
                layer_norm(layer, "ffn", n, after)

            norm_and_ffn("a", "attn_out", "up_a", "down_a", 0, "hgrn_in")

            a0, b0 = GAIN_AT["lb0"], GAIN_AT["lb1"]
            l0, l1 = gains[:, a0:a0 + HG_HEADS], gains[:, b0:b0 + HG_HEADS]
            tt(lbp[:, 4, :], l0, l1, ALU.max)
            settle()
            tt(lbp[:, 2, :], l0, lbp[:, 4, :], ALU.subtract)
            tt(lbp[:, 3, :], l1, lbp[:, 4, :], ALU.subtract).then_inc(lb_half, 1)
            dve.wait_ge(lb_exp, 1)
            tt(lbp[:, 4, :], lbp[:, 2, :], lbp[:, 3, :], ALU.add)
            settle()
            dve.reciprocal(lbp[:, 5, :], lbp[:, 4, :])
            settle()
            tt(lbp[:, 0, :], lbp[:, 3, :], lbp[:, 5, :], ALU.mult)
            tt(lbp[:, 1, :], lbp[:, 2, :], lbp[:, 5, :], ALU.mult)
            settle()
            rest("hgrn_in", lambda st, c, i: None)

            def head(hd, first):
                lb, rest_ = lbp[:, 0, ds(hd, 1)], lbp[:, 1, ds(hd, 1)]
                if not first:
                    dve.wait_ge(oh_done, hd)
                ts(tmp[:, 0, :], chunk(hg_s, hd), rest_, lb, ALU.mult, ALU.add)
                settle()
                tt(f_run[:, :], tmp[:, 0, :], run_mask[:, :], ALU.mult)
                tt(f_start[:, :], tmp[:, 0, :], start_mask[:, :], ALU.mult)
                settle()
                dve.tensor_tensor_scan(f_cum[:, :], f_run[:, :], f_start[:, :], 0.0, ALU.mult, ALU.add)
                settle()
                dve.reciprocal(f_run[:, :], f_cum[:, :])
                tt(q_dec[:, :], chunk(hg_q, hd), f_cum[:, :], ALU.mult)
                settle()
                stt(k_dec[:, :], chunk(hg_k, hd), rest_, f_run[:, :], ALU.mult, ALU.mult).then_inc(dec_ready, 1)
                dve.wait_ge(a_done, hd + 1)
                tt(tmp[:, 3, :], ps[:, 2, :], a_mask[:, :], ALU.mult).then_inc(a_ready, 1)
                dve.wait_ge(kv_done, hd + 1)
                for c in range(7):
                    kv = ps[:, 5 + c % 2, (c // 2) * P:(c // 2 + 1) * P]
                    decay = f_cum[:, CHUNK * c + CHUNK - 1:CHUNK * c + CHUNK]
                    if c == 0:
                        ts(state[:, 1, :], kv, decay, None, ALU.mult)
                        settle()
                    else:
                        tt(state[:, c + 1, :], kv, state[:, c, :], ALU.add)
                        settle()
                        last = ts(state[:, c + 1, :], state[:, c + 1, :], decay, None, ALU.mult)
                        settle()
                last.then_inc(st_ready, 1)
                dve.wait_ge(root_ready, SK["head0"] + hd + 1)
                dve.reciprocal(rstd[:, :], root[:, :]).then_inc(rstd_ready, 1)
                settle()
                stt(tmp[:, 0, :], ps[:, 0, :], gains[:, ds(GAIN_AT["g_hgrn"] + hd, 1)], rstd[:, :], ALU.mult, ALU.mult) \
                    .then_inc(oh_ready, 1)
                settle()
                part_lo("hgrn_out", hd, tmp[:, 0, :])
                settle()

            dve.wait_ge(hm_ready, 48)
            dve.wait_ge(tile_free["act"], STAGES["hgrn_in"].free0 + STAGES["hgrn_in"].tiles)
            head(0, True)
            with dve.Fori(1, HG_HEADS) as hd:
                head(hd, False)
            norm_and_ffn("h", "hgrn_out", "up_h", "down_h", 1, None)


def slabs(weight, kc, order, per, width=None):
    k, n = weight.shape
    tiles = weight.reshape(kc, P, n // P, P).transpose(2, 1, 0, 3)[order]
    tiles = tiles.reshape(len(order) // per, per, P, kc, P).transpose(0, 2, 1, 3, 4)
    return np.ascontiguousarray(tiles.reshape(len(order) // per, P, per * kc * P))


def columns(vector):
    return np.asarray(vector, np.float32).reshape(-1, P).T


def swap_matrix(period, half):
    m = np.zeros((P, P), np.float32)
    for f in range(P):
        d = f % period
        if d < half:
            m[f + half, f] = -1.0
        elif d < 2 * half:
            m[f - half, f] = 1.0
    return m


def shape_constants():
    i, j = np.arange(P)[:, None], np.arange(P)[None, :]

    def mask(valid):
        return np.where(valid, 0.0, NEG).astype(np.float32)

    parts = [mask(j > i), mask(j <= i), mask(j >= i), mask(j <= i)]
    for dilation in (4, 16):
        same = (i - j) % dilation == 0
        parts += [mask(same)] * 3 + [mask(same & (j <= i))]
    const = np.stack([np.eye(P), swap_matrix(64, 8), swap_matrix(64, 32), np.ones((P, P))], 1).astype(np.float32)
    t = np.arange(T, dtype=np.float32)
    d = np.arange(P) % 64
    inv1 = (np.float32(500000.0) ** (-np.arange(8, dtype=np.float32) * np.float32(2.0) / np.float32(16))).astype(np.float32)
    freq = np.where(d < 16, inv1[d % 8], 0.0).astype(np.float32)[:, None]
    inv2 = (np.float32(10000.0) ** (-np.arange(32, dtype=np.float32) * np.float32(2.0 / 64))).astype(np.float32)
    angle = (t[None, :] * inv2[np.arange(P) % 32][:, None]).astype(np.float32)
    rope2 = np.stack([np.cos(angle), np.sin(angle)], 1).astype(np.float32)
    s, c = np.arange(P)[:, None], np.arange(T)[None, :]
    inside = ((c % P) >= s) & ((c % P) // CHUNK == s // CHUNK)
    start = np.broadcast_to((np.arange(T) % CHUNK == 0)[None, :], (P, T))
    hmask = np.stack([inside, ~start, start], 1).astype(np.float32)
    return {
        "iota_in": np.ascontiguousarray(np.broadcast_to(t, (P, T))), "const_in": const, "freq_in": freq,
        "mask_in": np.ascontiguousarray(np.concatenate(parts, 1)), "rope2_in": rope2, "hmask_in": hmask,
    }


def layout(a):
    sent = {}
    w_in = a["w_in"][0]
    heads = w_in[:, HALF:2 * HALF].reshape(D, 2, 4, 64).transpose(0, 2, 1, 3).reshape(D, HALF)
    w_in = np.concatenate([w_in[:, :HALF], heads, w_in[:, 2 * HALF:]], 1)
    w_out = a["w_out"][0]
    rows = w_out[HALF:].reshape(2, 4, 64, D).transpose(1, 0, 2, 3).reshape(HALF, D)
    w_out = np.concatenate([w_out[:HALF], rows], 0)
    g_attn = a["g_attn_out"][0].reshape(2, 4, 64).transpose(1, 0, 2).reshape(HALF)
    w = {"w_in": slabs(w_in, 8, np.arange(10), 2),
         "w_glu": slabs(a["w_glu"][0], 4, np.arange(8).reshape(2, 4).T.ravel(), 4),
         "w_out": slabs(w_out, 8, np.arange(8), 2)}
    first = 0
    for n, c in enumerate(FFN1_PARTS):
        order = np.stack([np.arange(first, first + c), DFF // P + np.arange(first, first + c)], 1).ravel()
        w[f"gate_up{n}"] = slabs(a["w_gate_up"][0], 8, order, 2)
        w[f"down{n}"] = slabs(a["w_down"][0][first * P:(first + c) * P], c, np.arange(8), 1)
        first += c
    tiles = slabs(a["attn_w_in_2"][0], 8, np.arange(72).reshape(9, 8).T.ravel(), 1).reshape(8, 9, P, 8 * P)
    tiles = np.concatenate([tiles, np.zeros((8, 1, P, 8 * P), np.float32)], 1)
    w["attn_in"] = np.ascontiguousarray(tiles.reshape(40, 2, P, 8 * P).transpose(0, 2, 1, 3).reshape(40, P, SLAB))
    w["attn_out"] = slabs(a["attn_w_out_2"][0], 8, np.arange(8), 2)
    w["hgrn_in"] = slabs(a["hgrn_w_in_2"][0], 8, np.arange(24).reshape(3, 8).T.ravel(), 2)
    w["hgrn_out"] = slabs(a["hgrn_w_out_2"][0], 8, np.arange(8), 2)
    for layer, name in enumerate(("a", "h")):
        for n in range(2):
            w[f"up_{name}{n}"] = slabs(a["ffn_w_up_2"][layer], 8, np.arange(16 * n, 16 * n + 16), 2)
            w[f"down_{name}{n}"] = slabs(a["ffn_w_down_2"][layer][2048 * n:2048 * n + 2048], 16, np.arange(8), 1)
    for name, value in w.items():
        sent["w_" + name] = value
    sent["x_in"] = a["x"][0].reshape(T, DC, P).transpose(2, 1, 0)
    vectors = [a["g_pre_mix"], a["g_ssm_out"], g_attn, a["g_post_mix"], a["g_pre_ffn"], a["g_post_ffn"], a["ssm_d"],
               a["b_glu"], a["hgrn_norm_g_2"], a["lb_logits_2"][0], a["lb_logits_2"][1]]
    for layer in range(2):
        vectors += [a["ln_mix_g_2"][layer], a["ln_mix_b_2"][layer], a["ln_ffn_g_2"][layer], a["ln_ffn_b_2"][layer]]
    sent["gains_in"] = np.concatenate([columns(v) for v in vectors], 1)

    def by_state(v):
        return v.reshape(N_PAIR, P).T

    log_dt = np.broadcast_to(a["ssm_log_dt"][0][:, None], (32, 64))
    sent["lam_in"] = np.stack([by_state(a["ssm_lambda_re"][0]), by_state(a["ssm_lambda_im"][0]), by_state(log_dt)], 1)
    sent["sink_in"] = np.broadcast_to(a["attn_sinks"][0].reshape(2, 4).T.reshape(1, 8), (P, 8))

    def padded(v):
        o = np.zeros((N_PAIR, 2, 64, 2, 16), np.float32)
        v = v.reshape(N_PAIR, 2, 64, 16)
        for g in range(2):
            o[:, g, :, g, :] = v[:, g]
        return o.reshape(N_PAIR, P, GW).transpose(1, 0, 2)

    sent["b_in"] = np.stack([padded(a["ssm_b_re"][0]), padded(a["ssm_b_im"][0])], 1)
    sent["c_in"] = np.stack([padded(a["ssm_c_re"][0].transpose(0, 2, 1)), padded(a["ssm_c_im"][0].transpose(0, 2, 1))], 1)
    sent["pos_in"] = np.broadcast_to(a["positions"][0], (P, T))
    sent.update(shape_constants())
    return {k: np.ascontiguousarray(v) for k, v in sent.items()}


def kernel(**inputs):
    import concourse.bacc as bacc
    from concourse.bass_utils import run_bass_kernel_spmd

    sent = layout({k: np.asarray(v) for k, v in inputs.items()})
    nc = bacc.Bacc("TRN2", target_bir_lowering=False, num_devices=1)
    handles = {k: nc.dram_tensor(k, v.shape, mybir.dt.from_np(v.dtype), kind="ExternalInput").ap() for k, v in sent.items()}
    out = nc.dram_tensor("out", (P, DC, T), mybir.dt.float32, kind="ExternalOutput").ap()
    weights = {k: handles.pop("w_" + k) for k in STAGES}
    build(nc, weights, out=out, **handles)
    got = run_bass_kernel_spmd(nc, [sent], core_ids=[0]).results[0]["out"]
    return np.ascontiguousarray(got.transpose(2, 1, 0).reshape(1, T, D))
```

```python
from contextlib import ExitStack

import numpy as np

import concourse.bass as bass
from concourse import mybir

P = 128
T = 512
D = 1024
DC = D // P
TB = T // P
HALF = 512
N_PAIR = 16
GW = 32
DFF = 2816
FFN1_PARTS = (12, 10)
FFN2_PART = 16
HEAD_PAIRS = 8
GROUPS = 3
PAIR_TILES = 3 * GROUPS
CHUNK = 64
HG_HEADS = 8
SLAB = 2048
ALPHA = 4.0 ** 0.25
RMS_EPS = 1e-6
LN_EPS = 1e-5
NEG = -1e30
TWO_PI = 2.0 * np.pi
PI_HI = 6.28125
PI_LO = TWO_PI - PI_HI
PI_IN = 3.1415925
ROUND = 1.5 * 2.0 ** 23
LN2_HI = 0.693359375
LN2_LO = float(np.log(2.0) - 0.693359375)


class Stage:

    def __init__(self, name, slab0, tile0, slabs, kc, body, before, free0):
        self.name, self.slab0, self.tile0, self.slabs = name, slab0, tile0, slabs
        self.kc, self.body = kc, body
        self.reader = "act" if name.startswith(("attn_in", "up_", "hgrn_in")) else "dve"
        self.free0 = free0[self.reader]
        self.before = before
        self.cum = [0]
        for n in body:
            self.cum.append(self.cum[-1] + n)
        self.trips = slabs // len(body)
        self.tiles = self.cum[-1] * self.trips


def plan():
    rows = [("w_in", 5, 8, [2] * 5), ("w_glu", 2, 4, [4, 4]), ("w_out", 4, 8, [2, 2])]
    for n, c in enumerate(FFN1_PARTS):
        rows += [(f"gate_up{n}", c, 8, [2, 2]), (f"down{n}", 8, c, [1, 1])]
    rows += [("attn_in", 5 * HEAD_PAIRS, 8, [2, 2, 2, 2, 1] * 2), ("attn_out", 4, 8, [2, 2])]
    for n in range(2):
        rows += [(f"up_a{n}", 8, 8, [2, 2]), (f"down_a{n}", 8, 16, [1, 1])]
    rows += [("hgrn_in", 2 * HG_HEADS, 8, [2, 1] * 2), ("hgrn_out", 4, 8, [2, 2])]
    for n in range(2):
        rows += [(f"up_h{n}", 8, 8, [2, 2]), (f"down_h{n}", 8, 16, [1, 1])]
    stages, slab, tile, s, free = {}, 0, 0, None, {"act": 0, "dve": 0}
    for name, slabs, kc, body in rows:
        s = Stage(name, slab, tile, slabs, kc, body, s, free)
        stages[name] = s
        slab, tile = slab + s.slabs, tile + s.tiles
        free[s.reader] += s.tiles
    return stages


STAGES = plan()
GAINS = ["g_pre_mix", "g_ssm", "g_attn", "g_post_mix", "g_pre_ffn", "g_post_ffn", "d", "b_glu", "g_hgrn", "lb0", "lb1",
         "ln_mix_g0", "ln_mix_b0", "ln_ffn_g0", "ln_ffn_b0", "ln_mix_g1", "ln_mix_b1", "ln_ffn_g1", "ln_ffn_b1"]
GAIN_COLS = [8, 4, 4, 8, 8, 8, 4, 8, 8, 8, 8] + [8] * 8
GAIN_AT = dict(zip(GAINS, np.cumsum([0] + GAIN_COLS[:-1]).tolist()))
N_GAIN = sum(GAIN_COLS)


def build(nc, w, x_in, gains_in, lam_in, sink_in, b_in, c_in, pos_in, iota_in, const_in, freq_in, mask_in, rope2_in,
          hmask_in, out):
    f32, f32r, bf16, i32 = mybir.dt.float32, mybir.dt.float32r, mybir.dt.bfloat16, mybir.dt.int32
    ALU, ACT, AX = mybir.AluOpType, mybir.ActivationFunctionType, mybir.AxisListType
    ds = bass.ds

    base = (nc.sbuf_base + 63) // 64 * 64
    KB = 1024
    RAW_AT = base
    WH_AT = RAW_AT + 16 * KB
    WL_AT = WH_AT + 16 * KB
    XH_AT = WL_AT + 16 * KB
    XL_AT = XH_AT + 16 * KB
    H_AT = XL_AT + 16 * KB
    Y_AT = H_AT + 16 * KB
    BIG_AT = Y_AT + 16 * KB
    EX_AT = BIG_AT + 64 * KB
    used = [EX_AT]

    def at(name, offset, shape, dt=f32):
        return nc.alloc_sbuf_tensor_at(name, [P] + list(shape), dt, offset=offset)

    where = {}

    def extra(name, shape, dt=f32):
        size = int(np.prod(shape)) * (2 if dt == bf16 else 4)
        where[name] = used[0]
        used[0] += (size + 31) // 32 * 32
        return at(name, where[name], shape, dt)

    raw = at("raw", RAW_AT, [2, SLAB])
    w_hi = at("w_hi", WH_AT, [2, SLAB], f32r)
    w_lo = at("w_lo", WL_AT, [2, SLAB], f32r)
    x_hi = at("x_hi", XH_AT, [DC, T], f32r)
    x_lo = at("x_lo", XL_AT, [DC, T], f32r)
    h = at("h", H_AT, [DC, T])
    y = at("y", Y_AT, [DC, T])
    hid_hi = at("hid_hi", BIG_AT, [16, T], f32r)
    hid_lo = at("hid_lo", BIG_AT + 32 * KB, [16, T], f32r)

    x_raw = at("x_raw", Y_AT, [DC, T])
    u = at("u", Y_AT, [4, T])
    q1 = at("q1", Y_AT + 8 * KB, [4, T])
    o1_tok = at("o1_tok", Y_AT, [TB, HALF])
    mask_raw = at("mask_raw", H_AT, [1536])
    b_re = at("b_re", BIG_AT + 56 * KB, [N_PAIR, GW])
    b_im = at("b_im", BIG_AT + 58 * KB, [N_PAIR, GW])
    bb_re = at("bb_re", BIG_AT + 60 * KB, [N_PAIR, GW])
    bb_im = at("bb_im", BIG_AT + 62 * KB, [N_PAIR, GW])
    cos_t = at("cos_t", BIG_AT, [N_PAIR, T])
    sin_t = at("sin_t", BIG_AT + 32 * KB, [N_PAIR, T])
    prod = at("prod", H_AT, [4, T])
    k1 = at("k1", H_AT + 8 * KB, [T])
    v1 = at("v1", H_AT + 10 * KB, [T])
    v1_tok = at("v1_tok", H_AT + 12 * KB, [TB, P])
    qr1 = at("qr1", BIG_AT, [2, T])
    mod = at("mod", XH_AT + 8 * KB, [4, T])
    scan = at("scan", XL_AT + 8 * KB, [2, T])
    p1 = at("p1", BIG_AT + 4 * KB, [4, 4 * P])
    p1_t = at("p1_t", BIG_AT + 12 * KB, [2, 4 * P])

    qkv = at("qkv", BIG_AT, [2, PAIR_TILES, T])
    v_tok = at("v_tok", BIG_AT + 36 * KB, [2, GROUPS, TB, P])
    p2 = at("p2", BIG_AT + 48 * KB, [2, 10 * P])
    p2_t = at("p2_t", BIG_AT + 58 * KB, [10 * P])
    o2_tok = at("o2_tok", Y_AT, [TB, D])

    hg_q = at("hg_q", BIG_AT, [2, T])
    hg_s = at("hg_s", BIG_AT + 4 * KB, [2, T])
    hg_k = at("hg_k", BIG_AT + 8 * KB, [2, T])
    hg_v = at("hg_v", BIG_AT + 12 * KB, [2, T])
    f_cum = at("f_cum", BIG_AT + 16 * KB, [2, T])
    q_dec = at("q_dec", BIG_AT + 20 * KB, [2, T])
    k_dec = at("k_dec", BIG_AT + 24 * KB, [2, T])
    hg_o = at("hg_o", BIG_AT + 32 * KB, [HG_HEADS, T])
    f_run = at("f_run", Y_AT, [T])
    f_start = at("f_start", Y_AT + 2 * KB, [T])
    k_tok = at("k_tok", Y_AT + 12 * KB, [TB, P])
    v_htok = at("v_htok", Y_AT + 14 * KB, [TB, P])

    consts = extra("consts", [4, P])
    ident, swap1, swap2, ones = (consts[:, n, :] for n in range(4))
    ident_b = extra("ident_b", [P], bf16)
    masks = extra("masks", [1536], bf16)
    rope_c = extra("rope_c", [T])
    rope_s = extra("rope_s", [T])
    gains = extra("gains", [N_GAIN])
    lam = extra("lam", [3, N_PAIR])
    par = extra("par", [26, N_PAIR])
    sink = extra("sink", [8])
    eps = extra("eps", [3])
    freq = extra("freq", [1])
    sq = extra("sq", [2, T])
    root = extra("root", [T])
    rstd = extra("rstd", [T])
    tmp = extra("tmp", [4, T])
    c_re = extra("c_re", [N_PAIR, GW])
    c_im = extra("c_im", [N_PAIR, GW])
    assert used[0] <= nc.sbuf_usable_end, used[0] - nc.sbuf_usable_end
    b_lhs = at("b_lhs", where["sq"], [2, 4, P])
    c_neg = at("c_neg", where["root"], [N_PAIR, GW])
    iota = at("iota", where["tmp"] + 6 * KB, [T])
    pos = at("pos", where["tmp"], [T], i32)
    a_mask = at("a_mask", where["c_re"], [T])
    run_mask = at("run_mask", where["rope_c"], [T])
    stat = at("stat", where["c_im"], [4, 16])
    lbp = at("lbp", where["c_im"] + 256, [6, HG_HEADS])
    start_mask = at("start_mask", where["rope_s"], [T])
    state = at("state", where["tmp"] + 2 * KB, [8, P])
    acc, acc_sq = tmp[:, 0, :], tmp[:, 1, :]
    m1, m2, mp2, mp3 = masks[:, 0:256], masks[:, 256:512], masks[:, 512:1024], masks[:, 1024:1536]

    def gain(name, c):
        return gains[:, GAIN_AT[name] + c:GAIN_AT[name] + c + 1]

    def chunk(buf, c):
        if isinstance(c, int):
            return buf[:, c, :]
        return buf[:, ds(c, 1), :].rearrange("p a t -> p (a t)")

    ps = nc.alloc_psum_tensor("ps", [P, 8, T], f32)
    SUM = 7

    def counts(rows):
        at_, n = {}, 0
        for name, c in rows:
            at_[name] = n
            n += c
        return at_

    XB = counts([("w_in", 8), ("w_glu", 4), ("w_out", 8), ("gate_up", 8), ("attn_in", 8), ("attn_out", 8),
                 ("up_a", 8), ("hgrn_in", 8), ("hgrn_out", 8), ("up_h", 8)])
    LN = [(f"{kind}_{part}_{layer}", 8) for layer in "ah" for part in ("mix", "ffn") for kind in ("out", "mid", "res")]
    YB = counts([("attn1", 4), ("glu", 4), ("w_out", 8), ("res_mix", 8), ("ffn", 8), ("res_ffn", 8)] + LN)
    HB = counts([("0", FFN1_PARTS[0]), ("1", FFN1_PARTS[1])] +
                [(f"{layer}{n}", FFN2_PART) for layer in "ah" for n in range(2)])
    SUMS = [("pre_mix", 8), ("ssm", 4), ("attn", 4), ("post_mix", 0), ("pre_ffn", 8), ("post_ffn", 0)]
    for part in ("mix_a", "ffn_a"):
        SUMS += [("mean_" + part, 0), ("var_" + part, 8)]
    SUMS += [(f"head{n}", 1) for n in range(HG_HEADS)]
    for part in ("mix_h", "ffn_h"):
        SUMS += [("mean_" + part, 0), ("var_" + part, 8)]
    SB = counts(SUMS)
    SK = {name: k for k, (name, _) in enumerate(SUMS)}
    SK_ROOT = counts([(name, 0 if name.startswith("mean") else 1) for name, _ in SUMS])
    ACCS = [("post_mix", "w_out"), ("post_ffn", "ffn"), ("mean_mix_a", "out_mix_a"), ("mean_ffn_a", "out_ffn_a"),
            ("mean_mix_h", "out_mix_h"), ("mean_ffn_h", "out_ffn_h")]
    ACC = {name: k for k, (name, _) in enumerate(ACCS)}
    PR = {name: k for k, name in enumerate(
        ["lr", "dt", "z", "k", "f", "e", "two_k", "em1", "mag", "th", "r", "r_turn", "r_hi", "r_lo", "sin", "sin_half",
         "c1", "am1", "ai", "den", "nr", "ni", "fr", "fi", "t0", "t1"])}

    def sem(name):
        return nc.alloc_semaphore(name)

    raw_ready = [sem("raw_ready0"), sem("raw_ready1")]
    whi_ready = sem("whi_ready")
    wlo_ready = sem("wlo_ready")
    tile_done = sem("tile_done")
    tile_free = {e: sem("tile_free_" + e) for e in ("dve", "act")}
    xhi_ready = sem("xhi_ready")
    xlo_ready = sem("xlo_ready")
    y_ready = sem("y_ready")
    merge_ready = sem("merge_ready")
    gate_scaled = sem("gate_scaled")
    silu_ready = sem("silu_ready")
    hid_pre = sem("hid_pre")
    hid_half = sem("hid_half")
    hid_ready = sem("hid_ready")
    sq_ready = sem("sq_ready")
    sq_used = sem("sq_used")
    acc_ready = sem("acc_ready")
    acc_summed = sem("acc_summed")
    root_ready = sem("root_ready")
    result_ready = sem("result_ready")
    rstd_ready = sem("rstd_ready")
    x_ready = [sem("x_ready0"), sem("x_ready1")]
    gains_ready = sem("gains_ready")
    small_ready = sem("small_ready")
    eps_ready = sem("eps_ready")
    mask_ready = sem("mask_ready")
    dt_ready = sem("dt_ready")
    turn_ready = sem("turn_ready")
    sines_ready = sem("sines_ready")
    rope_ang = sem("rope_ang")
    rope_ready = sem("rope_ready")
    bb_ready = sem("bb_ready")
    bt_done = sem("bt_done")
    blhs_ready = sem("blhs_ready")
    ang_ready = {e: sem("ang_ready_" + e) for e in ("dve", "pool")}
    ang_used = sem("ang_used")
    bu_done = sem("bu_done")
    bu_free = sem("bu_free")
    scan_ready = sem("scan_ready")
    prod_ready = sem("prod_ready")
    yssm_done = sem("yssm_done")
    pre_gelu = sem("pre_gelu")
    gelu_ready = sem("gelu_ready")
    gate_ready = sem("gate_ready")
    vt1_done, vt1_ready = sem("vt1_done"), sem("vt1_ready")
    kr1_swap, kr1_ready = sem("kr1_swap"), sem("kr1_ready")
    qr1_swap, qr1_ready = sem("qr1_swap"), sem("qr1_ready")
    s1_done = sem("s1_done")
    max1_ready = sem("max1_ready")
    p1_ready = sem("p1_ready")
    p1t_done, p1t_ready = sem("p1t_done"), sem("p1t_ready")
    o1_done, o1_ready = sem("o1_done"), sem("o1_ready")
    o1t_done = sem("o1t_done")
    h_back = sem("h_back")
    swap_done = sem("swap_done")
    rot_ready = sem("rot_ready")
    vtok_ready = sem("vtok_ready")
    s2_done, max2_ready, p2_ready = sem("s2_done"), sem("max2_ready"), sem("p2_ready")
    p2t_done = sem("p2t_done")
    p2t_dve, p2t_act = sem("p2t_dve"), sem("p2t_act")
    o2_done, o2_ready = sem("o2_done"), sem("o2_ready")
    o2t_done = sem("o2t_done")
    rope2_ready = sem("rope2_ready")
    hm_ready = sem("hm_ready")
    lb_half, lb_exp = sem("lb_half"), sem("lb_exp")
    dec_ready = sem("dec_ready")
    a_done, a_ready = sem("a_done"), sem("a_ready")
    ht_done, ht_ready = sem("ht_done"), sem("ht_ready")
    kv_done, st_ready = sem("kv_done"), sem("st_ready")
    oh_done, oh_ready = sem("oh_done"), sem("oh_ready")
    out_done = sem("out_done")

    LAST = STAGES["down_h1"]
    SMALL = 11
    SCORES1 = (3, 4, 0, 1)
    ANGLES = (3, 6, 9, 12, N_PAIR)
    POOL_PAIRS = range(3, N_PAIR, 3)
    BLOCKS1 = [(b, min(b, 1) + 1) for b in range(TB)]
    BLOCKS2 = [(b, min(b, 1) + 1, b + 1) for b in range(TB)]
    STEPS2 = [(hh, *blk) for hh in range(2) for blk in BLOCKS2]
    ROUNDS = [-(-(n1 + 2 * n2) // 4) for _, _, n1, n2 in STEPS2]
    TURNS = np.cumsum([0] + ROUNDS).tolist()
    DVE_TURNS = np.cumsum([0] + [(r + 1) // 2 for r in ROUNDS]).tolist()
    ACT_TURNS = np.cumsum([0] + [r // 2 for r in ROUNDS]).tolist()

    def run(eng, st, body):
        if st.trips == 1:
            body(0, False)
        elif st is LAST:
            with eng.Fori(0, st.trips - 1) as i:
                body(i, False)
            body(st.trips - 1, True)
        else:
            with eng.Fori(0, st.trips) as i:
                body(i, False)

    with nc.Block() as block:

        @block.sync
        def _(sp):
            for half in range(2):
                sp.dma_start(x_raw[:, 4 * half:4 * half + 4, :], x_in[:, 4 * half:4 * half + 4, :]) \
                  .then_inc(x_ready[half], 16)
            for name, st in STAGES.items():

                def load(i, last, st=st, src=w[name]):
                    for c, tiles in enumerate(st.body):
                        n = st.slab0 + c + len(st.body) * i
                        slot, width = (st.slab0 + c) % 2, tiles * st.kc * P
                        if st.slab0 + c >= 2:
                            sp.wait_ge(wlo_ready, n - 1)
                        row = c + len(st.body) * i
                        part = src[row, :, 0:width] if isinstance(row, int) else \
                            src[ds(row, 1), :, 0:width].rearrange("a p n -> p (a n)")
                        sp.dma_start(raw[:, slot, 0:width], part).then_inc(raw_ready[slot], 16)

                with_loop = st.trips > 1
                if with_loop:
                    with sp.Fori(0, st.trips) as i:
                        load(i, False)
                else:
                    load(0, False)
            for c in range(DC):
                sp.wait_ge(result_ready, c + 1)
                sp.dma_start(out[:, c, :], h[:, c, :]).then_inc(out_done, 16)
            sp.wait_ge(out_done, 16 * DC)

        @block.gpsimd
        def _(pool):
            def angle_step(out, src, *how):
                pool.tensor_scalar(out, src, *how)
                pool.drain()

            pool.wait_ge(small_ready, 16 * SMALL)
            pool.wait_ge(turn_ready, 2)
            for pr in POOL_PAIRS:
                if pr == 12:
                    pool.wait_ge(bt_done, 1)
                ang, k = sin_t[:, pr, :], cos_t[:, pr, :]
                r_hi, r_lo, r_turn = (par[:, PR[n], pr:pr + 1] for n in ("r_hi", "r_lo", "r_turn"))
                pool.tensor_scalar(ang, iota[:, :], r_hi, None, ALU.mult)
                angle_step(k, iota[:, :], r_turn, ROUND, ALU.mult, ALU.add)
                angle_step(k, k, ROUND, None, ALU.subtract)
                pool.tensor_tensor(ang, ang, k, ALU.subtract)
                pool.drain()
                angle_step(k, iota[:, :], r_lo, None, ALU.mult)
                pool.tensor_tensor(ang, ang, k, ALU.add)
                pool.drain()
                pool.tensor_scalar(ang, ang, 0.5, -0.5, ALU.min, ALU.max).then_inc(ang_ready["pool"], 1)

            for pr in range(N_PAIR):
                for n, (part, by) in enumerate(((0, cos_t), (0, sin_t), (1, sin_t), (1, cos_t))):
                    pool.wait_ge(scan_ready, 2 * pr + part + 1)
                    if pr:
                        pool.wait_ge(yssm_done, 4 * pr + n - 3)
                    pool.tensor_tensor(prod[:, n, :], scan[:, part, :], by[:, pr, :], ALU.mult).then_inc(prod_ready, 1)

            for name, event in ACCS:
                plain = name.startswith("mean")
                for c in range(DC):
                    pool.wait_ge(y_ready, YB[event] + c + 1)
                    if plain and c == 1:
                        last = pool.tensor_tensor(acc, y[:, 0, :], y[:, 1, :], ALU.add)
                    elif plain and c:
                        last = pool.tensor_tensor(acc, acc, y[:, c, :], ALU.add)
                    elif not plain:
                        last = pool.tensor_tensor(acc_sq if c else acc, y[:, c, :], y[:, c, :], ALU.mult)
                        if c:
                            pool.drain()
                            last = pool.tensor_tensor(acc, acc, acc_sq, ALU.add)
                    if c < DC - 1 and (c or not plain):
                        pool.drain()
                last.then_inc(acc_ready, 1)

        @block.tensor
        def _(pe):
            def slab(st, c, i, xs=None):
                slot, per = (st.slab0 + c) % 2, st.cum[-1]
                pe.wait_ge(wlo_ready, st.slab0 + c + 1 + len(st.body) * i)
                hi, lo = xs or (x_hi, x_lo)
                for m in range(st.body[c]):
                    t0 = st.tile0 + st.cum[c] + m
                    if st.free0 + st.cum[c] + m >= 2:
                        pe.wait_ge(tile_free[st.reader], st.free0 + st.cum[c] + m - 1 + per * i)
                    o = ps[:, t0 % 2, :]
                    for k in range(st.kc):
                        a = (m * st.kc + k) * P
                        pe.matmul(o, w_lo[:, slot, a:a + P], hi[:, k, :], start=k == 0, stop=False)
                        pe.matmul(o, w_hi[:, slot, a:a + P], lo[:, k, :], start=False, stop=False)
                        last = pe.matmul(o, w_hi[:, slot, a:a + P], hi[:, k, :], start=False, stop=k == st.kc - 1)
                    last.then_inc(tile_done, 1)

            def read_out(before, st):
                if before.reader != st.reader:
                    pe.wait_ge(tile_free[before.reader], before.free0 + before.tiles)

            def first_slab(st, xs, ready, before, beside):
                slot = st.slab0 % 2
                pe.wait_ge(wlo_ready, st.slab0 + 1)
                hi, lo = xs or (x_hi, x_lo)
                for k in range(st.kc):
                    pe.wait_ge(ready, before + k + 1)
                    for m in range(st.body[0]):
                        if k == 0 and st.free0 + m >= 2:
                            pe.wait_ge(tile_free[st.reader], st.free0 + m - 1)
                        o, a = ps[:, (st.tile0 + m) % 2, :], (m * st.kc + k) * P
                        pe.matmul(o, w_lo[:, slot, a:a + P], hi[:, k, :], start=k == 0, stop=False)
                        pe.matmul(o, w_hi[:, slot, a:a + P], lo[:, k, :], start=False, stop=False)
                        last = pe.matmul(o, w_hi[:, slot, a:a + P], hi[:, k, :], start=False, stop=k == st.kc - 1)
                        if k == st.kc - 1:
                            last.then_inc(tile_done, 1)
                    if beside:
                        beside(k)

            def dense(name, operand=None, xs=None, hid=None, beside=None):
                st = STAGES[name]
                read_out(st.before, st)
                assert st.body[0] <= 2 or not beside
                if st.body[0] > 2:
                    pe.wait_ge(xlo_ready, XB[operand] + st.kc)
                    run(pe, st, lambda i, last: [slab(st, c, i, xs) for c in range(len(st.body))])
                    return
                if operand or hid is not None:
                    first_slab(st, xs, hid_ready if hid is not None else xlo_ready,
                               hid if hid is not None else XB[operand], beside)
                else:
                    slab(st, 0, 0, xs)
                for c in range(1, len(st.body)):
                    slab(st, c, 0, xs)
                with pe.Fori(1, st.trips) as i:
                    for c in range(len(st.body)):
                        slab(st, c, i, xs)

            def feature_sum(name, n):
                for c in range(n):
                    sum_chunk(name, n, c)

            def sum_chunk(name, n, c):
                if SK[name] and c == 0:
                    pe.wait_ge(root_ready, SK[name])
                j = SB[name] + c
                pe.wait_ge(sq_ready, j + 1)
                pe.matmul(ps[:, SUM, :], ones, sq[:, j % 2, :], start=c == 0, stop=c == n - 1).then_inc(sq_used, 1)

            def acc_sum(name):
                pe.wait_ge(root_ready, SK[name])
                pe.wait_ge(acc_ready, ACC[name] + 1)
                pe.matmul(ps[:, SUM, :], ones, acc, start=True, stop=True).then_inc(acc_summed, 1)

            pe.wait_ge(small_ready, 16 * SMALL)
            st = STAGES["w_in"]
            first_slab(st, None, xlo_ready, XB["w_in"], lambda k: sum_chunk("pre_mix", DC, k))
            for c in range(1, 5):
                slab(st, c, 0)
                if c == 2:
                    pe.wait_ge(bb_ready, 1)
                    for n, bb in enumerate((bb_re, bb_im)):
                        for i in range(4):
                            last = pe.transpose(ps[:, 2 + n, i * P:(i + 1) * P],
                                                bb[:, 4 * i:4 * i + 4, :].rearrange("p a c -> p (a c)"), ident)
                    last.then_inc(bt_done, 1)

            def ssm_in(pr):
                i, q = divmod(pr, 4)
                if pr >= 2:
                    pe.wait_ge(bu_free, pr - 1)
                for n in range(2):
                    last = pe.matmul(ps[:, 2 + 2 * (pr % 2) + n, :], b_lhs[GW * q:GW * q + GW, n, i, :],
                                     u[GW * q:GW * q + GW, i, :], start=True, stop=True)
                last.then_inc(bu_done, 1)

            def ssm_out(pr):
                i, q = divmod(pr, 4)
                if q == 0 and i:
                    pe.wait_ge(pre_gelu, i)
                for n, cc in enumerate((c_re, c_im, c_neg, c_im)):
                    pe.wait_ge(prod_ready, 4 * pr + n + 1)
                    pe.matmul(ps[GW * q:GW * q + GW, 6, :], cc[:, pr, :], prod[:, n, :],
                              start=n == 0, stop=n == 3).then_inc(yssm_done, 1)

            pe.wait_ge(blhs_ready, 1)
            pe.wait_ge(tile_free["dve"], STAGES["w_in"].tiles)
            ssm_in(0)
            ssm_in(1)
            for pr in range(N_PAIR):
                if pr + 2 < N_PAIR:
                    ssm_in(pr + 2)
                ssm_out(pr)

            pe.wait_ge(mask_ready, 1)
            pe.wait_ge(pre_gelu, 4)
            for b in range(TB):
                last = pe.transpose(ps[:, 2, b * P:(b + 1) * P], v1[:, b * P:(b + 1) * P], ident)
            last.then_inc(vt1_done, 1)
            pe.matmul(ps[:, 3, :], swap1, k1[:, :], start=True, stop=True).then_inc(kr1_swap, 1)
            pe.wait_ge(vt1_ready, 1)
            pe.wait_ge(kr1_ready, 1)
            steps = [(hh, b, n) for hh in range(2) for b, n in BLOCKS1]
            with pe.Fori(0, 2) as i:
                pe.wait_ge(o1_ready, 8 * i)
                for m in range(2):
                    pe.matmul(ps[:, (2, SUM)[m], :], swap1, chunk(q1, 2 * i + m), start=True, stop=True) \
                      .then_inc(qr1_swap, 1)
                pe.wait_ge(qr1_ready, 2 * i + 2)

                def scores1(s):
                    hh, b, n = steps[s]
                    if s >= 4:
                        pe.wait_ge(p1_ready, 8 * i + s - 3)
                    for m in range(2):
                        o = ps[:, SCORES1[s % 4], 2 * P * m:2 * P * m + n * P]
                        pe.matmul(o, qr1[64 * hh:64 * hh + 64, m, b * P:(b + 1) * P],
                                  k1[64 * hh:64 * hh + 64, (b + 1 - n) * P:(b + 1) * P], start=True, stop=False)
                        last = pe.matmul(o, ident_b[:, :], m1[:, 2 * P - n * P:2 * P], start=False, stop=True)
                    last.then_inc(s1_done, 1)

                def turn1(s):
                    hh, b, n = steps[s]
                    pe.wait_ge(p1_ready, 8 * i + s + 1)
                    if s >= 2:
                        pe.wait_ge(p1t_ready, 8 * i + s - 1)
                    for m in range(2):
                        for j in range(n):
                            last = pe.transpose(ps[:, (5, SUM)[s % 2], (m * n + j) * P:(m * n + j + 1) * P],
                                                p1[:, s % 4, (2 * m + j) * P:(2 * m + j + 1) * P], ident)
                    last.then_inc(p1t_done, 1)

                def values1(s):
                    hh, b, n = steps[s]
                    pe.wait_ge(p1t_ready, 8 * i + s + 1)
                    if s >= 2:
                        pe.wait_ge(o1_ready, 8 * i + s - 1)
                    for m in range(2):
                        for j in range(n):
                            last = pe.matmul(ps[:, (6, 2)[s % 2], 64 * m:64 * m + 64], p1_t[:, s % 2, (m * n + j) * P:(m * n + j + 1) * P],
                                             v1_tok[:, b + 1 - n + j, 64 * hh:64 * hh + 64], start=j == 0, stop=j == n - 1)
                    last.then_inc(o1_done, 1)

                scores1(0)
                scores1(1)
                for s in range(8):
                    if s < 6:
                        scores1(s + 2)
                    turn1(s)
                    if s:
                        values1(s - 1)
                values1(7)
            pe.wait_ge(o1_ready, 16)
            for c in range(4):
                if c >= 2:
                    pe.wait_ge(y_ready, YB["attn1"] + c - 1)
                for b in range(TB):
                    last = pe.transpose(ps[:, 4 + c % 2, b * P:(b + 1) * P], o1_tok[:, b, c * P:(c + 1) * P], ident)
                last.then_inc(o1t_done, 1)

            dense("w_glu", "w_glu")
            feature_sum("ssm", 4)
            feature_sum("attn", 4)
            dense("w_out", "w_out")
            acc_sum("post_mix")
            for n in range(2):
                if n == 0:
                    dense("gate_up0", "gate_up", beside=lambda k: sum_chunk("pre_ffn", DC, k))
                else:
                    dense("gate_up1")
                dense(f"down{n}", None, (hid_hi, hid_lo), HB[str(n)])
            acc_sum("post_ffn")

            st = STAGES["attn_in"]

            def attention(p, sub, i, project, attend):
                old, pa = 1 - sub, p - 1
                tile = st.free0 + PAIR_TILES * p
                for j in range(10):
                    s = j - 1
                    if attend and 1 <= j <= 8:
                        hh, b, n1, n2 = STEPS2[s]
                        nb = n1 + 2 * n2
                        pe.wait_ge(p2_ready, 8 * pa + s + 1)
                        for r in range(ROUNDS[s]):
                            if r == 2:
                                pe.wait_ge(p2t_dve, DVE_TURNS[-1] * pa + DVE_TURNS[s] + 1)
                            for a in range(4 * r, min(4 * r + 4, nb)):
                                last = pe.transpose(ps[:, 5 + r % 2, (a - 4 * r) * P:(a - 4 * r + 1) * P],
                                                    p2[:, s % 2, a * P:(a + 1) * P], ident)
                            last.then_inc(p2t_done, 1)
                    if attend and j <= 7:
                        hh, b, n1, n2 = STEPS2[j]
                        if j == 0:
                            pe.wait_ge(rot_ready, 6 * pa + 6)
                            pe.wait_ge(vtok_ready, 3 * pa + 3)
                        lo_, hi_ = 64 * hh, 64 * hh + 64
                        for g, (n, mask) in enumerate(((n1, m2), (n2, mp2), (n2, mp3))):
                            o = ps[:, 2 + g, 0:n * P]
                            k0 = b + 1 - n
                            pe.matmul(o, qkv[lo_:hi_, old, 3 * g, b * P:(b + 1) * P],
                                      qkv[lo_:hi_, old, 3 * g + 1, k0 * P:(b + 1) * P], start=True, stop=False)
                            full = 2 * P if g == 0 else 4 * P
                            last = pe.matmul(o, ident_b[:, :], mask[:, full - n * P:full], start=False, stop=True)
                        last.then_inc(s2_done, 1)
                    if attend and 1 <= j <= 8:
                        hh, b, n1, n2 = STEPS2[s]
                        pe.wait_ge(p2t_dve, DVE_TURNS[-1] * pa + DVE_TURNS[s + 1])
                        if ACT_TURNS[s + 1] > ACT_TURNS[s]:
                            pe.wait_ge(p2t_act, ACT_TURNS[-1] * pa + ACT_TURNS[s + 1])
                        if j >= 2 and project:
                            if (j - 2) % 3 == 2:
                                pe.wait_ge(vtok_ready, 3 * p + (j - 2) // 3 + 1)
                            else:
                                pe.wait_ge(rot_ready, 6 * p + 2 * ((j - 2) // 3) + (j - 2) % 3 + 1)
                        elif j >= 2:
                            pe.wait_ge(o2_ready, 8 * pa + s)
                        a = 0
                        nb = n1 + 2 * n2
                        for g, n in enumerate((n1, n2, n2)):
                            for kb in range(b + 1 - n, b + 1):
                                last = pe.matmul(ps[:, 7, 0:64], p2_t[:, a * P:(a + 1) * P],
                                                 v_tok[:, old, g, kb, 64 * hh:64 * hh + 64],
                                                 start=a == 0, stop=a == nb - 1)
                                a += 1
                        last.then_inc(o2_done, 1)
                    if project and j <= 8:
                        project_tile(p, sub, i, j)
                    if project and j >= 1:
                        t = j - 1
                        pe.wait_ge(tile_free["act"], tile + t + 1)
                        if attend and j <= 8:
                            pe.wait_ge(o2_ready, 8 * pa + s + 1)
                        elif t >= 1:
                            if (t - 1) % 3 == 2:
                                pe.wait_ge(vtok_ready, 3 * p + (t - 1) // 3 + 1)
                            else:
                                pe.wait_ge(rot_ready, 6 * p + 2 * ((t - 1) // 3) + (t - 1) % 3 + 1)
                        if t % 3 == 2:
                            for b in range(TB):
                                last = pe.transpose(ps[:, 7, b * P:(b + 1) * P], qkv[:, sub, t, b * P:(b + 1) * P], ident)
                        else:
                            last = pe.matmul(ps[:, 7, :], swap2, qkv[:, sub, t, :], start=True, stop=True)
                        last.then_inc(swap_done, 1)

            def project_tile(p, sub, i, j):
                c = 5 * sub + j // 2
                slot, m = (st.slab0 + c) % 2, j % 2
                if m == 0:
                    pe.wait_ge(wlo_ready, st.slab0 + 5 * p + j // 2 + 1)
                t0 = st.tile0 + 9 * sub + j
                if not (isinstance(p, int) and p == 0 and j < 2):
                    pe.wait_ge(tile_free["act"], st.free0 + 9 * p + j - 1)
                o = ps[:, t0 % 2, :]
                for k in range(DC):
                    if isinstance(p, int) and p == 0 and j == 0:
                        pe.wait_ge(xlo_ready, XB["attn_in"] + k + 1)
                    a = (m * DC + k) * P
                    pe.matmul(o, w_lo[:, slot, a:a + P], x_hi[:, k, :], start=k == 0, stop=False)
                    pe.matmul(o, w_hi[:, slot, a:a + P], x_lo[:, k, :], start=False, stop=False)
                    last = pe.matmul(o, w_hi[:, slot, a:a + P], x_hi[:, k, :], start=False, stop=k == DC - 1)
                last.then_inc(tile_done, 1)

            read_out(st.before, st)
            attention(0, 0, 0, True, False)
            with pe.Fori(0, HEAD_PAIRS // 2 - 1) as i:
                attention(2 * i + 1, 1, i, True, True)
                attention(2 * i + 2, 0, i, True, True)
            attention(HEAD_PAIRS - 1, 1, 0, True, True)
            attention(HEAD_PAIRS, 0, 0, False, True)
            pe.wait_ge(o2_ready, 8 * HEAD_PAIRS)
            for c in range(DC):
                if c >= 2:
                    pe.wait_ge(xlo_ready, XB["attn_out"] + c - 1)
                for b in range(TB):
                    last = pe.transpose(ps[:, 5 + c % 2, b * P:(b + 1) * P], o2_tok[:, b, c * P:(c + 1) * P], ident)
                last.then_inc(o2t_done, 1)

            def norm_and_ffn(layer, proj, up, down, part):
                dense(proj, proj)
                acc_sum(f"mean_mix_{layer}")
                feature_sum(f"var_mix_{layer}", DC)
                for n in range(2):
                    dense(f"{up}{n}", up if n == 0 else None)
                    dense(f"{down}{n}", None, (hid_hi, hid_lo), HB[f"{layer}{n}"])
                acc_sum(f"mean_ffn_{layer}")
                feature_sum(f"var_ffn_{layer}", DC)

            norm_and_ffn("a", "attn_out", "up_a", "down_a", FFN2_PART)

            st = STAGES["hgrn_in"]
            O_BANK = SUM

            def hgrn_tile(hd, par, j, chunks):
                c, m = 2 * par + j // 2, j % 2
                slot, o = (st.slab0 + c) % 2, ps[:, (st.tile0 + 3 * par + j) % 2, :]
                if 0 in chunks:
                    if m == 0:
                        pe.wait_ge(wlo_ready, st.slab0 + 2 * hd + j // 2 + 1)
                    pe.wait_ge(tile_free["act"], st.free0 + 3 * hd + j - 1)
                for k in chunks:
                    if isinstance(hd, int) and hd == 0 and j == 0:
                        pe.wait_ge(xlo_ready, XB["hgrn_in"] + k + 1)
                    a = (m * DC + k) * P
                    pe.matmul(o, w_lo[:, slot, a:a + P], x_hi[:, k, :], start=k == 0, stop=False)
                    pe.matmul(o, w_hi[:, slot, a:a + P], x_lo[:, k, :], start=False, stop=False)
                    last = pe.matmul(o, w_hi[:, slot, a:a + P], x_hi[:, k, :], start=False, stop=k == DC - 1)
                if DC - 1 in chunks:
                    last.then_inc(tile_done, 1)

            def step(hd, par, project, attend):
                a, old = hd - 1, 1 - par
                if project:
                    hgrn_tile(hd, par, 0, range(DC))
                if attend:
                    pe.wait_ge(dec_ready, a + 1)
                    for b in range(TB):
                        sl = slice(b * P, (b + 1) * P)
                        last = pe.matmul(ps[:, 2, sl], k_dec[:, old, sl], q_dec[:, old, sl], start=True, stop=True)
                    last.then_inc(a_done, 1)
                    pe.wait_ge(tile_free["act"], st.free0 + 3 * a + 3)
                    for n, src in enumerate((k_dec, hg_v)):
                        for b in range(TB):
                            sl = slice(b * P, (b + 1) * P)
                            last = pe.transpose(ps[:, 3 + n, sl], src[:, old, sl], ident)
                    last.then_inc(ht_done, 1)
                if project:
                    hgrn_tile(hd, par, 1, range(DC))
                if attend:
                    pe.wait_ge(ht_ready, a + 1)
                    pe.wait_ge(root_ready, SK["head0"] + a)
                    for c in range(7):
                        half = slice(CHUNK * (c % 2), CHUNK * (c % 2) + CHUNK)
                        last = pe.matmul(ps[:, 5 + c % 2, (c // 2) * P:(c // 2 + 1) * P], k_tok[half, c // 2, :],
                                         v_htok[half, c // 2, :], start=True, stop=True)
                    last.then_inc(kv_done, 1)
                    pe.wait_ge(a_ready, a + 1)
                    if not (isinstance(a, int) and a == 0):
                        pe.wait_ge(oh_ready, a)
                    for b in range(TB):
                        sl = slice(b * P, (b + 1) * P)
                        pe.matmul(ps[:, O_BANK, sl], v_htok[:, b, :], tmp[:, 3, sl], start=b == 0, stop=False,
                                  skip_group_check=True)
                if project:
                    hgrn_tile(hd, par, 2, range(DC - 1 if attend else DC))
                if attend:
                    pe.wait_ge(st_ready, a + 1)
                    for c in range(1, 8):
                        sl = slice(c * CHUNK, (c + 1) * CHUNK)
                        last = pe.matmul(ps[:, O_BANK, sl], state[:, c, :], q_dec[:, old, sl], start=False, stop=c == 7,
                                         skip_group_check=True)
                    last.then_inc(oh_done, 1)
                    if project:
                        hgrn_tile(hd, par, 2, (DC - 1,))
                    pe.wait_ge(sq_ready, SB["head0"] + a + 1)
                    pe.matmul(ps[:, 5, :], ones, sq[:, 0, :], start=True, stop=True).then_inc(sq_used, 1)

            pe.wait_ge(hm_ready, 48)
            read_out(st.before, st)
            step(0, 0, True, False)
            step(1, 1, True, True)
            with pe.Fori(1, HG_HEADS // 2) as i:
                step(2 * i, 0, True, True)
                step(2 * i + 1, 1, True, True)
            step(HG_HEADS, 0, False, True)
            pe.wait_ge(oh_ready, HG_HEADS)
            norm_and_ffn("h", "hgrn_out", "up_h", "down_h", FFN2_PART)

        @block.scalar
        def _(act):
            small = [(consts, const_in), (lam, lam_in), (sink, sink_in), (freq, freq_in),
                     (pos, pos_in), (iota, iota_in), (b_re, b_in[:, 0]), (b_im, b_in[:, 1]),
                     (c_re, c_in[:, 0]), (c_im, c_in[:, 1]), (mask_raw, mask_in)]
            assert len(small) == SMALL
            act.dma_start(gains[:, :], gains_in).then_inc(gains_ready, 16)
            for dst, src in small:
                dst = dst[:, :, :] if len(dst.shape) == 3 else dst[:, :]
                act.dma_start(dst, src).then_inc(small_ready, 16)

            def split_hi(st, c, i, unready=False):
                n0 = st.slab0 + c + 1
                slot, trip = n0 % 2, len(st.body)
                act.wait_ge(raw_ready[slot], 16 * (n0 // 2 + 1 + (trip // 2) * i))
                if n0 >= 2:
                    act.wait_ge(tile_done, st.tile0 + st.cum[c] + st.cum[-1] * i)
                act.activation(w_hi[:, slot, :], raw[:, slot, :], ACT.Copy).then_inc(whi_ready, 1)

            def part_hi(event, c, src, scale=1.0):
                act.activation(chunk(x_hi, c), src, ACT.Copy, scale=scale).then_inc(xhi_ready, 1)

            def square(name, c, src):
                j = SB[name] + c
                if j >= 2:
                    act.wait_ge(sq_used, j - 1)
                act.activation(sq[:, j % 2, :], src, ACT.Square).then_inc(sq_ready, 1)

            def take_root(name, n, width, e=0):
                if name in ACC:
                    act.wait_ge(acc_summed, ACC[name] + 1)
                else:
                    act.wait_ge(sq_used, SB[name] + n)
                act.wait_ge(eps_ready, 1)
                if SK[name]:
                    act.wait_ge(rstd_ready, SK_ROOT[name])
                act.activation(root[:, :], ps[:, SUM, :], ACT.Sqrt, bias=eps[:, e:e + 1], scale=1.0 / width) \
                   .then_inc(root_ready, 1)

            act.wait_ge(gains_ready, 16)
            for c in range(DC):
                if c % 4 == 0:
                    act.wait_ge(x_ready[c // 4], 16)
                part_hi("w_in", c, x_raw[:, c, :], gain("g_pre_mix", c))
            act.wait_ge(raw_ready[0], 16)
            act.activation(w_hi[:, 0, :], raw[:, 0, :], ACT.Copy).then_inc(whi_ready, 1)
            w_in = STAGES["w_in"]
            split_hi(w_in, 0, 0)
            for c in range(DC):
                square("pre_mix", c, x_raw[:, c, :])
            take_root("pre_mix", DC, D)
            act.wait_ge(small_ready, 16 * SMALL)
            act.wait_ge(turn_ready, 1)
            act.activation(par[:, PR["sin"], :], par[:, PR["r"], :], ACT.Sin)
            act.activation(par[:, PR["sin_half"], :], par[:, PR["r"], :], ACT.Sin, scale=0.5).then_inc(sines_ready, 1)

            def sin_cos(co, si, angle, unit):
                act.activation(co, angle, ACT.Abs, scale=unit)
                act.activation(si, angle, ACT.Sin, scale=unit)
                act.drain()
                return act.activation(co, co, ACT.Sin, scale=-1.0, bias=eps[:, 2:3])

            act.wait_ge(rope_ang, 1)
            sin_cos(rope_c[:, :], rope_s[:, :], tmp[:, 1, :], 1.0).then_inc(rope_ready, 1)
            act.activation(masks[:, :], mask_raw[:, :], ACT.Copy)
            act.activation(ident_b[:, :], ident, ACT.Copy).then_inc(mask_ready, 1)


            for c in range(1, 5):
                split_hi(w_in, c, 0)
                if c == 3:
                    act.wait_ge(bt_done, 1)
                    act.activation(b_lhs[:, 0, :, :].rearrange("p a c -> p (a c)"), ps[:, 2, :], ACT.Copy)
                    act.activation(b_lhs[:, 1, :, :].rearrange("p a c -> p (a c)"), ps[:, 3, :], ACT.Copy).then_inc(blhs_ready, 1)
                for pr in range(ANGLES[c - 2] if c > 1 else 0, ANGLES[c - 1] if c < 4 else N_PAIR):
                    if pr in POOL_PAIRS:
                        act.wait_ge(ang_ready["pool"], POOL_PAIRS.index(pr) + 1)
                    else:
                        act.wait_ge(ang_ready["dve"], pr - sum(other < pr for other in POOL_PAIRS) + 1)
                    sin_cos(cos_t[:, pr, :], sin_t[:, pr, :], sin_t[:, pr, :], 2 * PI_IN).then_inc(ang_used, 1)

            for i in range(4):
                act.wait_ge(pre_gelu, i + 1)
                if i >= 2:
                    act.wait_ge(xlo_ready, XB["w_glu"] + i - 1)
                act.activation(tmp[:, 2 + i % 2, :], tmp[:, i % 2, :], ACT.Gelu_apprx_tanh)
                act.drain()
                part_hi("w_glu", i, tmp[:, 2 + i % 2, :])

            act.wait_ge(vt1_done, 1)
            act.activation(v1_tok[:, :, :].rearrange("p a c -> p (a c)"), ps[:, 2, :], ACT.Copy).then_inc(vt1_ready, 1)
            with act.Fori(0, 2) as i:
                for s in range(8):
                    hh, (b, n) = s // 4, BLOCKS1[s % 4]
                    act.wait_ge(max1_ready, 8 * i + s + 1)
                    if s >= 4:
                        act.wait_ge(p1t_done, 8 * i + s - 3)
                    st_ = stat[:, s % 4, :]
                    for m in range(2):
                        act.activation(p1[:, s % 4, 2 * P * m:2 * P * m + n * P], ps[:, SCORES1[s % 4], 2 * P * m:2 * P * m + n * P],
                                       ACT.Exp, bias=st_[:, 4 + m:5 + m], scale=0.125, accum_out=st_[:, 8 + m:9 + m])
                    act.activation(st_[:, 6:8], st_[:, 6:8], ACT.Exp).then_inc(p1_ready, 1)

            st = STAGES["w_glu"]
            for c in range(2):
                split_hi(st, c, 0)
                for m in range(2):
                    j = 2 * c + m
                    act.wait_ge(tile_done, st.tile0 + 2 * j + 2)
                    if j >= 2:
                        act.wait_ge(y_ready, YB["glu"] + j - 1)
                    act.activation(tmp[:, j % 2, :], ps[:, (st.tile0 + 2 * j + 1) % 2, :], ACT.Sigmoid,
                                   bias=gain("b_glu", 4 + j)).then_inc(gate_ready, 1)

            act.wait_ge(y_ready, YB["glu"] + 4)
            act.dma_start(h[:, :, :], x_in).then_inc(h_back, 16)

            for c in range(4):
                square("ssm", c, y[:, c, :])
            take_root("ssm", 4, HALF)
            for c in range(4):
                square("attn", c, y[:, 4 + c, :])
            take_root("attn", 4, HALF)
            for c in range(DC):
                act.wait_ge(merge_ready, c + 1)
                part_hi("w_out", c, y[:, c, :])

            def rest(name, body=None):
                st = STAGES[name]

                def trip(i, last):
                    for c in range(len(st.body)):
                        if not (last and c == len(st.body) - 1):
                            split_hi(st, c, i)
                        if body:
                            body(st, c, i)

                run(act, st, trip)

            rest("w_out")
            take_root("post_mix", DC, D)
            for c in range(DC):
                act.wait_ge(y_ready, YB["res_mix"] + c + 1)
                part_hi("gate_up", c, h[:, c, :], gain("g_pre_ffn", c))
                square("pre_ffn", c, h[:, c, :])
            take_root("pre_ffn", DC, D)

            for n in range(2):

                def gated(st, c, i, n=n):
                    k = c + 2 * i
                    act.wait_ge(gate_scaled, HB[str(n)] + k + 1)
                    act.activation(tmp[:, 2, :], tmp[:, 0, :], ACT.Silu).then_inc(silu_ready, 1)
                    act.wait_ge(hid_pre, HB[str(n)] + k + 1)
                    if n == 0:
                        act.wait_ge(prod_ready, 4 * N_PAIR)
                    else:
                        act.wait_ge(tile_done, st.tile0)
                    act.activation(chunk(hid_hi, k), tmp[:, 3, :], ACT.Copy).then_inc(hid_half, 1)

                rest(f"gate_up{n}", gated)
                rest(f"down{n}")
            take_root("post_ffn", DC, D)
            for c in range(DC):
                act.wait_ge(y_ready, YB["res_ffn"] + c + 1)
                part_hi("attn_in", c, h[:, c, :])

            act.dma_start(rope_c[:, :], rope2_in[:, 0]).then_inc(rope2_ready, 16)
            act.dma_start(rope_s[:, :], rope2_in[:, 1]).then_inc(rope2_ready, 16)
            st = STAGES["attn_in"]

            def attention(p, sub, i, project, attend):
                pa = p - 1
                for j in range(10):
                    if attend and 1 <= j <= 8:
                        s = j - 1
                        for r in range(1, ROUNDS[s], 2):
                            act.wait_ge(p2t_done, TURNS[-1] * pa + TURNS[s] + r + 1)
                            nb = STEPS2[s][2] + 2 * STEPS2[s][3]
                            cols = (min(4 * r + 4, nb) - 4 * r) * P
                            act.activation(p2_t[:, 4 * r * P:4 * r * P + cols], ps[:, 5 + r % 2, 0:cols], ACT.Copy) \
                               .then_inc(p2t_act, 1)
                    if attend and j <= 7:
                        hh, b, n1, n2 = STEPS2[j]
                        act.wait_ge(max2_ready, 8 * pa + j + 1)
                        st_ = stat[:, j % 2, :]
                        act.activation(p2[:, j % 2, 0:n1 * P], ps[:, 2, 0:n1 * P], ACT.Exp, bias=st_[:, 2:3],
                                       scale=0.125, accum_out=st_[:, 4:5])
                        act.activation(p2[:, j % 2, n1 * P:(n1 + 2 * n2) * P].rearrange("p (a c) -> p a c", a=2),
                                       ps[:, 3:5, 0:n2 * P], ACT.Exp, bias=st_[:, 2:3],
                                       scale=0.125, accum_out=st_[:, 5:6]).then_inc(p2_ready, 1)
                    if project and j <= 8:
                        if j % 2 == 0:
                            c = 5 * sub + j // 2
                            n0 = st.slab0 + c + 1
                            act.wait_ge(raw_ready[n0 % 2], 16 * (n0 // 2 + 1 + 5 * i))
                            act.wait_ge(tile_done, st.tile0 + 9 * p + j)
                            act.activation(w_hi[:, n0 % 2, :], raw[:, n0 % 2, :], ACT.Copy).then_inc(whi_ready, 1)
                        act.wait_ge(tile_done, st.tile0 + 9 * p + j + 1)
                        act.activation(qkv[:, sub, j, :], ps[:, (st.tile0 + 9 * sub + j) % 2, :], ACT.Copy) \
                           .then_inc(tile_free["act"], 1)
                    if project and j >= 1 and (j - 1) % 3 == 2:
                        act.wait_ge(swap_done, 9 * p + j)
                        act.activation(v_tok[:, sub, (j - 1) // 3, :, :].rearrange("p a c -> p (a c)"), ps[:, 7, :],
                                       ACT.Copy).then_inc(vtok_ready, 1)

            attention(0, 0, 0, True, False)
            with act.Fori(0, HEAD_PAIRS // 2 - 1) as i:
                attention(2 * i + 1, 1, i, True, True)
                attention(2 * i + 2, 0, i + 1, True, True)
            attention(HEAD_PAIRS - 1, 1, HEAD_PAIRS // 2 - 1, True, True)
            attention(HEAD_PAIRS, 0, 0, False, True)
            for c in range(DC):
                act.wait_ge(o2t_done, c + 1)
                part_hi("attn_out", c, ps[:, 5 + c % 2, :])

            def hidden(key):

                def body(st, c, i):
                    for m in range(2):
                        t = 2 * c + m
                        k = t + 4 * i
                        act.wait_ge(tile_done, st.tile0 + t + 4 * i + 1)
                        act.wait_ge(hid_ready, HB[key] + k - 1)
                        act.activation(tmp[:, t % 2, :], ps[:, (st.tile0 + t) % 2, :], ACT.Relu).then_inc(tile_free["act"], 1)
                        act.drain()
                        act.activation(chunk(hid_hi, k), tmp[:, t % 2, :], ACT.Square).then_inc(hid_half, 1)

                return body

            def layer_norm(layer, part):
                act.wait_ge(acc_summed, ACC[f"mean_{part}_{layer}"] + 1)
                act.activation(root[:, :], ps[:, SUM, :], ACT.Copy, scale=1.0 / D).then_inc(root_ready, 1)
                for c in range(DC):
                    act.wait_ge(y_ready, YB[f"mid_{part}_{layer}"] + c + 1)
                    square(f"var_{part}_{layer}", c, y[:, c, :])
                take_root(f"var_{part}_{layer}", DC, D, 1)

            def normed(layer, part, n, after):
                for c in range(DC):
                    act.wait_ge(y_ready, YB[f"res_{part}_{layer}"] + c + 1)
                    g, b = gain(f"ln_{part}_g{n}", c), gain(f"ln_{part}_b{n}", c)
                    last = act.activation(h[:, c, :], y[:, c, :], ACT.Identity, scale=g, bias=b)
                    if after:
                        act.activation(x_hi[:, c, :], y[:, c, :], ACT.Identity, scale=g, bias=b).then_inc(xhi_ready, 1)
                    else:
                        last.then_inc(result_ready, 1)

            def norm_and_ffn(layer, proj, up, down, n, after):
                rest(proj)
                layer_norm(layer, "mix")
                normed(layer, "mix", n, up)
                for m in range(2):
                    rest(f"{up}{m}", hidden(f"{layer}{m}"))
                    rest(f"{down}{m}")
                layer_norm(layer, "ffn")
                normed(layer, "ffn", n, after)

            norm_and_ffn("a", "attn_out", "up_a", "down_a", 0, "hgrn_in")

            for n, dst in enumerate((a_mask, run_mask, start_mask)):
                act.dma_start(dst[:, :], hmask_in[:, n]).then_inc(hm_ready, 16)
            act.wait_ge(lb_half, 1)
            act.activation(lbp[:, 2:4, :].rearrange("p a c -> p (a c)"), lbp[:, 2:4, :].rearrange("p a c -> p (a c)"),
                           ACT.Exp).then_inc(lb_exp, 1)

            st = STAGES["hgrn_in"]

            def split_next(hd, par, i, n):
                c = 2 * par + n + 1
                slot, width = (st.slab0 + c) % 2, SLAB // 2 if n == 0 else SLAB
                act.wait_ge(raw_ready[slot], 16 * ((st.slab0 + c) // 2 + 1 + 2 * i))
                act.wait_ge(tile_done, st.tile0 + 3 * hd + 2 * n)
                act.activation(w_hi[:, slot, 0:width], raw[:, slot, 0:width], ACT.Copy).then_inc(whi_ready, 1)

            def step(hd, par, i, project, attend):
                a = hd - 1
                banks = [ps[:, (st.tile0 + 3 * par + j) % 2, :] for j in range(3)]
                if project:
                    split_next(hd, par, i, 0)
                    act.wait_ge(tile_done, st.tile0 + 3 * hd + 1)
                    if not (isinstance(hd, int) and hd < 2):
                        act.wait_ge(dec_ready, hd - 1)
                    act.activation(hg_q[:, par, :], banks[0], ACT.Silu).then_inc(tile_free["act"], 1)
                if attend:
                    act.wait_ge(ht_done, a + 1)
                    act.activation(k_tok[:, :, :].rearrange("p a c -> p (a c)"), ps[:, 3, :], ACT.Copy)
                    act.activation(v_htok[:, :, :].rearrange("p a c -> p (a c)"), ps[:, 4, :], ACT.Copy) \
                       .then_inc(ht_ready, 1)
                if project:
                    act.wait_ge(tile_done, st.tile0 + 3 * hd + 2)
                    act.activation(hg_s[:, par, :], banks[1], ACT.Sigmoid)
                    act.activation(hg_k[:, par, :], banks[1], ACT.Sigmoid, scale=-1.0).then_inc(tile_free["act"], 1)
                    split_next(hd, par, i, 1)
                if attend:
                    act.wait_ge(oh_done, a + 1)
                    act.activation(sq[:, 0, :], ps[:, SUM, :], ACT.Square).then_inc(sq_ready, 1)
                if project:
                    act.wait_ge(tile_done, st.tile0 + 3 * hd + 3)
                    act.activation(hg_v[:, par, :], banks[2], ACT.Copy).then_inc(tile_free["act"], 1)
                if attend:
                    act.wait_ge(sq_used, SB["head0"] + a + 1)
                    act.wait_ge(rstd_ready, SK_ROOT["head0"] + a)
                    act.activation(root[:, :], ps[:, 5, :], ACT.Sqrt, bias=eps[:, 0:1], scale=1.0 / P) \
                       .then_inc(root_ready, 1)

            def head_hi(hd):
                act.wait_ge(oh_ready, hd + 1)
                part_hi("hgrn_out", hd, hg_o[:, hd, :])

            step(0, 0, 0, True, False)
            step(1, 1, 0, True, True)
            with act.Fori(1, HG_HEADS // 2) as i:
                step(2 * i, 0, i, True, True)
                step(2 * i + 1, 1, i, True, True)
            act.wait_ge(tile_done, STAGES["hgrn_out"].tile0)
            for hd in range(6):
                head_hi(hd)
            step(HG_HEADS, 0, 0, False, True)
            for hd in range(6, HG_HEADS):
                head_hi(hd)
            norm_and_ffn("h", "hgrn_out", "up_h", "down_h", 1, None)

        @block.vector
        def _(dve):
            tt, ts, stt, settle = dve.tensor_tensor, dve.tensor_scalar, dve.scalar_tensor_tensor, dve.drain

            def split_lo(st, c, i):
                n0 = st.slab0 + c + 1
                slot = n0 % 2
                dve.wait_ge(whi_ready, n0 + 1 + len(st.body) * i)
                tt(w_lo[:, slot, :], raw[:, slot, :], w_hi[:, slot, :].bitcast(f32), ALU.subtract).then_inc(wlo_ready, 1)

            def part_lo(event, c, src):
                dve.wait_ge(xhi_ready, XB[event] + c + 1)
                tt(chunk(x_lo, c), src, chunk(x_hi, c).bitcast(f32), ALU.subtract).then_inc(xlo_ready, 1)

            def part_lo_gain(event, c, src, scale):
                dve.wait_ge(xhi_ready, XB[event] + c + 1)
                stt(x_lo[:, c, :], src, scale, x_hi[:, c, :].bitcast(f32), ALU.mult, ALU.subtract).then_inc(xlo_ready, 1)

            def invert(name):
                dve.wait_ge(root_ready, SK[name] + 1)
                dve.reciprocal(rstd[:, :], root[:, :]).then_inc(rstd_ready, 1)
                settle()

            for n, value in enumerate((RMS_EPS, LN_EPS, np.pi / 2)):
                last = dve.memset(eps[:, n:n + 1], float(value))
            last.then_inc(eps_ready, 1)
            dve.wait_ge(gains_ready, 16)
            for c in range(DC):
                part_lo_gain("w_in", c, x_raw[:, c, :], gain("g_pre_mix", c))
            dve.wait_ge(whi_ready, 1)
            tt(w_lo[:, 0, :], raw[:, 0, :], w_hi[:, 0, :].bitcast(f32), ALU.subtract).then_inc(wlo_ready, 1)
            split_lo(STAGES["w_in"], 0, 0)
            dve.wait_ge(small_ready, 16 * SMALL)

            def col(name):
                return par[:, PR[name], :]

            def exp_parts(z):
                ts(col("z"), z, -87.0, 88.0, ALU.max, ALU.min)
                settle()
                ts(col("k"), col("z"), float(1 / np.log(2.0)), ROUND, ALU.mult, ALU.add)
                settle()
                ts(col("k"), col("k"), ROUND, None, ALU.subtract)
                settle()
                stt(col("f"), col("k"), -LN2_HI, col("z"), ALU.mult, ALU.add)
                settle()
                stt(col("f"), col("k"), -LN2_LO, col("f"), ALU.mult, ALU.add)
                ts(col("two_k").bitcast(i32), col("k"), 127.0, 2.0 ** 23, ALU.add, ALU.mult)
                settle()
                ts(col("e"), col("f"), 1 / 5040.0, None, ALU.mult)
                for factor in (720.0, 120.0, 24.0, 6.0, 2.0, 1.0):
                    settle()
                    stt(col("e"), col("e"), 1 / factor, col("f"), ALU.add, ALU.mult)
                settle()

            def reduce_turns(angle, k, by):
                stt(angle, k, -PI_HI, angle, ALU.mult, ALU.add)
                settle()
                stt(angle, k, -PI_LO, angle, ALU.mult, ALU.add)
                settle()

            li = lam[:, 1, :]
            ts(col("lr"), lam[:, 0, :], -1e-4, None, ALU.min)
            exp_parts(lam[:, 2, :])
            stt(col("dt"), col("e"), 1.0, col("two_k"), ALU.add, ALU.mult)
            settle()
            tt(col("t0"), col("lr"), col("dt"), ALU.mult)
            tt(col("th"), li, col("dt"), ALU.mult)
            settle()
            exp_parts(col("t0"))
            tt(col("t0"), col("two_k"), col("e"), ALU.mult)
            settle()
            stt(col("em1"), col("two_k"), -1.0, col("t0"), ALU.add, ALU.add)
            ts(col("k"), col("th"), float(1 / TWO_PI), ROUND, ALU.mult, ALU.add)
            settle()
            ts(col("mag"), col("em1"), 1.0, None, ALU.add)
            ts(col("k"), col("k"), ROUND, None, ALU.subtract)
            dve.tensor_copy(col("r"), col("th"))
            settle()
            reduce_turns(col("r"), col("k"), 0)
            ts(col("r"), col("r"), PI_IN, -PI_IN, ALU.min, ALU.max)
            settle()
            ts(col("r_turn"), col("r"), float(1 / TWO_PI), None, ALU.mult).then_inc(turn_ready, 1)
            settle()
            ts(col("t1"), col("r_turn"), 65536.0, ROUND, ALU.mult, ALU.add)
            dve.tensor_copy(col("r_lo"), col("r"))
            settle()
            ts(col("r_hi"), col("t1"), ROUND, 1 / 65536.0, ALU.subtract, ALU.mult)
            settle()
            reduce_turns(col("r_lo"), col("r_hi"), 0)
            ts(col("r_lo"), col("r_lo"), float(1 / TWO_PI), None, ALU.mult).then_inc(turn_ready, 1)
            dve.tensor_copy(tmp[:, 1, :], pos[:, :])
            settle()
            ts(tmp[:, 1, :], tmp[:, 1, :], freq[:, 0:1], None, ALU.mult)
            settle()
            ts(tmp[:, 0, :], tmp[:, 1, :], float(1 / TWO_PI), ROUND, ALU.mult, ALU.add)
            settle()
            ts(tmp[:, 0, :], tmp[:, 0, :], ROUND, None, ALU.subtract)
            settle()
            reduce_turns(tmp[:, 1, :], tmp[:, 0, :], 0)
            ts(tmp[:, 1, :], tmp[:, 1, :], PI_IN, -PI_IN, ALU.min, ALU.max).then_inc(rope_ang, 1)

            def input_matrix():
                dve.wait_ge(sines_ready, 1)
                tt(col("c1"), col("sin_half"), col("sin_half"), ALU.mult)
                tt(col("ai"), col("mag"), col("sin"), ALU.mult)
                settle()
                stt(col("c1"), col("c1"), -2.0, col("mag"), ALU.mult, ALU.mult)
                settle()
                tt(col("am1"), col("c1"), col("em1"), ALU.add)
                tt(col("den"), col("lr"), col("lr"), ALU.mult)
                tt(col("t0"), li, li, ALU.mult)
                settle()
                tt(col("den"), col("den"), col("t0"), ALU.add)
                tt(col("nr"), col("am1"), col("lr"), ALU.mult)
                tt(col("t1"), col("ai"), li, ALU.mult)
                settle()
                dve.reciprocal(col("den"), col("den"))
                tt(col("nr"), col("nr"), col("t1"), ALU.add)
                tt(col("ni"), col("ai"), col("lr"), ALU.mult)
                tt(col("t0"), col("am1"), li, ALU.mult)
                settle()
                tt(col("ni"), col("ni"), col("t0"), ALU.subtract)
                settle()
                tt(col("fr"), col("nr"), col("den"), ALU.mult)
                tt(col("fi"), col("ni"), col("den"), ALU.mult)
                settle()
                fr = col("fr").unsqueeze(2).to_broadcast([P, N_PAIR, GW])
                fi = col("fi").unsqueeze(2).to_broadcast([P, N_PAIR, GW])
                scratch = tmp[:, 0, :].rearrange("p (a c) -> p a c", a=N_PAIR)
                for dst, first, second, op in ((bb_re, b_re, b_im, ALU.subtract), (bb_im, b_im, b_re, ALU.add)):
                    tt(dst[:, :, :], fr, first[:, :, :], ALU.mult)
                    tt(tmp[:, 2, :].rearrange("p (a c) -> p a c", a=N_PAIR), fi, second[:, :, :], ALU.mult)
                    settle()
                    last = tt(dst[:, :, :], dst[:, :, :], tmp[:, 2, :].rearrange("p (a c) -> p a c", a=N_PAIR), op)
                    settle()
                last.then_inc(bb_ready, 1)

            def angles(first, last):
                for pr in [pr for pr in range(first, last) if pr not in POOL_PAIRS]:
                    ang, k = sin_t[:, pr, :], cos_t[:, pr, :]
                    if pr == 13:
                        dve.wait_ge(bt_done, 1)
                    ts(ang, iota[:, :], par[:, PR["r_hi"], pr:pr + 1], None, ALU.mult)
                    ts(k, iota[:, :], par[:, PR["r_turn"], pr:pr + 1], ROUND, ALU.mult, ALU.add)
                    settle()
                    stt(k, k, ROUND, ang, ALU.subtract, ALU.subtract)
                    settle()
                    stt(ang, iota[:, :], par[:, PR["r_lo"], pr:pr + 1], k, ALU.mult, ALU.subtract)
                    settle()
                    ts(ang, ang, 0.5, -0.5, ALU.min, ALU.max).then_inc(ang_ready["dve"], 1)

            angles(0, ANGLES[0])
            invert("pre_mix")
            st = STAGES["w_in"]
            places = [u[:, c, :] for c in range(4)] + [q1[:, c, :] for c in range(4)] + [k1[:, :], v1[:, :]]
            dve.wait_ge(mask_ready, 1)
            dve.wait_ge(sq_used, DC)
            for c in range(5):
                if c:
                    split_lo(st, c, 0)
                for m in range(2):
                    t = 2 * c + m
                    dve.wait_ge(tile_done, t + 1)
                    tt(places[t], ps[:, t % 2, :], rstd[:, :], ALU.mult).then_inc(tile_free["dve"], 1)
                if c == 0:
                    input_matrix()
                else:
                    angles(ANGLES[c - 1], ANGLES[c])
            ts(c_neg[:, :, :], c_re[:, :, :], -1.0, None, ALU.mult)
            ts(c_im[:, :, :], c_im[:, :, :], -1.0, None, ALU.mult)
            settle()

            for pr in range(N_PAIR):
                i, q = divmod(pr, 4)
                dve.wait_ge(ang_used, pr + 1)
                dve.wait_ge(bu_done, pr + 1)
                re, im = ps[:, 2 + 2 * (pr % 2), :], ps[:, 3 + 2 * (pr % 2), :]
                mag = par[:, PR["mag"], pr:pr + 1].to_broadcast([P, T])
                settle()
                tt(mod[:, 0, :], re, cos_t[:, pr, :], ALU.mult)
                tt(mod[:, 1, :], im, sin_t[:, pr, :], ALU.mult)
                settle()
                tt(mod[:, 0, :], mod[:, 0, :], mod[:, 1, :], ALU.add)
                settle()
                if pr:
                    dve.wait_ge(prod_ready, 4 * pr - 2)
                dve.tensor_tensor_scan(scan[:, 0, :], mag, mod[:, 0, :], 0.0, ALU.mult, ALU.add).then_inc(scan_ready, 1)
                tt(mod[:, 2, :], im, cos_t[:, pr, :], ALU.mult)
                tt(mod[:, 3, :], re, sin_t[:, pr, :], ALU.mult).then_inc(bu_free, 1)
                settle()
                tt(mod[:, 2, :], mod[:, 2, :], mod[:, 3, :], ALU.subtract)
                settle()
                if pr:
                    dve.wait_ge(prod_ready, 4 * pr)
                dve.tensor_tensor_scan(scan[:, 1, :], mag, mod[:, 2, :], 0.0, ALU.mult, ALU.add).then_inc(scan_ready, 1)
                if (q == 0 and i) or pr == N_PAIR - 1:
                    done = [i - 1] if q == 0 else [i]
                    for c in done:
                        dve.wait_ge(yssm_done, 16 * c + 16)
                        if c >= 2:
                            dve.wait_ge(xlo_ready, XB["w_glu"] + c - 1)
                        stt(tmp[:, c % 2, :], u[:, c, :], gain("d", c), ps[:, 6, :], ALU.mult, ALU.add).then_inc(pre_gelu, 1)
                        part_lo("w_glu", c, tmp[:, 2 + c % 2, :])

            dve.wait_ge(kr1_swap, 1)
            tt(tmp[:, 0, :], ps[:, 3, :], rope_s[:, :], ALU.mult)
            tt(k1[:, :], k1[:, :], rope_c[:, :], ALU.mult)
            settle()
            tt(k1[:, :], k1[:, :], tmp[:, 0, :], ALU.add).then_inc(kr1_ready, 1)
            with dve.Fori(0, 2) as i:
                for m in range(2):
                    dve.wait_ge(qr1_swap, 2 * i + m + 1)
                    tt(tmp[:, m, :], ps[:, (2, SUM)[m], :], rope_s[:, :], ALU.mult)
                    tt(qr1[:, m, :], chunk(q1, 2 * i + m), rope_c[:, :], ALU.mult)
                    settle()
                    tt(qr1[:, m, :], qr1[:, m, :], tmp[:, m, :], ALU.add).then_inc(qr1_ready, 1)

                def maximum1(s):
                    hh, (b, n) = s // 4, BLOCKS1[s % 4]
                    st_ = stat[:, s % 4, :]
                    sinks = sink[:, ds(4 * i + 2 * hh, 2)]
                    dve.wait_ge(s1_done, 8 * i + s + 1)
                    scores = ps[:, SCORES1[s % 4], :].rearrange("p (m k) -> p m k", m=2)[:, :, 0:n * P]
                    dve.tensor_reduce(st_[:, 0:2], scores, AX.X, ALU.max)
                    settle()
                    stt(st_[:, 2:4], st_[:, 0:2], 0.125, sinks, ALU.mult, ALU.max)
                    settle()
                    ts(st_[:, 4:6], st_[:, 2:4], -1.0, None, ALU.mult)
                    tt(st_[:, 6:8], sinks, st_[:, 2:4], ALU.subtract).then_inc(max1_ready, 1)

                def scale1(s):
                    hh, (b, n) = s // 4, BLOCKS1[s % 4]
                    st_ = stat[:, s % 4, :]
                    tt(st_[:, 10:12], st_[:, 6:8], st_[:, 8:10], ALU.add)
                    settle()
                    dve.reciprocal(st_[:, 12:14], st_[:, 10:12])
                    settle()
                    dve.wait_ge(o1_done, 8 * i + s + 1)
                    for m in range(2):
                        last = ts(o1_tok[:, b, ds(256 * i + 128 * m + 64 * hh, 64)],
                                  ps[:, (6, 2)[s % 2], 64 * m:64 * m + 64], st_[:, 12 + m:13 + m], None, ALU.mult)
                    last.then_inc(o1_ready, 1)

                maximum1(0)
                maximum1(1)
                for s in range(8):
                    n = BLOCKS1[s % 4][1]
                    dve.wait_ge(p1t_done, 8 * i + s + 1)
                    dve.tensor_copy(p1_t[:, s % 2, 0:2 * n * P], ps[:, (5, SUM)[s % 2], 0:2 * n * P]) \
                        .then_inc(p1t_ready, 1)
                    if s < 6:
                        maximum1(s + 2)
                    if s:
                        scale1(s - 1)
                scale1(7)
            for c in range(4):
                dve.wait_ge(o1t_done, c + 1)
                dve.tensor_copy(y[:, 4 + c, :], ps[:, 4 + c % 2, :]).then_inc(y_ready, 1)

            st = STAGES["w_glu"]
            for c in range(2):
                split_lo(st, c, 0)
                for m in range(2):
                    j = 2 * c + m
                    dve.wait_ge(gate_ready, j + 1)
                    stt(y[:, j, :], ps[:, (st.tile0 + 2 * j) % 2, :], gain("b_glu", j), tmp[:, j % 2, :],
                        ALU.add, ALU.mult).then_inc(tile_free["dve"], 2)
                    settle()
                    dve.sem_inc(y_ready, 1)

            invert("ssm")
            for c in range(DC):
                if c == 4:
                    invert("attn")
                stt(y[:, c, :], y[:, c, :], gain("g_ssm", c) if c < 4 else gain("g_attn", c - 4), rstd[:, :],
                    ALU.mult, ALU.mult).then_inc(merge_ready, 1)
                settle()
                part_lo("w_out", c, y[:, c, :])

            def rest(name, body):
                st = STAGES[name]

                def trip(i, last):
                    for c in range(len(st.body)):
                        if not (last and c == len(st.body) - 1):
                            split_lo(st, c, i)
                        body(st, c, i)

                run(dve, st, trip)

            def tiles(put):

                def body(st, c, i):
                    for m in range(st.body[c]):
                        t = st.cum[c] + m
                        dve.wait_ge(tile_done, st.tile0 + t + st.cum[-1] * i + 1)
                        put(t + st.cum[-1] * i, ps[:, (st.tile0 + t) % 2, :])

                return body

            def keep(t, bank):
                ts(chunk(y, t), bank, 1.0, None, ALU.mult).then_inc(tile_free["dve"], 1)

            def keep_and_tell(t, bank):
                ts(chunk(y, t), bank, 1.0, None, ALU.mult).then_inc(tile_free["dve"], 1)
                settle()
                dve.sem_inc(y_ready, 1)

            def add_and_tell(t, bank):
                tt(chunk(y, t), bank, chunk(y, t), ALU.add).then_inc(tile_free["dve"], 1)
                settle()
                dve.sem_inc(y_ready, 1)

            def residual(t, bank):
                stt(chunk(y, t), chunk(h, t), ALPHA, bank, ALU.mult, ALU.add).then_inc(tile_free["dve"], 1)

            def residual_and_tell(t, bank):
                residual(t, bank)
                settle()
                dve.sem_inc(y_ready, 1)

            def post_norm(name, g, after, event):
                invert(name)
                for c in range(DC):
                    stt(y[:, c, :], y[:, c, :], gain(g, c), rstd[:, :], ALU.mult, ALU.mult)
                    settle()
                    tt(h[:, c, :], h[:, c, :], y[:, c, :], ALU.add).then_inc(y_ready, 1)
                    if c:
                        after(c - 1)
                settle()
                after(DC - 1)

            rest("w_out", tiles(keep_and_tell))
            dve.wait_ge(h_back, 16)
            post_norm("post_mix", "g_post_mix",
                      lambda c: part_lo_gain("gate_up", c, h[:, c, :], gain("g_pre_ffn", c)), "res_mix")

            invert("pre_ffn")
            for n in range(2):

                def gated(st, c, i, n=n):
                    k = c + 2 * i
                    for m in range(2):
                        t = 2 * c + m
                        dve.wait_ge(tile_done, st.tile0 + t + 4 * i + 1)
                        scaled = tt(tmp[:, m, :], ps[:, (st.tile0 + t) % 2, :], rstd[:, :], ALU.mult)
                        scaled.then_inc(tile_free["dve"], 1)
                        settle()
                        if m == 0:
                            dve.sem_inc(gate_scaled, 1)
                    dve.wait_ge(silu_ready, HB[str(n)] + k + 1)
                    tt(tmp[:, 3, :], tmp[:, 2, :], tmp[:, 1, :], ALU.mult).then_inc(hid_pre, 1)
                    settle()
                    dve.wait_ge(hid_half, HB[str(n)] + k + 1)
                    tt(chunk(hid_lo, k), tmp[:, 3, :], chunk(hid_hi, k).bitcast(f32), ALU.subtract).then_inc(hid_ready, 1)

                rest(f"gate_up{n}", gated)
                rest(f"down{n}", tiles(keep if n == 0 else add_and_tell))
            post_norm("post_ffn", "g_post_ffn", lambda c: part_lo("attn_in", c, h[:, c, :]), "res_ffn")

            dve.wait_ge(rope2_ready, 32)
            st = STAGES["attn_in"]

            def attention(p, sub, i, project, attend):
                pa = p - 1
                for j in range(10):
                    s = j - 1
                    if attend and 1 <= j <= 8:
                        hh, b, n1, n2 = STEPS2[s]
                        nb = n1 + 2 * n2
                        for r in range(0, ROUNDS[s], 2):
                            dve.wait_ge(p2t_done, TURNS[-1] * pa + TURNS[s] + r + 1)
                            cols = (min(4 * r + 4, nb) - 4 * r) * P
                            dve.tensor_copy(p2_t[:, 4 * r * P:4 * r * P + cols], ps[:, 5 + r % 2, 0:cols]) \
                               .then_inc(p2t_dve, 1)
                    if attend and j <= 7:
                        hh, b, n1, n2 = STEPS2[j]
                        st_ = stat[:, j % 2, :]
                        dve.wait_ge(s2_done, 8 * pa + j + 1)
                        dve.tensor_reduce(st_[:, 0:1], ps[:, 2, 0:n1 * P], AX.X, ALU.max)
                        dve.tensor_reduce(st_[:, 1:2], ps[:, 3:5, 0:n2 * P], AX.XY, ALU.max)
                        settle()
                        ts(st_[:, 2:3], st_[:, 0:1], st_[:, 1:2], -0.125, ALU.max, ALU.mult).then_inc(max2_ready, 1)
                    if attend and 1 <= j <= 8:
                        st_ = stat[:, s % 2, :]
                        dve.wait_ge(p2_ready, 8 * pa + s + 1)
                        tt(st_[:, 6:7], st_[:, 4:5], st_[:, 5:6], ALU.add)
                        settle()
                        dve.reciprocal(st_[:, 7:8], st_[:, 6:7])
                        settle()
                        dve.wait_ge(o2_done, 8 * pa + s + 1)
                        first = 128 * pa + 64 * hh if False else 128 * pa + 64 * STEPS2[s][0]
                        place = o2_tok[:, STEPS2[s][1], ds(first, 64)]
                        ts(place, ps[:, 7, 0:64], st_[:, 7:8], None, ALU.mult).then_inc(o2_ready, 1)
                    if project and j <= 8 and j % 2 == 0:
                        c = 5 * sub + j // 2
                        n0 = st.slab0 + c + 1
                        dve.wait_ge(whi_ready, st.slab0 + 5 * p + j // 2 + 2)
                        tt(w_lo[:, n0 % 2, :], raw[:, n0 % 2, :], w_hi[:, n0 % 2, :].bitcast(f32), ALU.subtract) \
                            .then_inc(wlo_ready, 1)
                    if project and j >= 1 and (j - 1) % 3 != 2:
                        dve.wait_ge(swap_done, 9 * p + j)
                        tile = qkv[:, sub, j - 1, :]
                        tt(tmp[:, 0, :], ps[:, 7, :], rope_s[:, :], ALU.mult)
                        tt(tile, tile, rope_c[:, :], ALU.mult)
                        settle()
                        tt(tile, tile, tmp[:, 0, :], ALU.add).then_inc(rot_ready, 1)
                        settle()

            attention(0, 0, 0, True, False)
            with dve.Fori(0, HEAD_PAIRS // 2 - 1) as i:
                attention(2 * i + 1, 1, i, True, True)
                attention(2 * i + 2, 0, i + 1, True, True)
            attention(HEAD_PAIRS - 1, 1, 0, True, True)
            attention(HEAD_PAIRS, 0, 0, False, True)
            for c in range(DC):
                part_lo("attn_out", c, ps[:, 5 + c % 2, :])

            def hidden(key):
                def body(st, c, i):
                    for m in range(2):
                        t = 2 * c + m
                        k = t + 4 * i
                        dve.wait_ge(hid_half, HB[key] + k + 1)
                        tt(tmp[:, 2 + t % 2, :], tmp[:, t % 2, :], tmp[:, t % 2, :], ALU.mult)
                        settle()
                        tt(chunk(hid_lo, k), tmp[:, 2 + t % 2, :], chunk(hid_hi, k).bitcast(f32), ALU.subtract) \
                            .then_inc(hid_ready, 1)

                return body

            def layer_norm(layer, part, n, after):
                dve.wait_ge(root_ready, SK[f"mean_{part}_{layer}"] + 1)
                for c in range(DC):
                    tt(y[:, c, :], y[:, c, :], root[:, :], ALU.subtract).then_inc(y_ready, 1)
                settle()
                invert(f"var_{part}_{layer}")
                for c in range(DC):
                    tt(y[:, c, :], y[:, c, :], rstd[:, :], ALU.mult).then_inc(y_ready, 1)
                    if after and c:
                        part_lo(after, c - 1, h[:, c - 1, :])
                if after:
                    part_lo(after, DC - 1, h[:, DC - 1, :])

            def norm_and_ffn(layer, proj, up, down, n, after):
                rest(proj, tiles(residual_and_tell))
                layer_norm(layer, "mix", n, up)
                rest(f"{up}0", hidden(f"{layer}0"))
                rest(f"{down}0", tiles(residual))
                rest(f"{up}1", hidden(f"{layer}1"))
                rest(f"{down}1", tiles(add_and_tell))
                layer_norm(layer, "ffn", n, after)

            norm_and_ffn("a", "attn_out", "up_a", "down_a", 0, "hgrn_in")

            a0, b0 = GAIN_AT["lb0"], GAIN_AT["lb1"]
            l0, l1 = gains[:, a0:a0 + HG_HEADS], gains[:, b0:b0 + HG_HEADS]
            tt(lbp[:, 4, :], l0, l1, ALU.max)
            settle()
            tt(lbp[:, 2, :], l0, lbp[:, 4, :], ALU.subtract)
            tt(lbp[:, 3, :], l1, lbp[:, 4, :], ALU.subtract).then_inc(lb_half, 1)
            dve.wait_ge(lb_exp, 1)
            tt(lbp[:, 4, :], lbp[:, 2, :], lbp[:, 3, :], ALU.add)
            settle()
            dve.reciprocal(lbp[:, 5, :], lbp[:, 4, :])
            settle()
            tt(lbp[:, 0, :], lbp[:, 3, :], lbp[:, 5, :], ALU.mult)
            tt(lbp[:, 1, :], lbp[:, 2, :], lbp[:, 5, :], ALU.mult)
            settle()
            dve.wait_ge(hm_ready, 48)
            st = STAGES["hgrn_in"]

            def split_next(hd, par, n):
                slot, width = (st.slab0 + 2 * par + n + 1) % 2, SLAB // 2 if n == 0 else SLAB
                dve.wait_ge(whi_ready, st.slab0 + 2 * hd + n + 2)
                tt(w_lo[:, slot, 0:width], raw[:, slot, 0:width], w_hi[:, slot, 0:width].bitcast(f32), ALU.subtract) \
                    .then_inc(wlo_ready, 1)

            def step(hd, par, project, attend):
                a, old = hd - 1, 1 - par
                if project:
                    split_next(hd, par, 0)
                if attend:
                    dve.wait_ge(a_done, a + 1)
                    tt(tmp[:, 3, :], ps[:, 2, :], a_mask[:, :], ALU.mult).then_inc(a_ready, 1)
                    dve.wait_ge(kv_done, a + 1)
                    for c in range(7):
                        kv = ps[:, 5 + c % 2, (c // 2) * P:(c // 2 + 1) * P]
                        decay = f_cum[:, old, CHUNK * c + CHUNK - 1:CHUNK * c + CHUNK]
                        if c:
                            tt(state[:, c + 1, :], kv, state[:, c, :], ALU.add)
                            settle()
                        last = ts(state[:, c + 1, :], state[:, c + 1, :] if c else kv, decay, None, ALU.mult)
                        if c < 6:
                            settle()
                    last.then_inc(st_ready, 1)
                if project:
                    split_next(hd, par, 1)
                    lb, rest_ = lbp[:, 0, ds(hd, 1)], lbp[:, 1, ds(hd, 1)]
                    dve.wait_ge(tile_free["act"], st.free0 + 3 * hd + 2)
                    ts(tmp[:, 0, :], hg_s[:, par, :], rest_, lb, ALU.mult, ALU.add)
                    settle()
                    tt(f_run[:, :], tmp[:, 0, :], run_mask[:, :], ALU.mult)
                    tt(f_start[:, :], tmp[:, 0, :], start_mask[:, :], ALU.mult)
                    settle()
                    dve.tensor_tensor_scan(f_cum[:, par, :], f_run[:, :], f_start[:, :], 0.0, ALU.mult, ALU.add)
                    settle()
                    dve.reciprocal(f_run[:, :], f_cum[:, par, :])
                    tt(q_dec[:, par, :], hg_q[:, par, :], f_cum[:, par, :], ALU.mult)
                    settle()
                    stt(k_dec[:, par, :], hg_k[:, par, :], rest_, f_run[:, :], ALU.mult, ALU.mult).then_inc(dec_ready, 1)
                if attend:
                    dve.wait_ge(root_ready, SK["head0"] + a + 1)
                    dve.reciprocal(rstd[:, :], root[:, :]).then_inc(rstd_ready, 1)
                    settle()
                    stt(chunk(hg_o, a), ps[:, SUM, :], gains[:, ds(GAIN_AT["g_hgrn"] + a, 1)], rstd[:, :], ALU.mult,
                        ALU.mult).then_inc(oh_ready, 1)

            step(0, 0, True, False)
            step(1, 1, True, True)
            with dve.Fori(1, HG_HEADS // 2) as i:
                step(2 * i, 0, True, True)
                step(2 * i + 1, 1, True, True)
            settle()
            for hd in range(6):
                part_lo("hgrn_out", hd, hg_o[:, hd, :])
            step(HG_HEADS, 0, False, True)
            settle()
            for hd in range(6, HG_HEADS):
                part_lo("hgrn_out", hd, hg_o[:, hd, :])
            norm_and_ffn("h", "hgrn_out", "up_h", "down_h", 1, None)


def slabs(weight, kc, order, per, width=None):
    k, n = weight.shape
    tiles = weight.reshape(kc, P, n // P, P).transpose(2, 1, 0, 3)[order]
    tiles = tiles.reshape(len(order) // per, per, P, kc, P).transpose(0, 2, 1, 3, 4)
    return np.ascontiguousarray(tiles.reshape(len(order) // per, P, per * kc * P))


def columns(vector):
    return np.asarray(vector, np.float32).reshape(-1, P).T


def swap_matrix(period, half):
    m = np.zeros((P, P), np.float32)
    for f in range(P):
        d = f % period
        if d < half:
            m[f + half, f] = -1.0
        elif d < 2 * half:
            m[f - half, f] = 1.0
    return m


def shape_constants():
    i, j = np.arange(P)[:, None], np.arange(P)[None, :]

    def mask(valid):
        return np.where(valid, 0.0, NEG).astype(np.float32)

    parts = [mask(j > i), mask(j <= i), mask(j >= i), mask(j <= i)]
    for dilation in (4, 16):
        same = (i - j) % dilation == 0
        parts += [mask(same)] * 3 + [mask(same & (j <= i))]
    const = np.stack([np.eye(P), swap_matrix(64, 8), swap_matrix(64, 32), np.ones((P, P))], 1).astype(np.float32)
    t = np.arange(T, dtype=np.float32)
    d = np.arange(P) % 64
    inv1 = (np.float32(500000.0) ** (-np.arange(8, dtype=np.float32) * np.float32(2.0) / np.float32(16))).astype(np.float32)
    freq = np.where(d < 16, inv1[d % 8], 0.0).astype(np.float32)[:, None]
    inv2 = (np.float32(10000.0) ** (-np.arange(32, dtype=np.float32) * np.float32(2.0 / 64))).astype(np.float32)
    angle = (t[None, :] * inv2[np.arange(P) % 32][:, None]).astype(np.float32)
    rope2 = np.stack([np.cos(angle), np.sin(angle)], 1).astype(np.float32)
    s, c = np.arange(P)[:, None], np.arange(T)[None, :]
    inside = ((c % P) >= s) & ((c % P) // CHUNK == s // CHUNK)
    start = np.broadcast_to((np.arange(T) % CHUNK == 0)[None, :], (P, T))
    hmask = np.stack([inside, ~start, start], 1).astype(np.float32)
    return {
        "iota_in": np.ascontiguousarray(np.broadcast_to(t, (P, T))), "const_in": const, "freq_in": freq,
        "mask_in": np.ascontiguousarray(np.concatenate(parts, 1)), "rope2_in": rope2, "hmask_in": hmask,
    }


def layout(a):
    sent = {}
    w_in = a["w_in"][0]
    heads = w_in[:, HALF:2 * HALF].reshape(D, 2, 4, 64).transpose(0, 2, 1, 3).reshape(D, HALF)
    w_in = np.concatenate([w_in[:, :HALF], heads, w_in[:, 2 * HALF:]], 1)
    w_out = a["w_out"][0]
    rows = w_out[HALF:].reshape(2, 4, 64, D).transpose(1, 0, 2, 3).reshape(HALF, D)
    w_out = np.concatenate([w_out[:HALF], rows], 0)
    g_attn = a["g_attn_out"][0].reshape(2, 4, 64).transpose(1, 0, 2).reshape(HALF)
    w = {"w_in": slabs(w_in, 8, np.arange(10), 2),
         "w_glu": slabs(a["w_glu"][0], 4, np.arange(8).reshape(2, 4).T.ravel(), 4),
         "w_out": slabs(w_out, 8, np.arange(8), 2)}
    first = 0
    for n, c in enumerate(FFN1_PARTS):
        order = np.stack([np.arange(first, first + c), DFF // P + np.arange(first, first + c)], 1).ravel()
        w[f"gate_up{n}"] = slabs(a["w_gate_up"][0], 8, order, 2)
        w[f"down{n}"] = slabs(a["w_down"][0][first * P:(first + c) * P], c, np.arange(8), 1)
        first += c
    tiles = slabs(a["attn_w_in_2"][0], 8, np.arange(72).reshape(9, 8).T.ravel(), 1).reshape(8, 9, P, 8 * P)
    tiles = np.concatenate([tiles, np.zeros((8, 1, P, 8 * P), np.float32)], 1)
    w["attn_in"] = np.ascontiguousarray(tiles.reshape(40, 2, P, 8 * P).transpose(0, 2, 1, 3).reshape(40, P, SLAB))
    w["attn_out"] = slabs(a["attn_w_out_2"][0], 8, np.arange(8), 2)
    tiles = slabs(a["hgrn_w_in_2"][0], 8, np.arange(24).reshape(3, 8).T.ravel(), 1).reshape(8, 3, P, 8 * P)
    tiles = np.concatenate([tiles, np.zeros((8, 1, P, 8 * P), np.float32)], 1)
    w["hgrn_in"] = np.ascontiguousarray(tiles.reshape(16, 2, P, 8 * P).transpose(0, 2, 1, 3).reshape(16, P, SLAB))
    w["hgrn_out"] = slabs(a["hgrn_w_out_2"][0], 8, np.arange(8), 2)
    for layer, name in enumerate(("a", "h")):
        for n in range(2):
            w[f"up_{name}{n}"] = slabs(a["ffn_w_up_2"][layer], 8, np.arange(16 * n, 16 * n + 16), 2)
            w[f"down_{name}{n}"] = slabs(a["ffn_w_down_2"][layer][2048 * n:2048 * n + 2048], 16, np.arange(8), 1)
    for name, value in w.items():
        sent["w_" + name] = value
    sent["x_in"] = a["x"][0].reshape(T, DC, P).transpose(2, 1, 0)
    vectors = [a["g_pre_mix"], a["g_ssm_out"], g_attn, a["g_post_mix"], a["g_pre_ffn"], a["g_post_ffn"], a["ssm_d"],
               a["b_glu"], a["hgrn_norm_g_2"], a["lb_logits_2"][0], a["lb_logits_2"][1]]
    for layer in range(2):
        vectors += [a["ln_mix_g_2"][layer], a["ln_mix_b_2"][layer], a["ln_ffn_g_2"][layer], a["ln_ffn_b_2"][layer]]
    sent["gains_in"] = np.concatenate([columns(v) for v in vectors], 1)

    def by_state(v):
        return v.reshape(N_PAIR, P).T

    log_dt = np.broadcast_to(a["ssm_log_dt"][0][:, None], (32, 64))
    sent["lam_in"] = np.stack([by_state(a["ssm_lambda_re"][0]), by_state(a["ssm_lambda_im"][0]), by_state(log_dt)], 1)
    sinks = a["attn_sinks"][0].reshape(2, 2, 2).transpose(1, 0, 2)
    sent["sink_in"] = np.broadcast_to(sinks.reshape(1, 8), (P, 8))

    def padded(v):
        o = np.zeros((N_PAIR, 2, 64, 2, 16), np.float32)
        v = v.reshape(N_PAIR, 2, 64, 16)
        for g in range(2):
            o[:, g, :, g, :] = v[:, g]
        return o.reshape(N_PAIR, P, GW).transpose(1, 0, 2)

    sent["b_in"] = np.stack([padded(a["ssm_b_re"][0]), padded(a["ssm_b_im"][0])], 1)
    sent["c_in"] = np.stack([padded(a["ssm_c_re"][0].transpose(0, 2, 1)), padded(a["ssm_c_im"][0].transpose(0, 2, 1))], 1)
    sent["pos_in"] = np.broadcast_to(a["positions"][0], (P, T))
    sent.update(shape_constants())
    return {k: np.ascontiguousarray(v) for k, v in sent.items()}


def kernel(**inputs):
    import concourse.bacc as bacc
    from concourse.bass_utils import run_bass_kernel_spmd

    sent = layout({k: np.asarray(v) for k, v in inputs.items()})
    nc = bacc.Bacc("TRN2", target_bir_lowering=False, num_devices=1)
    handles = {k: nc.dram_tensor(k, v.shape, mybir.dt.from_np(v.dtype), kind="ExternalInput").ap() for k, v in sent.items()}
    out = nc.dram_tensor("out", (P, DC, T), mybir.dt.float32, kind="ExternalOutput").ap()
    weights = {k: handles.pop("w_" + k) for k in STAGES}
    build(nc, weights, out=out, **handles)
    got = run_bass_kernel_spmd(nc, [sent], core_ids=[0]).results[0]["out"]
    return np.ascontiguousarray(got.transpose(2, 1, 0).reshape(1, T, D))
```

```python
from contextlib import ExitStack

import numpy as np

import concourse.bass as bass
from concourse import mybir

P = 128
T = 512
D = 1024
DC = D // P
TB = T // P
CLASSES = 4
assert CLASSES == TB
HALF = 512
N_PAIR = 16
GW = 32
DFF = 2816
FFN1_PARTS = (12, 10)
FFN2_PART = 16
HEAD_PAIRS = 8
GROUPS = 3
PAIR_TILES = 3 * GROUPS
CHUNK = 64
HG_HEADS = 8
SLAB = 2048
ALPHA = 4.0 ** 0.25
RMS_EPS = 1e-6
LN_EPS = 1e-5
NEG = -1e30
TWO_PI = 2.0 * np.pi
PI_HI = 6.28125
PI_LO = TWO_PI - PI_HI
PI_IN = 3.1415925
ROUND = 1.5 * 2.0 ** 23
LN2_HI = 0.693359375
LN2_LO = float(np.log(2.0) - 0.693359375)


class Stage:

    def __init__(self, name, slab0, tile0, slabs, kc, body, before, free0):
        self.name, self.slab0, self.tile0, self.slabs = name, slab0, tile0, slabs
        self.kc, self.body = kc, body
        self.reader = "act" if name.startswith(("attn_in", "up_", "hgrn_in")) else "dve"
        self.free0 = free0[self.reader]
        self.before = before
        self.cum = [0]
        for n in body:
            self.cum.append(self.cum[-1] + n)
        self.trips = slabs // len(body)
        self.tiles = self.cum[-1] * self.trips


def plan():
    rows = [("w_in", 5, 8, [2] * 5), ("w_glu", 4, 4, [2, 2]), ("w_out", 4, 8, [2, 2])]
    for n, c in enumerate(FFN1_PARTS):
        rows += [(f"gate_up{n}", c, 8, [2, 2]), (f"down{n}", 8, c, [1, 1])]
    rows += [("attn_in", 5 * HEAD_PAIRS, 8, [2, 2, 2, 2, 1] * 2), ("attn_out", 4, 8, [2, 2])]
    for n in range(2):
        rows += [(f"up_a{n}", 8, 8, [2, 2]), (f"down_a{n}", 8, 16, [1, 1])]
    rows += [("hgrn_in", 2 * HG_HEADS, 8, [2, 1] * 2), ("hgrn_out", 4, 8, [2, 2])]
    for n in range(2):
        rows += [(f"up_h{n}", 8, 8, [2, 2]), (f"down_h{n}", 8, 16, [1, 1])]
    stages, slab, tile, s, free = {}, 0, 0, None, {"act": 0, "dve": 0}
    for name, slabs, kc, body in rows:
        s = Stage(name, slab, tile, slabs, kc, body, s, free)
        stages[name] = s
        slab, tile = slab + s.slabs, tile + s.tiles
        free[s.reader] += s.tiles
    return stages


STAGES = plan()
GAINS = ["g_pre_mix", "g_ssm", "g_attn", "g_post_mix", "g_pre_ffn", "g_post_ffn", "d", "b_glu", "g_hgrn", "lb0", "lb1",
         "ln_mix_g0", "ln_mix_b0", "ln_ffn_g0", "ln_ffn_b0", "ln_mix_g1", "ln_mix_b1", "ln_ffn_g1", "ln_ffn_b1"]
GAIN_COLS = [8, 4, 4, 8, 8, 8, 4, 8, 8, 8, 8] + [8] * 8
GAIN_AT = dict(zip(GAINS, np.cumsum([0] + GAIN_COLS[:-1]).tolist()))
N_GAIN = sum(GAIN_COLS)


def build(nc, w, x_in, gains_in, lam_in, sink_in, b_in, c_in, pos_in, iota_in, const_in, freq_in, mask_in, rope2_in,
          hmask_in, out):
    f32, f32r, bf16, i32 = mybir.dt.float32, mybir.dt.float32r, mybir.dt.bfloat16, mybir.dt.int32
    ALU, ACT, AX = mybir.AluOpType, mybir.ActivationFunctionType, mybir.AxisListType
    ds = bass.ds

    base = (nc.sbuf_base + 63) // 64 * 64
    KB = 1024
    RAW_AT = base
    WH_AT = RAW_AT + 16 * KB
    WL_AT = WH_AT + 16 * KB
    XH_AT = WL_AT + 16 * KB
    XL_AT = XH_AT + 16 * KB
    H_AT = XL_AT + 16 * KB
    Y_AT = H_AT + 16 * KB
    BIG_AT = Y_AT + 16 * KB
    EX_AT = BIG_AT + 64 * KB
    used = [EX_AT]

    def at(name, offset, shape, dt=f32):
        return nc.alloc_sbuf_tensor_at(name, [P] + list(shape), dt, offset=offset)

    where = {}

    def extra(name, shape, dt=f32):
        size = int(np.prod(shape)) * (2 if dt == bf16 else 4)
        where[name] = used[0]
        used[0] += (size + 31) // 32 * 32
        return at(name, where[name], shape, dt)

    raw = at("raw", RAW_AT, [2, SLAB])
    w_hi = at("w_hi", WH_AT, [2, SLAB], f32r)
    w_lo = at("w_lo", WL_AT, [2, SLAB], f32r)
    x_hi = at("x_hi", XH_AT, [DC, T], f32r)
    x_lo = at("x_lo", XL_AT, [DC, T], f32r)
    h = at("h", H_AT, [DC, T])
    y = at("y", Y_AT, [DC, T])
    hid_hi = at("hid_hi", BIG_AT, [16, T], f32r)
    hid_lo = at("hid_lo", BIG_AT + 32 * KB, [16, T], f32r)

    x_raw = at("x_raw", Y_AT, [DC, T])
    u = at("u", Y_AT, [4, T])
    q1 = at("q1", Y_AT + 8 * KB, [4, T])
    o1_tok = at("o1_tok", BIG_AT + 16 * KB, [TB, HALF])
    mask_raw = at("mask_raw", H_AT, [6 * P])
    b_re = at("b_re", BIG_AT + 56 * KB, [N_PAIR, GW])
    b_im = at("b_im", BIG_AT + 58 * KB, [N_PAIR, GW])
    bb_re = at("bb_re", BIG_AT + 60 * KB, [N_PAIR, GW])
    bb_im = at("bb_im", BIG_AT + 62 * KB, [N_PAIR, GW])
    cos_t = at("cos_t", BIG_AT, [N_PAIR, T])
    sin_t = at("sin_t", BIG_AT + 32 * KB, [N_PAIR, T])
    prod = at("prod", H_AT, [4, T])
    k1 = at("k1", H_AT + 8 * KB, [T])
    v1 = at("v1", H_AT + 10 * KB, [T])
    v1_tok = at("v1_tok", H_AT + 12 * KB, [TB, P])
    qr1 = at("qr1", BIG_AT, [2, T])
    mod_even = at("mod_even", XH_AT + 8 * KB, [2, T])
    mod_odd = at("mod_odd", XL_AT + 12 * KB, [2, T])
    mod = [[m[:, n, :] for n in range(2)] for m in (mod_even, mod_odd)]
    mod_more = at("mod_more", XH_AT + 12 * KB, [2, T])
    scan_even = at("scan_even", XL_AT + 8 * KB, [2, T])
    scan_odd = at("scan_odd", H_AT + 14 * KB, [T])
    p1 = at("p1", BIG_AT + 4 * KB, [4, 4 * P])
    p1_t = at("p1_t", BIG_AT + 12 * KB, [2, 4 * P])

    qkv = at("qkv", BIG_AT, [2, PAIR_TILES, T])
    v_tok = at("v_tok", BIG_AT + 36 * KB, [2, GROUPS, TB, P])
    p2 = at("p2", BIG_AT + 48 * KB, [2, 4 * P])
    p2_t = at("p2_t", BIG_AT + 52 * KB, [2, 4 * P])
    o_near = at("o_near", BIG_AT + 56 * KB, [2, TB, 64])
    o_class = at("o_class", BIG_AT + 58 * KB, [2, CLASSES, 66])
    o_far = at("o_far", BIG_AT + 61 * KB, [2, TB, 66])
    o2_tok = at("o2_tok", Y_AT, [TB, D])

    hg_q = at("hg_q", BIG_AT, [2, T])
    hg_s = at("hg_s", BIG_AT + 4 * KB, [2, T])
    hg_k = at("hg_k", BIG_AT + 8 * KB, [2, T])
    hg_v = at("hg_v", BIG_AT + 12 * KB, [2, T])
    f_cum = at("f_cum", BIG_AT + 16 * KB, [2, T])
    q_dec = at("q_dec", BIG_AT + 20 * KB, [2, T])
    k_dec = at("k_dec", BIG_AT + 24 * KB, [2, T])
    hg_o = at("hg_o", BIG_AT + 32 * KB, [HG_HEADS, T])
    f_run = at("f_run", Y_AT, [T])
    f_start = at("f_start", Y_AT + 2 * KB, [T])
    k_tok = at("k_tok", Y_AT + 12 * KB, [TB, P])
    v_htok = at("v_htok", Y_AT + 14 * KB, [TB, P])

    consts = extra("consts", [3, P])
    ident, swap1, ones = (consts[:, n, :] for n in range(3))
    ident_b = extra("ident_b", [P], bf16)
    masks = extra("masks", [6 * P], bf16)
    rope_c = extra("rope_c", [T])
    rope_s = extra("rope_s", [T])
    gains = extra("gains", [N_GAIN])
    lam = extra("lam", [3, N_PAIR])
    par = extra("par", [26, N_PAIR])
    sink = extra("sink", [8])
    eps = extra("eps", [3])
    freq = extra("freq", [1])
    sq = extra("sq", [2, T])
    root = extra("root", [T])
    rstd = extra("rstd", [T])
    tmp = extra("tmp", [4, T])
    c_re = extra("c_re", [N_PAIR, GW])
    c_im = extra("c_im", [N_PAIR, GW])
    assert used[0] <= nc.sbuf_usable_end, used[0] - nc.sbuf_usable_end
    b_lhs = at("b_lhs", where["sq"], [2, 4, P])
    scan = [[scan_even[:, 0, :], scan_even[:, 1, :]], [scan_odd[:, :], rstd[:, :]]]
    c_neg = at("c_neg", where["root"], [N_PAIR, GW])
    iota = at("iota", where["tmp"] + 6 * KB, [T])
    pos = at("pos", where["tmp"], [T], i32)
    swapped = at("swapped", where["tmp"] + 2 * KB, [2, T])
    a_mask = at("a_mask", where["c_re"], [T])
    run_mask = at("run_mask", where["rope_c"], [T])
    stat = at("stat", where["c_im"], [4, 16])
    near_max = at("near_max", where["c_im"] + 512, [2, TB])
    near_sum = at("near_sum", where["c_im"] + 544, [2, TB])
    mix = at("mix", where["c_im"] + 576, [5, TB])
    lbp = at("lbp", where["c_im"] + 256, [6, HG_HEADS])
    start_mask = at("start_mask", where["rope_s"], [T])
    state = at("state", where["tmp"] + 2 * KB, [8, P])
    acc, acc_sq = tmp[:, 0, :], tmp[:, 1, :]
    m1, m2, m_class = masks[:, 0:256], masks[:, 256:512], (masks[:, 512:640], masks[:, 640:768])

    def gain(name, c):
        return gains[:, GAIN_AT[name] + c:GAIN_AT[name] + c + 1]

    def by_class(tile, r):
        return tile.rearrange("p (u r) -> p r u", r=CLASSES)[:, r, :]

    def chunk(buf, c):
        if isinstance(c, int):
            return buf[:, c, :]
        return buf[:, ds(c, 1), :].rearrange("p a t -> p (a t)")

    ps = nc.alloc_psum_tensor("ps", [P, 8, T], f32)
    SUM = 7

    def counts(rows):
        at_, n = {}, 0
        for name, c in rows:
            at_[name] = n
            n += c
        return at_

    XB = counts([("w_in", 8), ("w_glu", 4), ("w_out", 8), ("gate_up", 8), ("attn_in", 8), ("attn_out", 8),
                 ("up_a", 8), ("hgrn_in", 8), ("hgrn_out", 8), ("up_h", 8)])
    LN = [(f"{kind}_{part}_{layer}", 8) for layer in "ah" for part in ("mix", "ffn") for kind in ("out", "mid", "res")]
    YB = counts([("glu", 4), ("attn1", 4), ("w_out", 8), ("res_mix", 8), ("ffn", 8), ("res_ffn", 8)] + LN)
    HB = counts([("0", FFN1_PARTS[0]), ("1", FFN1_PARTS[1])] +
                [(f"{layer}{n}", FFN2_PART) for layer in "ah" for n in range(2)])
    SUMS = [("pre_mix", 8), ("ssm", 4), ("attn", 4), ("post_mix", 1), ("pre_ffn", 8), ("post_ffn", 1)]
    for part in ("mix_a", "ffn_a"):
        SUMS += [("mean_" + part, 0), ("var_" + part, 8)]
    SUMS += [(f"head{n}", 1) for n in range(HG_HEADS)]
    for part in ("mix_h", "ffn_h"):
        SUMS += [("mean_" + part, 0), ("var_" + part, 8)]
    SB = counts(SUMS)
    SK = {name: k for k, (name, _) in enumerate(SUMS)}
    SK_ROOT = counts([(name, 0 if name.startswith("mean") else 1) for name, _ in SUMS])
    ACCS = [("post_mix", "w_out"), ("post_ffn", "ffn"), ("mean_mix_a", "out_mix_a"), ("mean_ffn_a", "out_ffn_a"),
            ("mean_mix_h", "out_mix_h"), ("mean_ffn_h", "out_ffn_h")]
    ACC = {name: k for k, (name, _) in enumerate(ACCS)}
    MEANS = {name: k for k, (name, _) in enumerate(ACCS[2:])}
    PR = {name: k for k, name in enumerate(
        ["lr", "dt", "z", "k", "f", "e", "two_k", "em1", "mag", "th", "r", "r_turn", "r_hi", "r_lo", "sin", "sin_half",
         "c1", "am1", "ai", "den", "nr", "ni", "fr", "fi", "t0", "t1"])}

    def sem(name):
        return nc.alloc_semaphore(name)

    raw_ready = [sem("raw_ready0"), sem("raw_ready1")]
    whi_ready = sem("whi_ready")
    wlo_ready = sem("wlo_ready")
    tile_done = sem("tile_done")
    tile_free = {e: sem("tile_free_" + e) for e in ("dve", "act")}
    xhi_ready = sem("xhi_ready")
    xlo_ready = sem("xlo_ready")
    y_ready = sem("y_ready")
    merge_ready = sem("merge_ready")
    gate_scaled = sem("gate_scaled")
    silu_ready = sem("silu_ready")
    hid_pre = sem("hid_pre")
    hid_half = sem("hid_half")
    hid_ready = sem("hid_ready")
    sq_ready = sem("sq_ready")
    sq_used = sem("sq_used")
    acc_ready = sem("acc_ready")
    acc_summed = sem("acc_summed")
    root_ready = sem("root_ready")
    result_ready = sem("result_ready")
    rstd_ready = sem("rstd_ready")
    x_ready = [sem("x_ready0"), sem("x_ready1")]
    gains_ready = sem("gains_ready")
    consts_ready = sem("consts_ready")
    small_ready = sem("small_ready")
    eps_ready = sem("eps_ready")
    mask_ready = sem("mask_ready")
    turn_ready = sem("turn_ready")
    sines_ready = sem("sines_ready")
    rope_ang = sem("rope_ang")
    rope_ready = sem("rope_ready")
    bb_ready = sem("bb_ready")
    bt_done = sem("bt_done")
    blhs_ready = sem("blhs_ready")
    ang_ready = {e: sem("ang_ready_" + e) for e in ("dve", "pool")}
    ang_used = sem("ang_used")
    bu_done = sem("bu_done")
    bu_free = sem("bu_free")
    scan_ready = sem("scan_ready")
    prod_ready = sem("prod_ready")
    yssm_done = sem("yssm_done")
    pre_gelu = sem("pre_gelu")
    gate_ready = sem("gate_ready")
    vt1_done, vt1_ready = sem("vt1_done"), sem("vt1_ready")
    kr1_swap, kr1_ready = sem("kr1_swap"), sem("kr1_ready")
    qr1_swap, qr1_ready = sem("qr1_swap"), sem("qr1_ready")
    s1_done = sem("s1_done")
    max1_ready = sem("max1_ready")
    p1_ready = sem("p1_ready")
    p1t_done, p1t_ready = sem("p1t_done"), sem("p1t_ready")
    o1_done, o1_ready = sem("o1_done"), sem("o1_ready")
    o1t_done = sem("o1t_done")
    h_back = sem("h_back")
    vt2_done = sem("vt2_done")
    rot_ready = sem("rot_ready")
    vtok_ready = sem("vtok_ready")
    s2_done, max2_ready, p2_ready = sem("s2_done"), sem("max2_ready"), sem("p2_ready")
    p2t_done = sem("p2t_done")
    p2t_ready = sem("p2t_ready")
    far_ready = sem("far_ready")
    mix_half, mix_exp = sem("mix_half"), sem("mix_exp")
    sums_sent = sem("sums_sent")
    joined = sem("joined")
    o2_done, o2_ready = sem("o2_done"), sem("o2_ready")
    o2t_done = sem("o2t_done")
    rope2_ready = sem("rope2_ready")
    hm_ready = sem("hm_ready")
    lb_half, lb_exp = sem("lb_half"), sem("lb_exp")
    dec_ready = sem("dec_ready")
    a_done, a_ready = sem("a_done"), sem("a_ready")
    ht_done, ht_ready = sem("ht_done"), sem("ht_ready")
    kv_done, st_ready = sem("kv_done"), sem("st_ready")
    oh_done, oh_ready = sem("oh_done"), sem("oh_ready")
    out_done = sem("out_done")

    LAST = STAGES["down_h1"]
    SMALL = 10
    SPARE_BANKS = {"w_in": 4, "gate_up0": 2}
    GLU_BANKS = (0, 1, 2, 1)
    ANGLES = (3, 6, 9, 12, N_PAIR)
    POOL_PAIRS = range(3, N_PAIR, 3)
    BLOCKS1 = [(b, min(b, 1) + 1) for b in range(TB)]
    STEPS2 = [(hh, b, min(b, 1) + 1) for hh in range(2) for b in range(TB)]

    def joins(p, j):
        if j == 2 and not (isinstance(p, int) and p == 1):
            return -1
        if j == 7:
            return 0
        return 1 if j == 9 and isinstance(p, int) and p == HEAD_PAIRS else None

    def first(i):
        return isinstance(i, int) and i == 0

    def run(eng, st, body):
        if st.trips == 1:
            body(0, False)
        elif st is LAST:
            with eng.Fori(0, st.trips - 1) as i:
                body(i, False)
            body(st.trips - 1, True)
        else:
            with eng.Fori(0, st.trips) as i:
                body(i, False)

    with nc.Block() as block:

        @block.sync
        def _(sp):
            def load_x():
                for half in range(2):
                    sp.dma_start(x_raw[:, 4 * half:4 * half + 4, :], x_in[:, 4 * half:4 * half + 4, :]) \
                      .then_inc(x_ready[half], 16)

            for name, st in STAGES.items():

                def load(i, last, st=st, src=w[name]):
                    for c, tiles in enumerate(st.body):
                        n = st.slab0 + c + len(st.body) * i
                        slot, width = (st.slab0 + c) % 2, tiles * st.kc * P
                        if st.slab0 + c >= 2:
                            sp.wait_ge(wlo_ready, n - 1)
                        row = c + len(st.body) * i
                        part = src[row, :, 0:width] if isinstance(row, int) else \
                            src[ds(row, 1), :, 0:width].rearrange("a p n -> p (a n)")
                        sp.dma_start(raw[:, slot, 0:width], part).then_inc(raw_ready[slot], 16)
                        if st.slab0 + c == 0:
                            load_x()

                with_loop = st.trips > 1
                if with_loop:
                    with sp.Fori(0, st.trips) as i:
                        load(i, False)
                else:
                    load(0, False)
            for c in range(DC):
                sp.wait_ge(result_ready, c + 1)
                sp.dma_start(out[:, c, :], h[:, c, :]).then_inc(out_done, 16)
            sp.wait_ge(out_done, 16 * DC)

        @block.gpsimd
        def _(pool):
            def angle_step(out, src, *how):
                pool.tensor_scalar(out, src, *how)
                pool.drain()

            pool.wait_ge(small_ready, 16 * SMALL)
            pool.wait_ge(turn_ready, 2)
            for pr in POOL_PAIRS:
                if pr == 12:
                    pool.wait_ge(bt_done, 1)
                ang, k = sin_t[:, pr, :], cos_t[:, pr, :]
                r_hi, r_lo, r_turn = (par[:, PR[n], pr:pr + 1] for n in ("r_hi", "r_lo", "r_turn"))
                pool.tensor_scalar(ang, iota[:, :], r_hi, None, ALU.mult)
                angle_step(k, iota[:, :], r_turn, ROUND, ALU.mult, ALU.add)
                angle_step(k, k, ROUND, None, ALU.subtract)
                pool.tensor_tensor(ang, ang, k, ALU.subtract)
                pool.drain()
                angle_step(k, iota[:, :], r_lo, None, ALU.mult)
                pool.tensor_tensor(ang, ang, k, ALU.add)
                pool.drain()
                pool.tensor_scalar(ang, ang, 0.5, -0.5, ALU.min, ALU.max).then_inc(ang_ready["pool"], 1)

            for pr in range(N_PAIR):
                for n, (part, by) in enumerate(((0, cos_t), (0, sin_t), (1, sin_t), (1, cos_t))):
                    pool.wait_ge(scan_ready, 2 * pr + part + 1)
                    if pr:
                        pool.wait_ge(yssm_done, 4 * pr + n - 3)
                    pool.tensor_tensor(prod[:, n, :], scan[pr % 2][part], by[:, pr, :], ALU.mult).then_inc(prod_ready, 1)

            def accumulate(name, event):
                plain = name.startswith("mean")
                for c in range(DC - 1):
                    pool.wait_ge(y_ready, YB[event] + c + 1)
                    if plain and c == 1:
                        last = pool.tensor_tensor(acc, y[:, 0, :], y[:, 1, :], ALU.add)
                    elif plain and c:
                        last = pool.tensor_tensor(acc, acc, y[:, c, :], ALU.add)
                    elif not plain:
                        last = pool.tensor_tensor(acc_sq if c else acc, y[:, c, :], y[:, c, :], ALU.mult)
                        if c:
                            pool.drain()
                            last = pool.tensor_tensor(acc, acc, acc_sq, ALU.add)
                    if c < DC - 2 and (c or not plain):
                        pool.drain()
                last.then_inc(acc_ready, 1)

            def send(pa, hh, again):
                pool.wait_ge(o2_ready, 8 * pa + 4 * hh + 4)
                if again:
                    pool.wait_ge(joined, 2 * pa + hh - 1)
                pool.sem_inc(sums_sent, 1)
                for b in range(TB):
                    pool.dma_start(o_far[:, hh, b, :], o_class[32 * b:32 * b + 32, hh, :, :]).then_inc(far_ready, 16)

            for name, event in ACCS[:2]:
                accumulate(name, event)
            for hh in range(2):
                send(0, hh, False)
            with pool.Fori(1, HEAD_PAIRS) as pa:
                for hh in range(2):
                    send(pa, hh, True)
            for name, event in ACCS[2:]:
                accumulate(name, event)

        @block.tensor
        def _(pe):
            def spare(st, t, i):
                return first(i) and st.name in SPARE_BANKS and t in (2, 3)

            def slab(st, c, i, xs=None):
                slot, per = (st.slab0 + c) % 2, st.cum[-1]
                pe.wait_ge(wlo_ready, st.slab0 + c + 1 + len(st.body) * i)
                hi, lo = xs or (x_hi, x_lo)
                for m in range(st.body[c]):
                    t0 = st.tile0 + st.cum[c] + m
                    own = spare(st, st.cum[c] + m, i)
                    if not own and st.free0 + st.cum[c] + m >= 2:
                        pe.wait_ge(tile_free[st.reader], st.free0 + st.cum[c] + m - 1 + per * i)
                    o = ps[:, SPARE_BANKS[st.name] + m if own else t0 % 2, :]
                    for k in range(st.kc):
                        a = (m * st.kc + k) * P
                        pe.matmul(o, w_lo[:, slot, a:a + P], hi[:, k, :], start=k == 0, stop=False)
                        pe.matmul(o, w_hi[:, slot, a:a + P], lo[:, k, :], start=False, stop=False)
                        last = pe.matmul(o, w_hi[:, slot, a:a + P], hi[:, k, :], start=False, stop=k == st.kc - 1)
                    last.then_inc(tile_done, 1)

            def read_out(before, st):
                if before.reader != st.reader:
                    pe.wait_ge(tile_free[before.reader], before.free0 + before.tiles)

            def first_slab(st, xs, ready, before, beside=None, chunks=None):
                slot, chunks = st.slab0 % 2, chunks or range(st.kc)
                if 0 in chunks:
                    pe.wait_ge(wlo_ready, st.slab0 + 1)
                hi, lo = xs or (x_hi, x_lo)
                for k in chunks:
                    first, last_one = k == 0, k == st.kc - 1
                    pe.wait_ge(ready, before + k + 1)
                    for m in range(st.body[0]):
                        if first and st.free0 + m >= 2:
                            pe.wait_ge(tile_free[st.reader], st.free0 + m - 1)
                        o, a = ps[:, (st.tile0 + m) % 2, :], (m * st.kc + k) * P
                        pe.matmul(o, w_lo[:, slot, a:a + P], hi[:, k, :], start=first, stop=False)
                        pe.matmul(o, w_hi[:, slot, a:a + P], lo[:, k, :], start=False, stop=False)
                        last = pe.matmul(o, w_hi[:, slot, a:a + P], hi[:, k, :], start=False, stop=last_one)
                        if last_one:
                            last.then_inc(tile_done, 1)
                    if beside:
                        beside(k)

            def dense(name, operand=None, xs=None, hid=None, beside=None, begun=0):
                st = STAGES[name]
                if not begun:
                    read_out(st.before, st)
                if operand or hid is not None:
                    first_slab(st, xs, hid_ready if hid is not None else xlo_ready,
                               hid if hid is not None else XB[operand], beside, range(begun, st.kc))
                else:
                    slab(st, 0, 0, xs)
                for c in range(1, len(st.body)):
                    slab(st, c, 0, xs)
                with pe.Fori(1, st.trips) as i:
                    for c in range(len(st.body)):
                        slab(st, c, i, xs)

            def feature_sum(name, n):
                for c in range(n):
                    sum_chunk(name, n, c)

            def sum_chunk(name, n, c):
                if SK[name] and c == 0:
                    pe.wait_ge(root_ready, SK[name])
                j = SB[name] + c
                pe.wait_ge(sq_ready, j + 1)
                pe.matmul(ps[:, SUM, :], ones, sq[:, j % 2, :], start=c == 0, stop=c == n - 1).then_inc(sq_used, 1)

            def acc_sum(name):
                pe.wait_ge(root_ready, SK[name])
                pe.wait_ge(acc_ready, ACC[name] + 1)
                pe.matmul(ps[:, SUM, :], ones, acc, start=True, stop=False)
                if name in MEANS:
                    pe.wait_ge(y_ready, YB[ACCS[ACC[name]][1]] + DC)
                    pe.matmul(ps[:, SUM, :], ones, y[:, DC - 1, :], start=False, stop=True).then_inc(acc_summed, 1)
                else:
                    pe.wait_ge(sq_ready, SB[name] + 1)
                    pe.matmul(ps[:, SUM, :], ones, sq[:, SB[name] % 2, :], start=False, stop=True).then_inc(sq_used, 1)

            pe.wait_ge(consts_ready, 16)
            st = STAGES["w_in"]
            first_slab(st, None, xlo_ready, XB["w_in"], lambda k: sum_chunk("pre_mix", DC, k))
            for c in range(1, 5):
                slab(st, c, 0)
                if c == 2:
                    pe.wait_ge(bb_ready, 1)
                    for n, bb in enumerate((bb_re, bb_im)):
                        for i in range(4):
                            last = pe.transpose(ps[:, 2 + n, i * P:(i + 1) * P],
                                                bb[:, 4 * i:4 * i + 4, :].rearrange("p a c -> p (a c)"), ident)
                    last.then_inc(bt_done, 1)

            def ssm_in(pr):
                i, q = divmod(pr, 4)
                if pr >= 2:
                    pe.wait_ge(bu_free, pr - 1)
                for n in range(2):
                    last = pe.matmul(ps[:, 2 + 2 * (pr % 2) + n, :], b_lhs[GW * q:GW * q + GW, n, i, :],
                                     u[GW * q:GW * q + GW, i, :], start=True, stop=True)
                last.then_inc(bu_done, 1)

            def ssm_out(pr):
                i, q = divmod(pr, 4)
                if q == 0 and i >= 2:
                    pe.wait_ge(pre_gelu, i - 1)
                for n, cc in enumerate((c_re, c_im, c_neg, c_im)):
                    pe.wait_ge(prod_ready, 4 * pr + n + 1)
                    pe.matmul(ps[GW * q:GW * q + GW, (6, SUM)[i % 2], :], cc[:, pr, :], prod[:, n, :],
                              start=n == 0, stop=n == 3).then_inc(yssm_done, 1)

            pe.wait_ge(blhs_ready, 1)
            pe.wait_ge(tile_free["dve"], STAGES["w_in"].tiles)
            ssm_in(0)
            ssm_in(1)
            for pr in range(N_PAIR):
                if pr + 2 < N_PAIR:
                    ssm_in(pr + 2)
                ssm_out(pr)

            pe.wait_ge(mask_ready, 1)
            pe.wait_ge(pre_gelu, 4)
            for b in range(TB):
                last = pe.transpose(ps[:, 2, b * P:(b + 1) * P], v1[:, b * P:(b + 1) * P], ident)
            last.then_inc(vt1_done, 1)
            pe.matmul(ps[:, 3, :], swap1, k1[:, :], start=True, stop=True).then_inc(kr1_swap, 1)
            pe.wait_ge(vt1_ready, 1)
            pe.wait_ge(kr1_ready, 1)
            steps = [(hh, b, n) for hh in range(2) for b, n in BLOCKS1]
            glu_st = STAGES["w_glu"]
            with pe.Fori(0, 2) as i:
                pe.wait_ge(o1_ready, 8 * i)
                for m in range(2):
                    pe.matmul(ps[:, (5, SUM)[m], :], swap1, chunk(q1, 2 * i + m), start=True, stop=True) \
                      .then_inc(qr1_swap, 1)
                pe.wait_ge(qr1_ready, 2 * i + 2)

                def scores1(s):
                    hh, b, n = steps[s]
                    for m in range(2):
                        o = ps[:, 3 + s % 2, 2 * P * m:2 * P * m + n * P]
                        pe.matmul(o, qr1[64 * hh:64 * hh + 64, m, b * P:(b + 1) * P],
                                  k1[64 * hh:64 * hh + 64, (b + 1 - n) * P:(b + 1) * P], start=True, stop=False)
                        last = pe.matmul(o, ident_b[:, :], m1[:, 2 * P - n * P:2 * P], start=False, stop=True)
                    last.then_inc(s1_done, 1)

                def turn1(s):
                    hh, b, n = steps[s]
                    pe.wait_ge(p1_ready, 8 * i + s + 1)
                    if s >= 2:
                        pe.wait_ge(p1t_ready, 8 * i + s - 1)
                    for m in range(2):
                        for j in range(n):
                            last = pe.transpose(ps[:, (5, SUM)[s % 2], (m * n + j) * P:(m * n + j + 1) * P],
                                                p1[:, s % 4, (2 * m + j) * P:(2 * m + j + 1) * P], ident)
                    last.then_inc(p1t_done, 1)

                def glu_part(s):
                    m = s // 2
                    slot = (glu_st.slab0 + m // 2) % 2
                    if s == 0:
                        pe.wait_ge(xlo_ready, XB["w_glu"] + glu_st.kc)
                    if s % 4 == 0:
                        pe.wait_ge(wlo_ready, glu_st.slab0 + m // 2 + 1 + 2 * i)
                    if s % 2 == 0:
                        pe.wait_ge(tile_free["dve"], glu_st.free0 + (-2, 0, 0, 2)[m] + 4 * i)
                    o = ps[:, GLU_BANKS[m], :]
                    for k in (0, 1) if s % 2 == 0 else (2, 3):
                        a = ((m % 2) * glu_st.kc + k) * P
                        pe.matmul(o, w_lo[:, slot, a:a + P], x_hi[:, k, :], start=k == 0, stop=False)
                        pe.matmul(o, w_hi[:, slot, a:a + P], x_lo[:, k, :], start=False, stop=False)
                        last = pe.matmul(o, w_hi[:, slot, a:a + P], x_hi[:, k, :], start=False, stop=k == 3)
                    if s % 2:
                        last.then_inc(tile_done, 1)

                def values1(s):
                    hh, b, n = steps[s]
                    pe.wait_ge(p1t_ready, 8 * i + s + 1)
                    if s:
                        pe.wait_ge(o1_ready, 8 * i + s)
                    for m in range(2):
                        for j in range(n):
                            last = pe.matmul(ps[:, 6, 64 * m:64 * m + 64], p1_t[:, s % 2, (m * n + j) * P:(m * n + j + 1) * P],
                                             v1_tok[:, b + 1 - n + j, 64 * hh:64 * hh + 64], start=j == 0, stop=j == n - 1)
                    last.then_inc(o1_done, 1)

                scores1(0)
                scores1(1)
                for s in range(8):
                    turn1(s)
                    if s < 6:
                        scores1(s + 2)
                    glu_part(s)
                    if s:
                        values1(s - 1)
                values1(7)
            pe.wait_ge(o1_ready, 16)
            for c in range(4):
                if c >= 2:
                    pe.wait_ge(y_ready, YB["attn1"] + c - 1)
                for b in range(TB):
                    last = pe.transpose(ps[:, 4 + c % 2, b * P:(b + 1) * P], o1_tok[:, b, c * P:(c + 1) * P], ident)
                last.then_inc(o1t_done, 1)

            feature_sum("ssm", 4)
            feature_sum("attn", 4)
            dense("w_out", "w_out")
            acc_sum("post_mix")
            for n in range(2):
                if n == 0:
                    dense("gate_up0", "gate_up", beside=lambda k: sum_chunk("pre_ffn", DC, k))
                else:
                    dense("gate_up1")
                dense(f"down{n}", None, (hid_hi, hid_lo), HB[str(n)])
            acc_sum("post_ffn")

            st = STAGES["attn_in"]

            def attention(p, sub, i, project, attend):
                old, pa = 1 - sub, p - 1
                tile = st.free0 + PAIR_TILES * p
                for j in range(10):
                    s = j - 1
                    if attend and 1 <= j <= 8:
                        hh, b, near = STEPS2[s]
                        pe.wait_ge(p2_ready, 8 * pa + s + 1)
                        if s >= 2:
                            pe.wait_ge(p2t_ready, 8 * pa + s - 1)
                        for a in range(near + 2):
                            last = pe.transpose(ps[:, 5 + s % 2, a * P:(a + 1) * P], p2[:, s % 2, a * P:(a + 1) * P], ident)
                        last.then_inc(p2t_done, 1)
                    if attend and j <= 7:
                        hh, b, near = STEPS2[j]
                        if j == 0:
                            pe.wait_ge(rot_ready, 6 * pa + 6)
                            pe.wait_ge(vtok_ready, 3 * pa + 3)
                        rows = slice(64 * hh, 64 * hh + 64)
                        o = ps[:, 2 + j % 2, 0:near * P]
                        pe.matmul(o, qkv[rows, old, 0, b * P:(b + 1) * P],
                                  qkv[rows, old, 1, (b + 1 - near) * P:(b + 1) * P], start=True, stop=False)
                        pe.matmul(o, ident_b[:, :], m2[:, 2 * P - near * P:2 * P], start=False, stop=True)
                        for g in range(1, GROUPS):
                            o = ps[:, 2 + j % 2, (1 + g) * P:(2 + g) * P]
                            pe.matmul(o, by_class(qkv[rows, old, 3 * g, :], b), by_class(qkv[rows, old, 3 * g + 1, :], b),
                                      start=True, stop=False)
                            last = pe.matmul(o, ident_b[:, :], m_class[g - 1], start=False, stop=True)
                        last.then_inc(s2_done, 1)
                    if project and j <= 8 and not (first(p) and j < 2):
                        project_tile(p, sub, i, j)
                    elif first(p) and j == 0:
                        first_slab(st, None, xlo_ready, XB["attn_in"])
                    if not project and j < DC - 1:
                        turn_output(j, 7)
                    if not project and 2 <= j <= DC:
                        out = STAGES["attn_out"]
                        if j == 2:
                            read_out(out.before, out)
                        first_slab(out, None, xlo_ready, XB["attn_out"], chunks=range(j - 2, j - 1))
                    if attend and 1 <= j <= 8:
                        hh, b, near = STEPS2[s]
                        pe.wait_ge(p2t_ready, 8 * pa + s + 1)
                        pe.wait_ge(o2_ready, 8 * pa + s)
                        value = slice(64 * hh, 64 * hh + 64)
                        for a in range(near):
                            pe.matmul(ps[:, 4, 0:64], p2_t[:, s % 2, a * P:(a + 1) * P],
                                      v_tok[:, old, 0, b + 1 - near + a, value], start=a == 0, stop=a == near - 1)
                        for g in range(1, GROUPS):
                            a = near + g - 1
                            last = pe.matmul(ps[:, 4, 64:128], p2_t[:, s % 2, a * P:(a + 1) * P],
                                             v_tok[:, old, g, b, value], start=g == 1, stop=g == GROUPS - 1)
                        last.then_inc(o2_done, 1)
                    if project and j >= 1 and (j - 1) % 3 == 2:
                        t = j - 1
                        pe.wait_ge(tile_free["act"], tile + t + 1)
                        pe.wait_ge(vtok_ready, 3 * p + t // 3)
                        for b in range(TB):
                            tokens = by_class(qkv[:, sub, t, :], b) if t // 3 else qkv[:, sub, t, b * P:(b + 1) * P]
                            last = pe.transpose(ps[:, 7, b * P:(b + 1) * P], tokens, ident)
                        last.then_inc(vt2_done, 1)

            def turn_output(c, bank):
                if 1 <= c < DC - 1:
                    pe.wait_ge(xlo_ready, XB["attn_out"] + c)
                pe.wait_ge(joined, 2 * c + 2)
                for b in range(TB):
                    last = pe.transpose(ps[:, bank, b * P:(b + 1) * P], o2_tok[:, b, c * P:(c + 1) * P], ident)
                last.then_inc(o2t_done, 1)

            def project_tile(p, sub, i, j):
                c = 5 * sub + j // 2
                slot, m = (st.slab0 + c) % 2, j % 2
                if m == 0:
                    pe.wait_ge(wlo_ready, st.slab0 + 5 * p + j // 2 + 1)
                t0 = st.tile0 + 9 * sub + j
                pe.wait_ge(tile_free["act"], st.free0 + 9 * p + j - 1)
                o = ps[:, t0 % 2, :]
                for k in range(DC):
                    a = (m * DC + k) * P
                    pe.matmul(o, w_lo[:, slot, a:a + P], x_hi[:, k, :], start=k == 0, stop=False)
                    pe.matmul(o, w_hi[:, slot, a:a + P], x_lo[:, k, :], start=False, stop=False)
                    last = pe.matmul(o, w_hi[:, slot, a:a + P], x_hi[:, k, :], start=False, stop=k == DC - 1)
                last.then_inc(tile_done, 1)

            read_out(st.before, st)
            attention(0, 0, 0, True, False)
            attention(1, 1, 0, True, True)
            with pe.Fori(0, HEAD_PAIRS // 2 - 1) as i:
                attention(2 * i + 2, 0, i + 1, True, True)
                attention(2 * i + 3, 1, i + 1, True, True)
            attention(HEAD_PAIRS, 0, 0, False, True)
            turn_output(DC - 1, 5)

            def norm_and_ffn(layer, proj, up, down):
                dense(proj, proj, begun=DC - 1)
                acc_sum(f"mean_mix_{layer}")
                feature_sum(f"var_mix_{layer}", DC)
                for n in range(2):
                    dense(f"{up}{n}", up if n == 0 else None)
                    dense(f"{down}{n}", None, (hid_hi, hid_lo), HB[f"{layer}{n}"])
                acc_sum(f"mean_ffn_{layer}")
                feature_sum(f"var_ffn_{layer}", DC)

            norm_and_ffn("a", "attn_out", "up_a", "down_a")

            st = STAGES["hgrn_in"]
            O_BANK = SUM

            def hgrn_tile(hd, par, j, chunks):
                c, m = 2 * par + j // 2, j % 2
                slot, o = (st.slab0 + c) % 2, ps[:, (st.tile0 + 3 * par + j) % 2, :]
                if 0 in chunks:
                    if m == 0:
                        pe.wait_ge(wlo_ready, st.slab0 + 2 * hd + j // 2 + 1)
                    pe.wait_ge(tile_free["act"], st.free0 + 3 * hd + j - 1)
                for k in chunks:
                    if isinstance(hd, int) and hd == 0 and j == 0:
                        pe.wait_ge(xlo_ready, XB["hgrn_in"] + k + 1)
                    a = (m * DC + k) * P
                    pe.matmul(o, w_lo[:, slot, a:a + P], x_hi[:, k, :], start=k == 0, stop=False)
                    pe.matmul(o, w_hi[:, slot, a:a + P], x_lo[:, k, :], start=False, stop=False)
                    last = pe.matmul(o, w_hi[:, slot, a:a + P], x_hi[:, k, :], start=False, stop=k == DC - 1)
                if DC - 1 in chunks:
                    last.then_inc(tile_done, 1)

            def step(hd, par, project, attend):
                a, old = hd - 1, 1 - par
                if project:
                    hgrn_tile(hd, par, 0, range(DC))
                if attend:
                    pe.wait_ge(dec_ready, a + 1)
                    for b in range(TB):
                        sl = slice(b * P, (b + 1) * P)
                        last = pe.matmul(ps[:, 2, sl], k_dec[:, old, sl], q_dec[:, old, sl], start=True, stop=True)
                    last.then_inc(a_done, 1)
                    pe.wait_ge(tile_free["act"], st.free0 + 3 * a + 3)
                    for n, src in enumerate((k_dec, hg_v)):
                        for b in range(TB):
                            sl = slice(b * P, (b + 1) * P)
                            last = pe.transpose(ps[:, 3 + n, sl], src[:, old, sl], ident)
                    last.then_inc(ht_done, 1)
                if project:
                    hgrn_tile(hd, par, 1, range(DC))
                if attend:
                    pe.wait_ge(ht_ready, a + 1)
                    pe.wait_ge(root_ready, SK["head0"] + a)
                    for c in range(7):
                        half = slice(CHUNK * (c % 2), CHUNK * (c % 2) + CHUNK)
                        last = pe.matmul(ps[:, 5 + c % 2, (c // 2) * P:(c // 2 + 1) * P], k_tok[half, c // 2, :],
                                         v_htok[half, c // 2, :], start=True, stop=True)
                    last.then_inc(kv_done, 1)
                    pe.wait_ge(a_ready, a + 1)
                    if not (isinstance(a, int) and a == 0):
                        pe.wait_ge(oh_ready, a)
                    for b in range(TB):
                        sl = slice(b * P, (b + 1) * P)
                        pe.matmul(ps[:, O_BANK, sl], v_htok[:, b, :], tmp[:, 3, sl], start=b == 0, stop=False,
                                  skip_group_check=True)
                    if not project:
                        out_slab(range(0, 4))
                if project:
                    hgrn_tile(hd, par, 2, range(DC - 1 if attend else DC))
                if attend:
                    pe.wait_ge(st_ready, a + 1)
                    for c in range(1, 8):
                        sl = slice(c * CHUNK, (c + 1) * CHUNK)
                        last = pe.matmul(ps[:, O_BANK, sl], state[:, c, :], q_dec[:, old, sl], start=False, stop=c == 7,
                                         skip_group_check=True)
                    last.then_inc(oh_done, 1)
                    if project:
                        hgrn_tile(hd, par, 2, (DC - 1,))
                    else:
                        out_slab(range(4, 5))
                    pe.wait_ge(sq_ready, SB["head0"] + a + 1)
                    pe.matmul(ps[:, 5, :], ones, sq[:, 0, :], start=True, stop=True).then_inc(sq_used, 1)
                    if not project:
                        out_slab(range(5, DC - 1))

            def out_slab(chunks):
                first_slab(STAGES["hgrn_out"], None, xlo_ready, XB["hgrn_out"], chunks=chunks)

            read_out(st.before, st)
            step(0, 0, True, False)
            step(1, 1, True, True)
            with pe.Fori(1, HG_HEADS // 2) as i:
                step(2 * i, 0, True, True)
                step(2 * i + 1, 1, True, True)
            read_out(st, STAGES["hgrn_out"])
            step(HG_HEADS, 0, False, True)
            pe.wait_ge(oh_ready, HG_HEADS)
            norm_and_ffn("h", "hgrn_out", "up_h", "down_h")

        @block.scalar
        def _(act):
            small = [(lam, lam_in), (sink, sink_in), (freq, freq_in),
                     (pos, pos_in), (iota, iota_in), (b_re, b_in[:, 0]), (b_im, b_in[:, 1]),
                     (c_re, c_in[:, 0]), (c_im, c_in[:, 1]), (mask_raw, mask_in)]
            assert len(small) == SMALL
            act.dma_start(gains[:, :], gains_in).then_inc(gains_ready, 16)
            act.dma_start(consts[:, :, :], const_in).then_inc(consts_ready, 16)
            for dst, src in small:
                dst = dst[:, :, :] if len(dst.shape) == 3 else dst[:, :]
                act.dma_start(dst, src).then_inc(small_ready, 16)

            def split_hi(st, c, i, unready=False):
                n0 = st.slab0 + c + 1
                slot, trip = n0 % 2, len(st.body)
                act.wait_ge(raw_ready[slot], 16 * (n0 // 2 + 1 + (trip // 2) * i))
                if n0 >= 2:
                    act.wait_ge(tile_done, st.tile0 + st.cum[c] + st.cum[-1] * i)
                act.activation(w_hi[:, slot, :], raw[:, slot, :], ACT.Copy).then_inc(whi_ready, 1)

            def part_hi(event, c, src, scale=1.0):
                act.activation(chunk(x_hi, c), src, ACT.Copy, scale=scale).then_inc(xhi_ready, 1)

            def square(name, c, src):
                j = SB[name] + c
                if j >= 2:
                    act.wait_ge(sq_used, j - 1)
                act.activation(sq[:, j % 2, :], src, ACT.Square).then_inc(sq_ready, 1)

            def take_root(name, n, width, e=0):
                act.wait_ge(sq_used, SB[name] + n)
                act.wait_ge(eps_ready, 1)
                if SK[name]:
                    act.wait_ge(rstd_ready, SK_ROOT[name])
                act.activation(root[:, :], ps[:, SUM, :], ACT.Sqrt, bias=eps[:, e:e + 1], scale=1.0 / width) \
                   .then_inc(root_ready, 1)

            act.wait_ge(raw_ready[0], 16)
            act.activation(w_hi[:, 0, :], raw[:, 0, :], ACT.Copy).then_inc(whi_ready, 1)
            act.wait_ge(gains_ready, 16)
            for c in range(DC):
                if c % 4 == 0:
                    act.wait_ge(x_ready[c // 4], 16)
                part_hi("w_in", c, x_raw[:, c, :], gain("g_pre_mix", c))
            w_in = STAGES["w_in"]
            split_hi(w_in, 0, 0)
            for c in range(DC):
                square("pre_mix", c, x_raw[:, c, :])
            take_root("pre_mix", DC, D)
            act.wait_ge(small_ready, 16 * SMALL)
            act.wait_ge(turn_ready, 1)
            act.activation(par[:, PR["sin"], :], par[:, PR["r"], :], ACT.Sin)
            act.activation(par[:, PR["sin_half"], :], par[:, PR["r"], :], ACT.Sin, scale=0.5).then_inc(sines_ready, 1)

            def sin_cos(co, si, angle, unit):
                act.activation(co, angle, ACT.Abs, scale=unit)
                act.activation(si, angle, ACT.Sin, scale=unit)
                act.drain()
                return act.activation(co, co, ACT.Sin, scale=-1.0, bias=eps[:, 2:3])

            act.wait_ge(rope_ang, 1)
            sin_cos(rope_c[:, :], rope_s[:, :], tmp[:, 1, :], 1.0).then_inc(rope_ready, 1)
            act.activation(masks[:, :], mask_raw[:, :], ACT.Copy)
            act.activation(ident_b[:, :], ident, ACT.Copy).then_inc(mask_ready, 1)


            for c in range(1, 5):
                split_hi(w_in, c, 0)
                if c == 3:
                    act.wait_ge(bt_done, 1)
                    act.activation(b_lhs[:, 0, :, :].rearrange("p a c -> p (a c)"), ps[:, 2, :], ACT.Copy)
                    act.activation(b_lhs[:, 1, :, :].rearrange("p a c -> p (a c)"), ps[:, 3, :], ACT.Copy).then_inc(blhs_ready, 1)
                for pr in range(ANGLES[c - 2] if c > 1 else 0, ANGLES[c - 1] if c < 4 else N_PAIR):
                    if pr in POOL_PAIRS:
                        act.wait_ge(ang_ready["pool"], POOL_PAIRS.index(pr) + 1)
                    else:
                        act.wait_ge(ang_ready["dve"], pr - sum(other < pr for other in POOL_PAIRS) + 1)
                    sin_cos(cos_t[:, pr, :], sin_t[:, pr, :], sin_t[:, pr, :], 2 * PI_IN).then_inc(ang_used, 1)

            for i in range(4):
                act.wait_ge(pre_gelu, i + 1)
                if i >= 2:
                    act.wait_ge(xlo_ready, XB["w_glu"] + i - 1)
                act.activation(tmp[:, 2 + i % 2, :], tmp[:, i % 2, :], ACT.Gelu_apprx_tanh)
                act.drain()
                part_hi("w_glu", i, tmp[:, 2 + i % 2, :])

            act.wait_ge(vt1_done, 1)
            act.activation(v1_tok[:, :, :].rearrange("p a c -> p (a c)"), ps[:, 2, :], ACT.Copy).then_inc(vt1_ready, 1)
            st = STAGES["w_glu"]

            def gate(c, i):
                act.wait_ge(tile_done, st.tile0 + 2 * c + 2 + 4 * i)
                act.wait_ge(tile_free["dve"], st.free0 + 2 * c - 2 + 4 * i)
                act.wait_ge(gains_ready, 16)
                act.activation(tmp[:, c, :], ps[:, GLU_BANKS[2 * c + 1], :], ACT.Sigmoid,
                               bias=gains[:, ds(2 * i + GAIN_AT["b_glu"] + 4 + c, 1)]).then_inc(gate_ready, 1)

            with act.Fori(0, 2) as i:
                for s in range(8):
                    hh, (b, n) = s // 4, BLOCKS1[s % 4]
                    if s % 4 == 0:
                        split_hi(st, s // 4, i)
                    act.wait_ge(max1_ready, 8 * i + s + 1)
                    if s >= 4:
                        act.wait_ge(p1t_done, 8 * i + s - 3)
                    st_ = stat[:, s % 4, :]
                    for m in range(2):
                        act.activation(p1[:, s % 4, 2 * P * m:2 * P * m + n * P], ps[:, 3 + s % 2, 2 * P * m:2 * P * m + n * P],
                                       ACT.Exp, bias=st_[:, 4 + m:5 + m], scale=0.125, accum_out=st_[:, 8 + m:9 + m])
                    act.activation(st_[:, 6:8], st_[:, 6:8], ACT.Exp).then_inc(p1_ready, 1)
                    if s == 5:
                        gate(0, i)
                gate(1, i)

            def merged_hi(first, last):
                for c in range(first, last):
                    act.wait_ge(merge_ready, c + 1)
                    part_hi("w_out", c, y[:, c, :])

            for c in range(4):
                act.wait_ge(y_ready, YB["glu"] + c + 1)
                square("ssm", c, y[:, c, :])
            take_root("ssm", 4, HALF)
            for c in range(4):
                act.wait_ge(y_ready, YB["attn1"] + c + 1)
                square("attn", c, y[:, 4 + c, :])
            act.dma_start(h[:, :, :], x_in).then_inc(h_back, 16)
            merged_hi(0, 4)
            take_root("attn", 4, HALF)
            merged_hi(4, DC)

            def rest(name, body=None):
                st = STAGES[name]

                def trip(i, last):
                    for c in range(len(st.body)):
                        if not (last and c == len(st.body) - 1) and not (name == "gate_up0" and first(i) and c == 0):
                            split_hi(st, c, i)
                        if body:
                            body(st, c, i)

                if name in SPARE_BANKS:
                    trip(0, False)
                    with act.Fori(1, st.trips) as i:
                        trip(i, False)
                else:
                    run(act, st, trip)

            rest("w_out")
            act.wait_ge(y_ready, YB["w_out"] + DC)
            square("post_mix", 0, y[:, DC - 1, :])
            take_root("post_mix", 1, D)
            for c in range(DC):
                act.wait_ge(y_ready, YB["res_mix"] + c + 1)
                part_hi("gate_up", c, h[:, c, :], gain("g_pre_ffn", c))
                square("pre_ffn", c, h[:, c, :])
            split_hi(STAGES["gate_up0"], 0, 0)
            take_root("pre_ffn", DC, D)

            for n in range(2):

                def gated(st, c, i, n=n):
                    k = c + 2 * i
                    act.wait_ge(gate_scaled, HB[str(n)] + k + 1)
                    act.activation(tmp[:, 2, :], tmp[:, 0, :], ACT.Silu).then_inc(silu_ready, 1)
                    act.wait_ge(hid_pre, HB[str(n)] + k + 1)
                    if n == 0:
                        act.wait_ge(prod_ready, 4 * N_PAIR)
                    else:
                        act.wait_ge(tile_done, st.tile0)
                    act.activation(chunk(hid_hi, k), tmp[:, 3, :], ACT.Copy).then_inc(hid_half, 1)

                rest(f"gate_up{n}", gated)
                rest(f"down{n}")
            act.wait_ge(y_ready, YB["ffn"] + DC)
            square("post_ffn", 0, y[:, DC - 1, :])
            take_root("post_ffn", 1, D)
            for c in range(DC):
                act.wait_ge(y_ready, YB["res_ffn"] + c + 1)
                part_hi("attn_in", c, h[:, c, :])

            act.dma_start(rope_c[:, :], rope2_in[:, 0]).then_inc(rope2_ready, 16)
            act.dma_start(rope_s[:, :], rope2_in[:, 1]).then_inc(rope2_ready, 16)
            st = STAGES["attn_in"]

            def attention(p, sub, i, project, attend):
                pa = p - 1
                for j in range(10):
                    if attend and j <= 7:
                        hh, b, near = STEPS2[j]
                        act.wait_ge(max2_ready, 8 * pa + j + 1)
                        act.activation(p2[:, j % 2, 0:near * P], ps[:, 2 + j % 2, 0:near * P], ACT.Exp,
                                       bias=near_max[:, hh, b:b + 1], scale=0.125, accum_out=near_sum[:, hh, b:b + 1])
                        act.activation(p2[:, j % 2, near * P:(near + 2) * P], ps[:, 2 + j % 2, 2 * P:4 * P], ACT.Exp,
                                       bias=o_class[:, hh, b, 64:65], scale=0.125, accum_out=o_class[:, hh, b, 65:66]) \
                           .then_inc(p2_ready, 1)
                    if attend and joins(p, j) is not None:
                        act.wait_ge(mix_half, 2 * pa + joins(p, j) + 1)
                        both = mix[:, 1:3, :].rearrange("p a b -> p (a b)")
                        act.activation(both, both, ACT.Exp).then_inc(mix_exp, 1)
                    if not project and j < DC - 1:
                        output_hi(j, 7)
                    if project and j <= 8:
                        if j % 2 == 0:
                            c = 5 * sub + j // 2
                            n0 = st.slab0 + c + 1
                            act.wait_ge(raw_ready[n0 % 2], 16 * (n0 // 2 + 1 + 5 * i))
                            act.wait_ge(tile_done, st.tile0 + 9 * p + j)
                            act.activation(w_hi[:, n0 % 2, :], raw[:, n0 % 2, :], ACT.Copy).then_inc(whi_ready, 1)
                        act.wait_ge(tile_done, st.tile0 + 9 * p + j + 1)
                        bank = ps[:, (st.tile0 + 9 * sub + j) % 2, :]
                        last = act.activation(qkv[:, sub, j, :], bank, ACT.Copy)
                        if j % 3 != 2:
                            n = 2 * (j // 3) + j % 3
                            if not (isinstance(p, int) and p == 0 and n < 2):
                                act.wait_ge(rot_ready, 6 * p + n - 1)
                            for a in range(4):
                                to, at_ = 32 * a, 32 * (a ^ 1)
                                last = act.activation(swapped[to:to + 32, n % 2, :], bank[at_:at_ + 32, :], ACT.Copy)
                        last.then_inc(tile_free["act"], 1)
                    if project and j >= 1 and (j - 1) % 3 == 2:
                        act.wait_ge(vt2_done, 3 * p + (j - 1) // 3 + 1)
                        act.activation(v_tok[:, sub, (j - 1) // 3, :, :].rearrange("p a c -> p (a c)"), ps[:, 7, :],
                                       ACT.Copy).then_inc(vtok_ready, 1)

            def output_hi(c, bank):
                act.wait_ge(o2t_done, c + 1)
                part_hi("attn_out", c, ps[:, bank, :])

            attention(0, 0, 0, True, False)
            attention(1, 1, 0, True, True)
            with act.Fori(0, HEAD_PAIRS // 2 - 1) as i:
                attention(2 * i + 2, 0, i + 1, True, True)
                attention(2 * i + 3, 1, i + 1, True, True)
            attention(HEAD_PAIRS, 0, 0, False, True)
            output_hi(DC - 1, 5)

            def hidden(key):

                def body(st, c, i):
                    for m in range(2):
                        t = 2 * c + m
                        k = t + 4 * i
                        act.wait_ge(tile_done, st.tile0 + t + 4 * i + 1)
                        act.wait_ge(hid_ready, HB[key] + k - 1)
                        act.activation(tmp[:, t % 2, :], ps[:, (st.tile0 + t) % 2, :], ACT.Relu).then_inc(tile_free["act"], 1)
                        act.drain()
                        act.activation(chunk(hid_hi, k), tmp[:, t % 2, :], ACT.Square).then_inc(hid_half, 1)

                return body

            def layer_norm(layer, part):
                act.wait_ge(acc_summed, MEANS[f"mean_{part}_{layer}"] + 1)
                act.activation(root[:, :], ps[:, SUM, :], ACT.Copy, scale=1.0 / D).then_inc(root_ready, 1)
                for c in range(DC):
                    act.wait_ge(y_ready, YB[f"mid_{part}_{layer}"] + c + 1)
                    square(f"var_{part}_{layer}", c, y[:, c, :])
                take_root(f"var_{part}_{layer}", DC, D, 1)

            def normed(layer, part, n, after):
                for c in range(DC):
                    act.wait_ge(y_ready, YB[f"res_{part}_{layer}"] + c + 1)
                    g, b = gain(f"ln_{part}_g{n}", c), gain(f"ln_{part}_b{n}", c)
                    last = act.activation(h[:, c, :], y[:, c, :], ACT.Identity, scale=g, bias=b)
                    if after:
                        act.activation(x_hi[:, c, :], y[:, c, :], ACT.Identity, scale=g, bias=b).then_inc(xhi_ready, 1)
                    else:
                        last.then_inc(result_ready, 1)

            def norm_and_ffn(layer, proj, up, down, n, after):
                rest(proj)
                layer_norm(layer, "mix")
                normed(layer, "mix", n, up)
                for m in range(2):
                    rest(f"{up}{m}", hidden(f"{layer}{m}"))
                    rest(f"{down}{m}")
                layer_norm(layer, "ffn")
                normed(layer, "ffn", n, after)

            act.wait_ge(rot_ready, 6 * HEAD_PAIRS)
            for n, dst in enumerate((a_mask, run_mask, start_mask)):
                act.dma_start(dst[:, :], hmask_in[:, n]).then_inc(hm_ready, 16)
            act.wait_ge(lb_half, 1)
            act.activation(lbp[:, 2:4, :].rearrange("p a c -> p (a c)"), lbp[:, 2:4, :].rearrange("p a c -> p (a c)"),
                           ACT.Exp).then_inc(lb_exp, 1)

            norm_and_ffn("a", "attn_out", "up_a", "down_a", 0, "hgrn_in")

            st = STAGES["hgrn_in"]

            def split_next(hd, par, i, n):
                c = 2 * par + n + 1
                slot, width = (st.slab0 + c) % 2, SLAB // 2 if n == 0 else SLAB
                act.wait_ge(raw_ready[slot], 16 * ((st.slab0 + c) // 2 + 1 + 2 * i))
                act.wait_ge(tile_done, st.tile0 + 3 * hd + 2 * n)
                act.activation(w_hi[:, slot, 0:width], raw[:, slot, 0:width], ACT.Copy).then_inc(whi_ready, 1)

            def step(hd, par, i, project, attend):
                a = hd - 1
                banks = [ps[:, (st.tile0 + 3 * par + j) % 2, :] for j in range(3)]
                if project:
                    split_next(hd, par, i, 0)
                    act.wait_ge(tile_done, st.tile0 + 3 * hd + 1)
                    if not (isinstance(hd, int) and hd < 2):
                        act.wait_ge(dec_ready, hd - 1)
                    act.activation(hg_q[:, par, :], banks[0], ACT.Silu).then_inc(tile_free["act"], 1)
                if attend:
                    act.wait_ge(ht_done, a + 1)
                    act.activation(k_tok[:, :, :].rearrange("p a c -> p (a c)"), ps[:, 3, :], ACT.Copy)
                    act.activation(v_htok[:, :, :].rearrange("p a c -> p (a c)"), ps[:, 4, :], ACT.Copy) \
                       .then_inc(ht_ready, 1)
                if project:
                    act.wait_ge(tile_done, st.tile0 + 3 * hd + 2)
                    act.activation(hg_s[:, par, :], banks[1], ACT.Sigmoid)
                    act.activation(hg_k[:, par, :], banks[1], ACT.Sigmoid, scale=-1.0).then_inc(tile_free["act"], 1)
                    split_next(hd, par, i, 1)
                if attend:
                    act.wait_ge(oh_done, a + 1)
                    act.activation(sq[:, 0, :], ps[:, SUM, :], ACT.Square).then_inc(sq_ready, 1)
                if project:
                    act.wait_ge(tile_done, st.tile0 + 3 * hd + 3)
                    act.activation(hg_v[:, par, :], banks[2], ACT.Copy).then_inc(tile_free["act"], 1)
                if attend:
                    act.wait_ge(sq_used, SB["head0"] + a + 1)
                    act.wait_ge(rstd_ready, SK_ROOT["head0"] + a)
                    act.activation(root[:, :], ps[:, 5, :], ACT.Sqrt, bias=eps[:, 0:1], scale=1.0 / P) \
                       .then_inc(root_ready, 1)

            def head_hi(hd):
                act.wait_ge(oh_ready, hd + 1)
                part_hi("hgrn_out", hd, hg_o[:, hd, :])

            step(0, 0, 0, True, False)
            step(1, 1, 0, True, True)
            with act.Fori(1, HG_HEADS // 2) as i:
                step(2 * i, 0, i, True, True)
                step(2 * i + 1, 1, i, True, True)
            act.wait_ge(tile_done, STAGES["hgrn_out"].tile0)
            for hd in range(HG_HEADS - 1):
                head_hi(hd)
            step(HG_HEADS, 0, 0, False, True)
            head_hi(HG_HEADS - 1)
            norm_and_ffn("h", "hgrn_out", "up_h", "down_h", 1, None)

        @block.vector
        def _(dve):
            tt, ts, stt, settle = dve.tensor_tensor, dve.tensor_scalar, dve.scalar_tensor_tensor, dve.drain

            def split_lo(st, c, i):
                n0 = st.slab0 + c + 1
                slot = n0 % 2
                dve.wait_ge(whi_ready, n0 + 1 + len(st.body) * i)
                tt(w_lo[:, slot, :], raw[:, slot, :], w_hi[:, slot, :].bitcast(f32), ALU.subtract).then_inc(wlo_ready, 1)

            def part_lo(event, c, src):
                dve.wait_ge(xhi_ready, XB[event] + c + 1)
                tt(chunk(x_lo, c), src, chunk(x_hi, c).bitcast(f32), ALU.subtract).then_inc(xlo_ready, 1)

            def part_lo_gain(event, c, src, scale):
                dve.wait_ge(xhi_ready, XB[event] + c + 1)
                stt(x_lo[:, c, :], src, scale, x_hi[:, c, :].bitcast(f32), ALU.mult, ALU.subtract).then_inc(xlo_ready, 1)

            def invert(name):
                dve.wait_ge(root_ready, SK[name] + 1)
                dve.reciprocal(rstd[:, :], root[:, :]).then_inc(rstd_ready, 1)
                settle()

            for n, value in enumerate((RMS_EPS, LN_EPS, np.pi / 2)):
                last = dve.memset(eps[:, n:n + 1], float(value))
            last.then_inc(eps_ready, 1)
            dve.wait_ge(whi_ready, 1)
            tt(w_lo[:, 0, :], raw[:, 0, :], w_hi[:, 0, :].bitcast(f32), ALU.subtract).then_inc(wlo_ready, 1)
            dve.wait_ge(gains_ready, 16)
            for c in range(DC):
                part_lo_gain("w_in", c, x_raw[:, c, :], gain("g_pre_mix", c))
            split_lo(STAGES["w_in"], 0, 0)
            dve.wait_ge(small_ready, 16 * SMALL)

            def col(name):
                return par[:, PR[name], :]

            def exp_parts(z):
                ts(col("z"), z, -87.0, 88.0, ALU.max, ALU.min)
                settle()
                ts(col("k"), col("z"), float(1 / np.log(2.0)), ROUND, ALU.mult, ALU.add)
                settle()
                ts(col("k"), col("k"), ROUND, None, ALU.subtract)
                settle()
                stt(col("f"), col("k"), -LN2_HI, col("z"), ALU.mult, ALU.add)
                settle()
                stt(col("f"), col("k"), -LN2_LO, col("f"), ALU.mult, ALU.add)
                ts(col("two_k").bitcast(i32), col("k"), 127.0, 2.0 ** 23, ALU.add, ALU.mult)
                settle()
                ts(col("e"), col("f"), 1 / 5040.0, None, ALU.mult)
                for factor in (720.0, 120.0, 24.0, 6.0, 2.0, 1.0):
                    settle()
                    stt(col("e"), col("e"), 1 / factor, col("f"), ALU.add, ALU.mult)
                settle()

            def reduce_turns(angle, k, by):
                stt(angle, k, -PI_HI, angle, ALU.mult, ALU.add)
                settle()
                stt(angle, k, -PI_LO, angle, ALU.mult, ALU.add)
                settle()

            li = lam[:, 1, :]
            ts(col("lr"), lam[:, 0, :], -1e-4, None, ALU.min)
            exp_parts(lam[:, 2, :])
            stt(col("dt"), col("e"), 1.0, col("two_k"), ALU.add, ALU.mult)
            settle()
            tt(col("t0"), col("lr"), col("dt"), ALU.mult)
            tt(col("th"), li, col("dt"), ALU.mult)
            settle()
            exp_parts(col("t0"))
            tt(col("t0"), col("two_k"), col("e"), ALU.mult)
            settle()
            stt(col("em1"), col("two_k"), -1.0, col("t0"), ALU.add, ALU.add)
            ts(col("k"), col("th"), float(1 / TWO_PI), ROUND, ALU.mult, ALU.add)
            settle()
            ts(col("mag"), col("em1"), 1.0, None, ALU.add)
            ts(col("k"), col("k"), ROUND, None, ALU.subtract)
            dve.tensor_copy(col("r"), col("th"))
            settle()
            reduce_turns(col("r"), col("k"), 0)
            ts(col("r"), col("r"), PI_IN, -PI_IN, ALU.min, ALU.max)
            settle()
            ts(col("r_turn"), col("r"), float(1 / TWO_PI), None, ALU.mult).then_inc(turn_ready, 1)
            settle()
            ts(col("t1"), col("r_turn"), 65536.0, ROUND, ALU.mult, ALU.add)
            dve.tensor_copy(col("r_lo"), col("r"))
            settle()
            ts(col("r_hi"), col("t1"), ROUND, 1 / 65536.0, ALU.subtract, ALU.mult)
            settle()
            reduce_turns(col("r_lo"), col("r_hi"), 0)
            ts(col("r_lo"), col("r_lo"), float(1 / TWO_PI), None, ALU.mult).then_inc(turn_ready, 1)
            dve.tensor_copy(tmp[:, 1, :], pos[:, :])
            settle()
            ts(tmp[:, 1, :], tmp[:, 1, :], freq[:, 0:1], None, ALU.mult)
            settle()
            ts(tmp[:, 0, :], tmp[:, 1, :], float(1 / TWO_PI), ROUND, ALU.mult, ALU.add)
            settle()
            ts(tmp[:, 0, :], tmp[:, 0, :], ROUND, None, ALU.subtract)
            settle()
            reduce_turns(tmp[:, 1, :], tmp[:, 0, :], 0)
            ts(tmp[:, 1, :], tmp[:, 1, :], PI_IN, -PI_IN, ALU.min, ALU.max).then_inc(rope_ang, 1)

            def input_matrix():
                dve.wait_ge(sines_ready, 1)
                tt(col("c1"), col("sin_half"), col("sin_half"), ALU.mult)
                tt(col("ai"), col("mag"), col("sin"), ALU.mult)
                settle()
                stt(col("c1"), col("c1"), -2.0, col("mag"), ALU.mult, ALU.mult)
                settle()
                tt(col("am1"), col("c1"), col("em1"), ALU.add)
                tt(col("den"), col("lr"), col("lr"), ALU.mult)
                tt(col("t0"), li, li, ALU.mult)
                settle()
                tt(col("den"), col("den"), col("t0"), ALU.add)
                tt(col("nr"), col("am1"), col("lr"), ALU.mult)
                tt(col("t1"), col("ai"), li, ALU.mult)
                settle()
                dve.reciprocal(col("den"), col("den"))
                tt(col("nr"), col("nr"), col("t1"), ALU.add)
                tt(col("ni"), col("ai"), col("lr"), ALU.mult)
                tt(col("t0"), col("am1"), li, ALU.mult)
                settle()
                tt(col("ni"), col("ni"), col("t0"), ALU.subtract)
                settle()
                tt(col("fr"), col("nr"), col("den"), ALU.mult)
                tt(col("fi"), col("ni"), col("den"), ALU.mult)
                settle()
                fr = col("fr").unsqueeze(2).to_broadcast([P, N_PAIR, GW])
                fi = col("fi").unsqueeze(2).to_broadcast([P, N_PAIR, GW])
                scratch = tmp[:, 0, :].rearrange("p (a c) -> p a c", a=N_PAIR)
                for dst, first, second, op in ((bb_re, b_re, b_im, ALU.subtract), (bb_im, b_im, b_re, ALU.add)):
                    tt(dst[:, :, :], fr, first[:, :, :], ALU.mult)
                    tt(tmp[:, 2, :].rearrange("p (a c) -> p a c", a=N_PAIR), fi, second[:, :, :], ALU.mult)
                    settle()
                    last = tt(dst[:, :, :], dst[:, :, :], tmp[:, 2, :].rearrange("p (a c) -> p a c", a=N_PAIR), op)
                    settle()
                last.then_inc(bb_ready, 1)

            def angles(first, last):
                for pr in [pr for pr in range(first, last) if pr not in POOL_PAIRS]:
                    ang, k = sin_t[:, pr, :], cos_t[:, pr, :]
                    if pr == 13:
                        dve.wait_ge(bt_done, 1)
                    ts(ang, iota[:, :], par[:, PR["r_hi"], pr:pr + 1], None, ALU.mult)
                    ts(k, iota[:, :], par[:, PR["r_turn"], pr:pr + 1], ROUND, ALU.mult, ALU.add)
                    settle()
                    stt(k, k, ROUND, ang, ALU.subtract, ALU.subtract)
                    settle()
                    stt(ang, iota[:, :], par[:, PR["r_lo"], pr:pr + 1], k, ALU.mult, ALU.subtract)
                    settle()
                    ts(ang, ang, 0.5, -0.5, ALU.min, ALU.max).then_inc(ang_ready["dve"], 1)

            angles(0, ANGLES[0])
            invert("pre_mix")
            st = STAGES["w_in"]
            places = [u[:, c, :] for c in range(4)] + [q1[:, c, :] for c in range(4)] + [k1[:, :], v1[:, :]]
            dve.wait_ge(mask_ready, 1)
            dve.wait_ge(sq_used, DC)
            for c in range(5):
                if c:
                    split_lo(st, c, 0)
                for m in range(2):
                    t = 2 * c + m
                    dve.wait_ge(tile_done, t + 1)
                    tt(places[t], ps[:, 4 + m if c == 1 else t % 2, :], rstd[:, :], ALU.mult).then_inc(tile_free["dve"], 1)
                if c == 1:
                    input_matrix()
                if c:
                    angles(ANGLES[c - 1], ANGLES[c])
            ts(c_neg[:, :, :], c_re[:, :, :], -1.0, None, ALU.mult)
            ts(c_im[:, :, :], c_im[:, :, :], -1.0, None, ALU.mult)
            settle()

            def ssm_chunk(c):
                dve.wait_ge(yssm_done, 16 * c + 16)
                if c >= 2:
                    dve.wait_ge(xlo_ready, XB["w_glu"] + c - 1)
                stt(tmp[:, c % 2, :], u[:, c, :], gain("d", c), ps[:, (6, SUM)[c % 2], :], ALU.mult, ALU.add) \
                    .then_inc(pre_gelu, 1)

            def modulate(pr):
                re, im = ps[:, 2 + 2 * (pr % 2), :], ps[:, 3 + 2 * (pr % 2), :]
                v_re, v_im = mod[pr % 2]
                dve.wait_ge(ang_used, pr + 1)
                dve.wait_ge(bu_done, pr + 1)
                tt(v_re, re, cos_t[:, pr, :], ALU.mult)
                tt(mod_more[:, 0, :], im, sin_t[:, pr, :], ALU.mult)
                tt(v_im, im, cos_t[:, pr, :], ALU.mult)
                tt(mod_more[:, 1, :], re, sin_t[:, pr, :], ALU.mult).then_inc(bu_free, 1)
                settle()
                tt(v_re, v_re, mod_more[:, 0, :], ALU.add)
                tt(v_im, v_im, mod_more[:, 1, :], ALU.subtract)
                settle()

            settle()
            modulate(0)
            for pr in range(N_PAIR):
                i, q = divmod(pr, 4)
                mag = par[:, PR["mag"], pr:pr + 1].to_broadcast([P, T])
                for part in range(2):
                    if pr >= 2:
                        dve.wait_ge(prod_ready, 4 * pr - 6 + 2 * part)
                    dve.tensor_tensor_scan(scan[pr % 2][part], mag, mod[pr % 2][part], 0.0, ALU.mult, ALU.add) \
                       .then_inc(scan_ready, 1)
                if pr + 1 < N_PAIR:
                    modulate(pr + 1)
                if q == 1 and i:
                    ssm_chunk(i - 1)
                if q == 2 and i:
                    part_lo("w_glu", i - 1, tmp[:, 2 + (i - 1) % 2, :])
            ssm_chunk(3)
            part_lo("w_glu", 3, tmp[:, 3, :])

            dve.wait_ge(kr1_swap, 1)
            tt(tmp[:, 0, :], ps[:, 3, :], rope_s[:, :], ALU.mult)
            tt(k1[:, :], k1[:, :], rope_c[:, :], ALU.mult)
            settle()
            tt(k1[:, :], k1[:, :], tmp[:, 0, :], ALU.add).then_inc(kr1_ready, 1)
            glu_st = STAGES["w_glu"]

            def glu(c, i):
                dve.wait_ge(gate_ready, c + 1 + 2 * i)
                stt(chunk(y, 2 * i + c), ps[:, GLU_BANKS[2 * c], :], gains[:, ds(2 * i + GAIN_AT["b_glu"] + c, 1)],
                    tmp[:, c, :], ALU.add, ALU.mult).then_inc(tile_free["dve"], 2)
                settle()
                dve.sem_inc(y_ready, 1)

            with dve.Fori(0, 2) as i:
                for m in range(2):
                    dve.wait_ge(qr1_swap, 2 * i + m + 1)
                    tt(tmp[:, m, :], ps[:, (5, SUM)[m], :], rope_s[:, :], ALU.mult)
                    tt(qr1[:, m, :], chunk(q1, 2 * i + m), rope_c[:, :], ALU.mult)
                    settle()
                    tt(qr1[:, m, :], qr1[:, m, :], tmp[:, m, :], ALU.add).then_inc(qr1_ready, 1)

                def maximum1(s):
                    hh, (b, n) = s // 4, BLOCKS1[s % 4]
                    st_ = stat[:, s % 4, :]
                    sinks = sink[:, ds(4 * i + 2 * hh, 2)]
                    dve.wait_ge(s1_done, 8 * i + s + 1)
                    scores = ps[:, 3 + s % 2, :].rearrange("p (m k) -> p m k", m=2)[:, :, 0:n * P]
                    dve.tensor_reduce(st_[:, 0:2], scores, AX.X, ALU.max)
                    settle()
                    stt(st_[:, 2:4], st_[:, 0:2], 0.125, sinks, ALU.mult, ALU.max)
                    settle()
                    ts(st_[:, 4:6], st_[:, 2:4], -1.0, None, ALU.mult)
                    tt(st_[:, 6:8], sinks, st_[:, 2:4], ALU.subtract).then_inc(max1_ready, 1)

                def scale1(s):
                    hh, (b, n) = s // 4, BLOCKS1[s % 4]
                    st_ = stat[:, s % 4, :]
                    tt(st_[:, 10:12], st_[:, 6:8], st_[:, 8:10], ALU.add)
                    settle()
                    dve.reciprocal(st_[:, 12:14], st_[:, 10:12])
                    settle()
                    dve.wait_ge(o1_done, 8 * i + s + 1)
                    for m in range(2):
                        last = ts(o1_tok[:, b, ds(256 * i + 128 * m + 64 * hh, 64)],
                                  ps[:, 6, 64 * m:64 * m + 64], st_[:, 12 + m:13 + m], None, ALU.mult)
                    last.then_inc(o1_ready, 1)

                maximum1(0)
                maximum1(1)
                for s in range(8):
                    n = BLOCKS1[s % 4][1]
                    if s % 4 == 0:
                        split_lo(glu_st, s // 4, i)
                    if s == 6:
                        glu(0, i)
                    dve.wait_ge(p1t_done, 8 * i + s + 1)
                    dve.tensor_copy(p1_t[:, s % 2, 0:2 * n * P], ps[:, (5, SUM)[s % 2], 0:2 * n * P]) \
                        .then_inc(p1t_ready, 1)
                    if s < 6:
                        maximum1(s + 2)
                    if s:
                        scale1(s - 1)
                scale1(7)
                glu(1, i)
            for c in range(4):
                dve.wait_ge(o1t_done, c + 1)
                dve.tensor_copy(y[:, 4 + c, :], ps[:, 4 + c % 2, :]).then_inc(y_ready, 1)

            def merge(name, chunks):
                for c in chunks:
                    stt(y[:, c, :], y[:, c, :], gain(name, c % 4), rstd[:, :], ALU.mult, ALU.mult).then_inc(merge_ready, 1)
                    if c > chunks[0]:
                        part_lo("w_out", c - 1, y[:, c - 1, :])
                settle()
                part_lo("w_out", chunks[-1], y[:, chunks[-1], :])

            invert("ssm")
            merge("g_ssm", range(4))
            invert("attn")
            merge("g_attn", range(4, DC))

            def rest(name, body):
                st = STAGES[name]

                def trip(i, last):
                    for c in range(len(st.body)):
                        if not (last and c == len(st.body) - 1) and not (name == "gate_up0" and first(i) and c == 0):
                            split_lo(st, c, i)
                        body(st, c, i)

                if name in SPARE_BANKS:
                    trip(0, False)
                    with dve.Fori(1, st.trips) as i:
                        trip(i, False)
                else:
                    run(dve, st, trip)

            def tiles(put):

                def body(st, c, i):
                    for m in range(st.body[c]):
                        t = st.cum[c] + m
                        dve.wait_ge(tile_done, st.tile0 + t + st.cum[-1] * i + 1)
                        put(t + st.cum[-1] * i, ps[:, (st.tile0 + t) % 2, :])

                return body

            def keep(t, bank):
                ts(chunk(y, t), bank, 1.0, None, ALU.mult).then_inc(tile_free["dve"], 1)

            def keep_and_tell(t, bank):
                ts(chunk(y, t), bank, 1.0, None, ALU.mult).then_inc(tile_free["dve"], 1)
                settle()
                dve.sem_inc(y_ready, 1)

            def add_and_tell(t, bank):
                tt(chunk(y, t), bank, chunk(y, t), ALU.add).then_inc(tile_free["dve"], 1)
                settle()
                dve.sem_inc(y_ready, 1)

            def residual(t, bank):
                stt(chunk(y, t), chunk(h, t), ALPHA, bank, ALU.mult, ALU.add).then_inc(tile_free["dve"], 1)

            def residual_and_tell(t, bank):
                residual(t, bank)
                settle()
                dve.sem_inc(y_ready, 1)

            def post_norm(name, g, after):
                invert(name)
                for c in range(DC):
                    stt(y[:, c, :], y[:, c, :], gain(g, c), rstd[:, :], ALU.mult, ALU.mult)
                    settle()
                    tt(h[:, c, :], h[:, c, :], y[:, c, :], ALU.add).then_inc(y_ready, 1)
                    if c:
                        after(c - 1)
                settle()
                after(DC - 1)

            rest("w_out", tiles(keep_and_tell))
            dve.wait_ge(h_back, 16)
            post_norm("post_mix", "g_post_mix",
                      lambda c: part_lo_gain("gate_up", c, h[:, c, :], gain("g_pre_ffn", c)))

            split_lo(STAGES["gate_up0"], 0, 0)
            invert("pre_ffn")
            for n in range(2):

                def gated(st, c, i, n=n):
                    k = c + 2 * i
                    for m in range(2):
                        t = 2 * c + m
                        dve.wait_ge(tile_done, st.tile0 + t + 4 * i + 1)
                        own = n == 0 and c == 1 and first(i)
                        bank = ps[:, SPARE_BANKS["gate_up0"] + m if own else (st.tile0 + t) % 2, :]
                        scaled = tt(tmp[:, m, :], bank, rstd[:, :], ALU.mult)
                        scaled.then_inc(tile_free["dve"], 1)
                        settle()
                        if m == 0:
                            dve.sem_inc(gate_scaled, 1)
                    dve.wait_ge(silu_ready, HB[str(n)] + k + 1)
                    tt(tmp[:, 3, :], tmp[:, 2, :], tmp[:, 1, :], ALU.mult).then_inc(hid_pre, 1)
                    settle()
                    dve.wait_ge(hid_half, HB[str(n)] + k + 1)
                    tt(chunk(hid_lo, k), tmp[:, 3, :], chunk(hid_hi, k).bitcast(f32), ALU.subtract).then_inc(hid_ready, 1)

                rest(f"gate_up{n}", gated)
                rest(f"down{n}", tiles(keep if n == 0 else add_and_tell))
            post_norm("post_ffn", "g_post_ffn", lambda c: part_lo("attn_in", c, h[:, c, :]))

            dve.wait_ge(rope2_ready, 32)
            st = STAGES["attn_in"]

            def join(pa, n):
                nth, hh = 2 * pa + n, n % 2
                dve.wait_ge(far_ready, 64 * (nth + 1))
                near, far, far_max, far_sum = o_near[:, hh], o_far[:, hh, :, 0:64], o_far[:, hh, :, 64], o_far[:, hh, :, 65]
                tt(mix[:, 0, :], near_max[:, hh, :], far_max, ALU.min)
                settle()
                tt(mix[:, 1, :], mix[:, 0, :], near_max[:, hh, :], ALU.subtract)
                tt(mix[:, 2, :], mix[:, 0, :], far_max, ALU.subtract).then_inc(mix_half, 1)
                dve.wait_ge(mix_exp, nth + 1)
                tt(mix[:, 3, :], mix[:, 1, :], near_sum[:, hh, :], ALU.mult)
                tt(mix[:, 4, :], mix[:, 2, :], far_sum, ALU.mult)
                settle()
                tt(mix[:, 3, :], mix[:, 3, :], mix[:, 4, :], ALU.add)
                settle()
                dve.reciprocal(mix[:, 4, :], mix[:, 3, :])
                settle()
                tt(mix[:, 1, :], mix[:, 1, :], mix[:, 4, :], ALU.mult)
                tt(mix[:, 2, :], mix[:, 2, :], mix[:, 4, :], ALU.mult)
                settle()
                tt(near, near, mix[:, 1, :].unsqueeze(2).to_broadcast([P, TB, 64]), ALU.mult)
                tt(far, far, mix[:, 2, :].unsqueeze(2).to_broadcast([P, TB, 64]), ALU.mult)
                settle()
                tt(o2_tok[:, :, ds(64 * nth, 64)], near, far, ALU.add).then_inc(joined, 1)

            def attention(p, sub, i, project, attend):
                pa = p - 1
                for j in range(10):
                    s = j - 1
                    if attend and 1 <= j <= 8:
                        hh, b, near = STEPS2[s]
                        dve.wait_ge(p2t_done, 8 * pa + s + 1)
                        dve.tensor_copy(p2_t[:, s % 2, 0:(near + 2) * P], ps[:, 5 + s % 2, 0:(near + 2) * P]) \
                            .then_inc(p2t_ready, 1)
                    if attend and j <= 7:
                        hh, b, near = STEPS2[j]
                        st_ = stat[:, j % 2, :]
                        dve.wait_ge(s2_done, 8 * pa + j + 1)
                        dve.tensor_reduce(st_[:, 0:1], ps[:, 2 + j % 2, 0:near * P], AX.X, ALU.max)
                        dve.tensor_reduce(st_[:, 1:2], ps[:, 2 + j % 2, 2 * P:4 * P], AX.X, ALU.max)
                        settle()
                        ts(near_max[:, hh, b:b + 1], st_[:, 0:1], -0.125, None, ALU.mult)
                        ts(o_class[:, hh, b, 64:65], st_[:, 1:2], -0.125, None, ALU.mult).then_inc(max2_ready, 1)
                    if attend and 2 <= j <= 9:
                        hh, b, near = STEPS2[j - 2]
                        dve.wait_ge(o2_done, 8 * pa + j - 1)
                        dve.tensor_copy(o_near[:, hh, b, :], ps[:, 4, 0:64])
                        dve.tensor_copy(o_class[:, hh, b, 0:64], ps[:, 4, 64:128]).then_inc(o2_ready, 1)
                    if attend and joins(p, j) is not None:
                        join(pa, joins(p, j))
                    if not project and j < DC - 1:
                        part_lo("attn_out", j, ps[:, 7, :])
                    if project and j <= 8 and j % 2 == 0:
                        c = 5 * sub + j // 2
                        n0 = st.slab0 + c + 1
                        dve.wait_ge(whi_ready, st.slab0 + 5 * p + j // 2 + 2)
                        tt(w_lo[:, n0 % 2, :], raw[:, n0 % 2, :], w_hi[:, n0 % 2, :].bitcast(f32), ALU.subtract) \
                            .then_inc(wlo_ready, 1)
                    if project and j >= 1 and (j - 1) % 3 != 2:
                        dve.wait_ge(tile_free["act"], st.free0 + 9 * p + j)
                        tile = qkv[:, sub, j - 1, :]
                        n = 2 * ((j - 1) // 3) + (j - 1) % 3
                        tt(tmp[:, 0, :], swapped[:, n % 2, :], rope_s[:, :], ALU.mult)
                        tt(tile, tile, rope_c[:, :], ALU.mult)
                        settle()
                        tt(tile, tile, tmp[:, 0, :], ALU.add).then_inc(rot_ready, 1)
                        settle()

            attention(0, 0, 0, True, False)
            attention(1, 1, 0, True, True)
            with dve.Fori(0, HEAD_PAIRS // 2 - 1) as i:
                attention(2 * i + 2, 0, i + 1, True, True)
                attention(2 * i + 3, 1, i + 1, True, True)
            attention(HEAD_PAIRS, 0, 0, False, True)
            part_lo("attn_out", DC - 1, ps[:, 5, :])

            def hidden(key):
                def body(st, c, i):
                    for m in range(2):
                        t = 2 * c + m
                        k = t + 4 * i
                        dve.wait_ge(hid_half, HB[key] + k + 1)
                        tt(tmp[:, 2 + t % 2, :], tmp[:, t % 2, :], tmp[:, t % 2, :], ALU.mult)
                        settle()
                        tt(chunk(hid_lo, k), tmp[:, 2 + t % 2, :], chunk(hid_hi, k).bitcast(f32), ALU.subtract) \
                            .then_inc(hid_ready, 1)

                return body

            def layer_norm(layer, part, n, after):
                dve.wait_ge(root_ready, SK[f"mean_{part}_{layer}"] + 1)
                for c in range(DC):
                    tt(y[:, c, :], y[:, c, :], root[:, :], ALU.subtract).then_inc(y_ready, 1)
                settle()
                invert(f"var_{part}_{layer}")
                for c in range(DC):
                    tt(y[:, c, :], y[:, c, :], rstd[:, :], ALU.mult).then_inc(y_ready, 1)
                    if after and c:
                        part_lo(after, c - 1, h[:, c - 1, :])
                if after:
                    part_lo(after, DC - 1, h[:, DC - 1, :])

            def norm_and_ffn(layer, proj, up, down, n, after):
                rest(proj, tiles(residual_and_tell))
                layer_norm(layer, "mix", n, up)
                rest(f"{up}0", hidden(f"{layer}0"))
                rest(f"{down}0", tiles(residual))
                rest(f"{up}1", hidden(f"{layer}1"))
                rest(f"{down}1", tiles(add_and_tell))
                layer_norm(layer, "ffn", n, after)

            a0, b0 = GAIN_AT["lb0"], GAIN_AT["lb1"]
            l0, l1 = gains[:, a0:a0 + HG_HEADS], gains[:, b0:b0 + HG_HEADS]
            tt(lbp[:, 4, :], l0, l1, ALU.max)
            settle()
            tt(lbp[:, 2, :], l0, lbp[:, 4, :], ALU.subtract)
            tt(lbp[:, 3, :], l1, lbp[:, 4, :], ALU.subtract).then_inc(lb_half, 1)
            dve.wait_ge(lb_exp, 1)
            tt(lbp[:, 4, :], lbp[:, 2, :], lbp[:, 3, :], ALU.add)
            settle()
            dve.reciprocal(lbp[:, 5, :], lbp[:, 4, :])
            settle()
            tt(lbp[:, 0, :], lbp[:, 3, :], lbp[:, 5, :], ALU.mult)
            tt(lbp[:, 1, :], lbp[:, 2, :], lbp[:, 5, :], ALU.mult)
            settle()

            norm_and_ffn("a", "attn_out", "up_a", "down_a", 0, "hgrn_in")

            dve.wait_ge(hm_ready, 48)
            st = STAGES["hgrn_in"]

            def split_next(hd, par, n):
                slot, width = (st.slab0 + 2 * par + n + 1) % 2, SLAB // 2 if n == 0 else SLAB
                dve.wait_ge(whi_ready, st.slab0 + 2 * hd + n + 2)
                tt(w_lo[:, slot, 0:width], raw[:, slot, 0:width], w_hi[:, slot, 0:width].bitcast(f32), ALU.subtract) \
                    .then_inc(wlo_ready, 1)

            def step(hd, par, project, attend):
                a, old = hd - 1, 1 - par
                if project:
                    split_next(hd, par, 0)
                if attend:
                    dve.wait_ge(a_done, a + 1)
                    tt(tmp[:, 3, :], ps[:, 2, :], a_mask[:, :], ALU.mult).then_inc(a_ready, 1)
                    dve.wait_ge(kv_done, a + 1)
                    for c in range(7):
                        kv = ps[:, 5 + c % 2, (c // 2) * P:(c // 2 + 1) * P]
                        decay = f_cum[:, old, CHUNK * c + CHUNK - 1:CHUNK * c + CHUNK]
                        if c:
                            tt(state[:, c + 1, :], kv, state[:, c, :], ALU.add)
                            settle()
                        last = ts(state[:, c + 1, :], state[:, c + 1, :] if c else kv, decay, None, ALU.mult)
                        if c < 6:
                            settle()
                    last.then_inc(st_ready, 1)
                if project:
                    split_next(hd, par, 1)
                    lb, rest_ = lbp[:, 0, ds(hd, 1)], lbp[:, 1, ds(hd, 1)]
                    dve.wait_ge(tile_free["act"], st.free0 + 3 * hd + 2)
                    ts(tmp[:, 0, :], hg_s[:, par, :], rest_, lb, ALU.mult, ALU.add)
                    settle()
                    tt(f_run[:, :], tmp[:, 0, :], run_mask[:, :], ALU.mult)
                    tt(f_start[:, :], tmp[:, 0, :], start_mask[:, :], ALU.mult)
                    settle()
                    dve.tensor_tensor_scan(f_cum[:, par, :], f_run[:, :], f_start[:, :], 0.0, ALU.mult, ALU.add)
                    settle()
                    dve.reciprocal(f_run[:, :], f_cum[:, par, :])
                    tt(q_dec[:, par, :], hg_q[:, par, :], f_cum[:, par, :], ALU.mult)
                    settle()
                    stt(k_dec[:, par, :], hg_k[:, par, :], rest_, f_run[:, :], ALU.mult, ALU.mult).then_inc(dec_ready, 1)
                if attend:
                    dve.wait_ge(root_ready, SK["head0"] + a + 1)
                    dve.reciprocal(rstd[:, :], root[:, :]).then_inc(rstd_ready, 1)
                    settle()
                    stt(chunk(hg_o, a), ps[:, SUM, :], gains[:, ds(GAIN_AT["g_hgrn"] + a, 1)], rstd[:, :], ALU.mult,
                        ALU.mult).then_inc(oh_ready, 1)

            step(0, 0, True, False)
            step(1, 1, True, True)
            with dve.Fori(1, HG_HEADS // 2) as i:
                step(2 * i, 0, True, True)
                step(2 * i + 1, 1, True, True)
            settle()
            for hd in range(HG_HEADS - 1):
                part_lo("hgrn_out", hd, hg_o[:, hd, :])
            step(HG_HEADS, 0, False, True)
            settle()
            part_lo("hgrn_out", HG_HEADS - 1, hg_o[:, HG_HEADS - 1, :])
            norm_and_ffn("h", "hgrn_out", "up_h", "down_h", 1, None)


def slabs(weight, kc, order, per, width=None):
    k, n = weight.shape
    tiles = weight.reshape(kc, P, n // P, P).transpose(2, 1, 0, 3)[order]
    tiles = tiles.reshape(len(order) // per, per, P, kc, P).transpose(0, 2, 1, 3, 4)
    return np.ascontiguousarray(tiles.reshape(len(order) // per, P, per * kc * P))


def columns(vector):
    return np.asarray(vector, np.float32).reshape(-1, P).T


def swap_matrix(period, half):
    m = np.zeros((P, P), np.float32)
    for f in range(P):
        d = f % period
        if d < half:
            m[f + half, f] = -1.0
        elif d < 2 * half:
            m[f - half, f] = 1.0
    return m


def shape_constants():
    i, j = np.arange(P)[:, None], np.arange(P)[None, :]

    def mask(valid):
        return np.where(valid, 0.0, NEG).astype(np.float32)

    parts = [mask(j > i), mask(j <= i), mask(j >= i), mask(j <= i), mask(j <= i), mask(((i - j) % CLASSES == 0) & (j <= i))]
    const = np.stack([np.eye(P), swap_matrix(64, 8), np.ones((P, P))], 1).astype(np.float32)
    t = np.arange(T, dtype=np.float32)
    d = np.arange(P) % 64
    inv1 = (np.float32(500000.0) ** (-np.arange(8, dtype=np.float32) * np.float32(2.0) / np.float32(16))).astype(np.float32)
    freq = np.where(d < 16, inv1[d % 8], 0.0).astype(np.float32)[:, None]
    inv2 = (np.float32(10000.0) ** (-np.arange(32, dtype=np.float32) * np.float32(2.0 / 64))).astype(np.float32)
    angle = (t[None, :] * inv2[np.arange(P) % 32][:, None]).astype(np.float32)
    rope2 = np.stack([np.cos(angle), np.sin(angle) * np.where(d < 32, -1.0, 1.0)[:, None]], 1).astype(np.float32)
    s, c = np.arange(P)[:, None], np.arange(T)[None, :]
    inside = ((c % P) >= s) & ((c % P) // CHUNK == s // CHUNK)
    start = np.broadcast_to((np.arange(T) % CHUNK == 0)[None, :], (P, T))
    hmask = np.stack([inside, ~start, start], 1).astype(np.float32)
    return {
        "iota_in": np.ascontiguousarray(np.broadcast_to(t, (P, T))), "const_in": const, "freq_in": freq,
        "mask_in": np.ascontiguousarray(np.concatenate(parts, 1)), "rope2_in": rope2, "hmask_in": hmask,
    }


def layout(a):
    sent = {}
    w_in = a["w_in"][0]
    heads = w_in[:, HALF:2 * HALF].reshape(D, 2, 4, 64).transpose(0, 2, 1, 3).reshape(D, HALF)
    w_in = np.concatenate([w_in[:, :HALF], heads, w_in[:, 2 * HALF:]], 1)
    w_out = a["w_out"][0]
    rows = w_out[HALF:].reshape(2, 4, 64, D).transpose(1, 0, 2, 3).reshape(HALF, D)
    w_out = np.concatenate([w_out[:HALF], rows], 0)
    g_attn = a["g_attn_out"][0].reshape(2, 4, 64).transpose(1, 0, 2).reshape(HALF)
    w = {"w_in": slabs(w_in, 8, np.arange(10), 2),
         "w_glu": slabs(a["w_glu"][0], 4, np.arange(8).reshape(2, 4).T.ravel(), 2),
         "w_out": slabs(w_out, 8, np.arange(8), 2)}
    first = 0
    for n, c in enumerate(FFN1_PARTS):
        order = np.stack([np.arange(first, first + c), DFF // P + np.arange(first, first + c)], 1).ravel()
        w[f"gate_up{n}"] = slabs(a["w_gate_up"][0], 8, order, 2)
        w[f"down{n}"] = slabs(a["w_down"][0][first * P:(first + c) * P], c, np.arange(8), 1)
        first += c
    tiles = slabs(a["attn_w_in_2"][0], 8, np.arange(72).reshape(9, 8).T.ravel(), 1).reshape(8, 9, P, 8 * P)
    tiles = np.concatenate([tiles, np.zeros((8, 1, P, 8 * P), np.float32)], 1)
    w["attn_in"] = np.ascontiguousarray(tiles.reshape(40, 2, P, 8 * P).transpose(0, 2, 1, 3).reshape(40, P, SLAB))
    w["attn_out"] = slabs(a["attn_w_out_2"][0], 8, np.arange(8), 2)
    tiles = slabs(a["hgrn_w_in_2"][0], 8, np.arange(24).reshape(3, 8).T.ravel(), 1).reshape(8, 3, P, 8 * P)
    tiles = np.concatenate([tiles, np.zeros((8, 1, P, 8 * P), np.float32)], 1)
    w["hgrn_in"] = np.ascontiguousarray(tiles.reshape(16, 2, P, 8 * P).transpose(0, 2, 1, 3).reshape(16, P, SLAB))
    w["hgrn_out"] = slabs(a["hgrn_w_out_2"][0], 8, np.arange(8), 2)
    for layer, name in enumerate(("a", "h")):
        for n in range(2):
            w[f"up_{name}{n}"] = slabs(a["ffn_w_up_2"][layer], 8, np.arange(16 * n, 16 * n + 16), 2)
            w[f"down_{name}{n}"] = slabs(a["ffn_w_down_2"][layer][2048 * n:2048 * n + 2048], 16, np.arange(8), 1)
    for name, value in w.items():
        sent["w_" + name] = value
    sent["x_in"] = a["x"][0].reshape(T, DC, P).transpose(2, 1, 0)
    vectors = [a["g_pre_mix"], a["g_ssm_out"], g_attn, a["g_post_mix"], a["g_pre_ffn"], a["g_post_ffn"], a["ssm_d"],
               a["b_glu"], a["hgrn_norm_g_2"], a["lb_logits_2"][0], a["lb_logits_2"][1]]
    for layer in range(2):
        vectors += [a["ln_mix_g_2"][layer], a["ln_mix_b_2"][layer], a["ln_ffn_g_2"][layer], a["ln_ffn_b_2"][layer]]
    sent["gains_in"] = np.concatenate([columns(v) for v in vectors], 1)

    def by_state(v):
        return v.reshape(N_PAIR, P).T

    log_dt = np.broadcast_to(a["ssm_log_dt"][0][:, None], (32, 64))
    sent["lam_in"] = np.stack([by_state(a["ssm_lambda_re"][0]), by_state(a["ssm_lambda_im"][0]), by_state(log_dt)], 1)
    sinks = a["attn_sinks"][0].reshape(2, 2, 2).transpose(1, 0, 2)
    sent["sink_in"] = np.broadcast_to(sinks.reshape(1, 8), (P, 8))

    def padded(v):
        o = np.zeros((N_PAIR, 2, 64, 2, 16), np.float32)
        v = v.reshape(N_PAIR, 2, 64, 16)
        for g in range(2):
            o[:, g, :, g, :] = v[:, g]
        return o.reshape(N_PAIR, P, GW).transpose(1, 0, 2)

    sent["b_in"] = np.stack([padded(a["ssm_b_re"][0]), padded(a["ssm_b_im"][0])], 1)
    sent["c_in"] = np.stack([padded(a["ssm_c_re"][0].transpose(0, 2, 1)), padded(a["ssm_c_im"][0].transpose(0, 2, 1))], 1)
    sent["pos_in"] = np.broadcast_to(a["positions"][0], (P, T))
    sent.update(shape_constants())
    return {k: np.ascontiguousarray(v) for k, v in sent.items()}


def kernel(**inputs):
    import concourse.bacc as bacc
    from concourse.bass_utils import run_bass_kernel_spmd

    sent = layout({k: np.asarray(v) for k, v in inputs.items()})
    nc = bacc.Bacc("TRN2", target_bir_lowering=False, num_devices=1)
    handles = {k: nc.dram_tensor(k, v.shape, mybir.dt.from_np(v.dtype), kind="ExternalInput").ap() for k, v in sent.items()}
    out = nc.dram_tensor("out", (P, DC, T), mybir.dt.float32, kind="ExternalOutput").ap()
    weights = {k: handles.pop("w_" + k) for k in STAGES}
    build(nc, weights, out=out, **handles)
    got = run_bass_kernel_spmd(nc, [sent], core_ids=[0]).results[0]["out"]
    return np.ascontiguousarray(got.transpose(2, 1, 0).reshape(1, T, D))
```
